# Optimizing a Trainium2 kernel written in Bass

```python
import jax, jax.numpy as jnp
from jax import lax
import numpy as np

D_MODEL = 1024
BATCH = 1
SEQ = 512
DEPTH = 2

D_MIX = D_MODEL
MLA_HEADS = 8
MLA_V_DIM = 64
MLA_NOPE_DIM = 64
MLA_ROPE_DIM = 32
MLA_QK_DIM = MLA_NOPE_DIM + MLA_ROPE_DIM
MLA_Q_RANK = 256
MLA_KV_RANK = 128
ROPE_THETA = 10000.0
Q_BLOCK = 128
MLSTM_HEADS = 4
MLSTM_HEAD_DIM = 128
D_MLSTM = MLSTM_HEADS * MLSTM_HEAD_DIM
CONV_WIDTH = 4
CHUNK = 64
N_GROUPS = 8
EXPERTS_PER_GROUP = 8
N_EXPERTS = N_GROUPS * EXPERTS_PER_GROUP
D_EXPERT = 256
TOP_K = 2
EXPERT_BLOCK = 128
DN_ALPHA = (2 * DEPTH) ** 0.25
DN_BETA = (8 * DEPTH) ** -0.25
LN_EPS = 1e-5
RMS_EPS = 1e-6
COL_SIZES = (MLA_Q_RANK, MLA_KV_RANK, MLA_ROPE_DIM, D_MLSTM, D_MLSTM, D_MLSTM, D_MLSTM, MLSTM_HEADS, MLSTM_HEADS)
D_IN = sum(COL_SIZES)

kernel_name = 'hymba_mla_mlstm_hmoe_deepnorm'

def _layer_norm(x, g, b):
    xf = x.astype(jnp.float32)
    mu = jnp.mean(xf, -1, keepdims=True)
    var = jnp.mean(jnp.square(xf - mu), -1, keepdims=True)
    return ((xf - mu) * lax.rsqrt(var + LN_EPS) * g + b).astype(x.dtype)

def _rms_norm(x, g):
    xf = x.astype(jnp.float32)
    return (xf * lax.rsqrt(jnp.mean(xf * xf, -1, keepdims=True) + RMS_EPS) * g).astype(x.dtype)

def _head_norm(h):
    hf = h.astype(jnp.float32)
    return (hf * lax.rsqrt(jnp.mean(hf * hf, -1, keepdims=True) + RMS_EPS)).astype(h.dtype)

def _rope(x, pos):
    half = MLA_ROPE_DIM // 2
    inv_freq = ROPE_THETA ** (-jnp.arange(half, dtype=jnp.float32) / half)
    ang = pos.astype(jnp.float32)[..., None] * inv_freq
    cos, sin = jnp.cos(ang), jnp.sin(ang)
    x1 = x[..., :half].astype(jnp.float32)
    x2 = x[..., half:].astype(jnp.float32)
    return jnp.concatenate([x1 * cos - x2 * sin, x2 * cos + x1 * sin], -1).astype(x.dtype)

def _mla(c_q, c_kv, k_rope, positions, q_a_g, kv_a_g, w_qb, w_kvb):
    B, S, _ = c_q.shape
    q = (_rms_norm(c_q, q_a_g) @ w_qb).reshape(B, S, MLA_HEADS, MLA_QK_DIM)
    q_nope = q[..., :MLA_NOPE_DIM]
    q_rope = _rope(q[..., MLA_NOPE_DIM:], positions[:, :, None])
    kv = (_rms_norm(c_kv, kv_a_g) @ w_kvb).reshape(B, S, MLA_HEADS, MLA_NOPE_DIM + MLA_V_DIM)
    k_nope, v = kv[..., :MLA_NOPE_DIM], kv[..., MLA_NOPE_DIM:]
    k_rope = _rope(k_rope, positions)
    n_blocks = S // Q_BLOCK

    def to_blocks(t):
        return t.reshape(B, n_blocks, Q_BLOCK, *t.shape[2:]).swapaxes(0, 1)

    key_idx = jnp.arange(S)
    scale = MLA_QK_DIM ** -0.5

    def attend(args):
        qn, qr, blk = args
        s = jnp.einsum('bqhd,bkhd->bhqk', qn, k_nope) + jnp.einsum('bqhr,bkr->bhqk', qr, k_rope)
        q_idx = blk * Q_BLOCK + jnp.arange(Q_BLOCK)
        s = jnp.where(key_idx[None, :] <= q_idx[:, None], s.astype(jnp.float32) * scale, -jnp.inf)
        p = jax.nn.softmax(s, axis=-1).astype(v.dtype)
        return jnp.einsum('bhqk,bkhd->bqhd', p, v)

    o = lax.map(attend, (to_blocks(q_nope), to_blocks(q_rope), jnp.arange(n_blocks)))
    return o.swapaxes(0, 1).reshape(B, S, MLA_HEADS, MLA_V_DIM)

def _causal_conv(x, w, b):
    S = x.shape[1]
    xp = jnp.pad(x, ((0, 0), (CONV_WIDTH - 1, 0), (0, 0)))
    return sum(xp[:, j:j + S] * w[j] for j in range(CONV_WIDTH)) + b

def _mlstm(q, k, v, i_pre, f_pre):
    B, S, H, dh = q.shape
    nc = S // CHUNK
    f32 = jnp.float32

    def vec_chunks(t):
        return t.astype(f32).transpose(0, 2, 1, 3).reshape(B, H, nc, CHUNK, dh).transpose(2, 0, 1, 3, 4)

    def gate_chunks(t):
        return t.astype(f32).transpose(0, 2, 1).reshape(B, H, nc, CHUNK).transpose(2, 0, 1, 3)

    xs = (vec_chunks(q) * dh ** -0.5, vec_chunks(k), vec_chunks(v),
          gate_chunks(i_pre),
          gate_chunks(jax.nn.log_sigmoid(f_pre.astype(f32))))
    causal = jnp.tril(jnp.ones((CHUNK, CHUNK), dtype=bool))

    def step(carry, inp):
        C, n, m = carry
        qc, kc, vc, log_i, log_f = inp
        b = jnp.cumsum(log_f, axis=-1)
        b_end = b[..., -1]
        log_d = jnp.where(causal, b[..., :, None] - b[..., None, :] + log_i[..., None, :], -jnp.inf)
        log_inter = b + m[..., None]
        m_t = jnp.maximum(log_inter, jnp.max(log_d, -1))
        w_intra = jnp.exp(log_d - m_t[..., None])
        w_inter = jnp.exp(log_inter - m_t)
        s = jnp.einsum('bhld,bhsd->bhls', qc, kc) * w_intra
        num = jnp.einsum('bhls,bhse->bhle', s, vc) + w_inter[..., None] * jnp.einsum('bhld,bhde->bhle', qc, C)
        den = jnp.sum(s, -1) + w_inter * jnp.einsum('bhld,bhd->bhl', qc, n)
        h = num / jnp.maximum(jnp.abs(den), jnp.exp(-m_t))[..., None]
        log_w = b_end[..., None] - b + log_i
        m_new = jnp.maximum(b_end + m, jnp.max(log_w, -1))
        w_s = jnp.exp(log_w - m_new[..., None])
        decay = jnp.exp(b_end + m - m_new)
        C = decay[..., None, None] * C + jnp.einsum('bhs,bhsd,bhse->bhde', w_s, kc, vc)
        n = decay[..., None] * n + jnp.einsum('bhs,bhsd->bhd', w_s, kc)
        return (C, n, m_new), h

    init = (jnp.zeros((B, H, dh, dh), f32), jnp.zeros((B, H, dh), f32), jnp.zeros((B, H), f32))
    _, h = lax.scan(step, init, xs)
    return h.transpose(1, 2, 0, 3, 4).reshape(B, H, S, dh).transpose(0, 2, 1, 3).astype(q.dtype)

def _moe(x, w_rg, w_re, w_gate, w_up, w_down):
    B, S, D = x.shape
    T = B * S
    xf = x.reshape(T, D)
    g_prob = jax.nn.softmax((xf @ w_rg).astype(jnp.float32), axis=-1)
    g_p, g_top = lax.top_k(g_prob, 1)
    e_logits = (xf @ w_re).astype(jnp.float32).reshape(T, N_GROUPS, EXPERTS_PER_GROUP)
    e_in_group = e_logits[jnp.arange(T), g_top[:, 0]]
    e_p, e_top = lax.top_k(jax.nn.softmax(e_in_group, axis=-1), TOP_K)
    e_p = e_p / jnp.sum(e_p, -1, keepdims=True)
    weights = g_p * e_p
    expert_id = g_top * EXPERTS_PER_GROUP + e_top
    n_assign = T * TOP_K
    flat_e = expert_id.reshape(-1)
    flat_tok = jnp.repeat(jnp.arange(T, dtype=jnp.int32), TOP_K)
    flat_w = weights.reshape(-1)
    order = jnp.argsort(flat_e)
    se, stok, sw = flat_e[order], flat_tok[order], flat_w[order]
    counts = jnp.zeros((N_EXPERTS,), jnp.int32).at[flat_e].add(1)
    starts = jnp.cumsum(counts) - counts
    padded = (counts + EXPERT_BLOCK - 1) // EXPERT_BLOCK * EXPERT_BLOCK
    pad_ends = jnp.cumsum(padded)
    pad_starts = pad_ends - padded
    dest = pad_starts[se] + jnp.arange(n_assign, dtype=jnp.int32) - starts[se]
    n_blocks = -(-n_assign // EXPERT_BLOCK) + N_EXPERTS
    n_slots = n_blocks * EXPERT_BLOCK
    slot_tok = jnp.full((n_slots,), T, jnp.int32).at[dest].set(stok)
    slot_w = jnp.zeros((n_slots,), jnp.float32).at[dest].set(sw)
    block_start = jnp.arange(n_blocks, dtype=jnp.int32) * EXPERT_BLOCK
    block_expert = jnp.minimum(jnp.searchsorted(pad_ends, block_start, side='right'), N_EXPERTS - 1)
    x_pad = jnp.concatenate([xf, jnp.zeros((1, D), xf.dtype)], 0)
    xb = x_pad[slot_tok].reshape(n_blocks, EXPERT_BLOCK, D)

    def expert_block(args):
        xs, e = args
        h = jax.nn.silu(xs @ w_gate[e]) * (xs @ w_up[e])
        return h @ w_down[e]

    yb = lax.map(expert_block, (xb, block_expert)).reshape(n_slots, D)
    yb = yb * slot_w[:, None].astype(yb.dtype)
    out = jnp.zeros((T + 1, D), yb.dtype).at[slot_tok].add(yb)[:T]
    return out.reshape(B, S, D).astype(x.dtype)

def _to_heads(t, n_heads):
    return t.reshape(t.shape[0], t.shape[1], n_heads, t.shape[2] // n_heads)

def setup_inputs(seed: int = 0) -> dict:
    key = jax.random.key(seed)
    ks = jax.random.split(key, 24)
    f32 = jnp.float32

    def nrm(k, shape, scale):
        return jax.random.normal(k, shape, f32) * scale

    x = nrm(ks[0], (BATCH, SEQ, D_MODEL), 1.0)
    positions = jnp.arange(SEQ, dtype=jnp.int32)[None, :] + jax.random.randint(ks[1], (BATCH, 1), 0, 1024, jnp.int32)
    w_in = nrm(ks[2], (DEPTH, D_MODEL, D_IN), D_MODEL ** -0.5)
    conv_w = nrm(ks[3], (DEPTH, CONV_WIDTH, 2 * D_MLSTM), CONV_WIDTH ** -0.5)
    conv_b = nrm(ks[4], (DEPTH, 2 * D_MLSTM), 0.01)
    i_bias = nrm(ks[5], (DEPTH, MLSTM_HEADS), 0.1)
    f_bias = jnp.linspace(3.0, 6.0, MLSTM_HEADS, dtype=f32)[None, :] + nrm(ks[6], (DEPTH, MLSTM_HEADS), 0.1)
    gate_b = jnp.concatenate([i_bias, f_bias], -1)
    q_a_g = 1.0 + nrm(ks[7], (DEPTH, MLA_Q_RANK), 0.02)
    kv_a_g = 1.0 + nrm(ks[8], (DEPTH, MLA_KV_RANK), 0.02)
    w_qb = nrm(ks[9], (DEPTH, MLA_Q_RANK, MLA_HEADS * MLA_QK_DIM), MLA_Q_RANK ** -0.5)
    w_kvb = nrm(ks[10], (DEPTH, MLA_KV_RANK, MLA_HEADS * (MLA_NOPE_DIM + MLA_V_DIM)), MLA_KV_RANK ** -0.5)
    out_g = 1.0 + nrm(ks[11], (DEPTH, D_MIX), 0.02)
    w_out = nrm(ks[12], (DEPTH, D_MIX, D_MODEL), D_MIX ** -0.5 * DN_BETA)
    ln1_g = 1.0 + nrm(ks[13], (DEPTH, D_MODEL), 0.02)
    ln1_b = nrm(ks[14], (DEPTH, D_MODEL), 0.02)
    w_rg = nrm(ks[15], (DEPTH, D_MODEL, N_GROUPS), D_MODEL ** -0.5)
    w_re = nrm(ks[16], (DEPTH, D_MODEL, N_EXPERTS), D_MODEL ** -0.5)
    w_gate = nrm(ks[17], (DEPTH, N_EXPERTS, D_MODEL, D_EXPERT), D_MODEL ** -0.5)
    w_up = nrm(ks[18], (DEPTH, N_EXPERTS, D_MODEL, D_EXPERT), D_MODEL ** -0.5 * DN_BETA)
    w_down = nrm(ks[19], (DEPTH, N_EXPERTS, D_EXPERT, D_MODEL), D_EXPERT ** -0.5 * DN_BETA)
    ln2_g = 1.0 + nrm(ks[20], (DEPTH, D_MODEL), 0.02)
    ln2_b = nrm(ks[21], (DEPTH, D_MODEL), 0.02)
    return {'x': x, 'positions': positions, 'w_in': w_in, 'conv_w': conv_w, 'conv_b': conv_b,
            'gate_b': gate_b, 'q_a_g': q_a_g, 'kv_a_g': kv_a_g, 'w_qb': w_qb, 'w_kvb': w_kvb,
            'out_g': out_g, 'w_out': w_out, 'ln1_g': ln1_g, 'ln1_b': ln1_b, 'w_rg': w_rg, 'w_re': w_re,
            'w_gate': w_gate, 'w_up': w_up, 'w_down': w_down, 'ln2_g': ln2_g, 'ln2_b': ln2_b}

def reference(x, positions, w_in, conv_w, conv_b, gate_b, q_a_g, kv_a_g, w_qb, w_kvb, out_g, w_out,
              ln1_g, ln1_b, w_rg, w_re, w_gate, w_up, w_down, ln2_g, ln2_b):
    B, S, _ = x.shape
    splits = [int(c) for c in np.cumsum(COL_SIZES)[:-1]]
    for l in range(DEPTH):
        proj = x @ w_in[l]
        c_q, c_kv, k_rope, m_q, m_k, m_v, m_o, m_i, m_f = jnp.split(proj, splits, axis=-1)
        a = _mla(c_q, c_kv, k_rope, positions, q_a_g[l], kv_a_g[l], w_qb[l], w_kvb[l])
        qk = jax.nn.silu(_causal_conv(jnp.concatenate([m_q, m_k], -1), conv_w[l], conv_b[l]))
        h = _mlstm(_to_heads(qk[..., :D_MLSTM], MLSTM_HEADS), _to_heads(qk[..., D_MLSTM:], MLSTM_HEADS),
                   _to_heads(m_v, MLSTM_HEADS),
                   m_i + gate_b[l, :MLSTM_HEADS], m_f + gate_b[l, MLSTM_HEADS:])
        h = _head_norm(h) * jax.nn.sigmoid(_to_heads(m_o, MLSTM_HEADS))
        mix = jnp.concatenate([_head_norm(a).reshape(B, S, MLA_HEADS * MLA_V_DIM),
                               h.reshape(B, S, D_MLSTM)], -1) * out_g[l]
        x = _layer_norm(DN_ALPHA * x + mix @ w_out[l], ln1_g[l], ln1_b[l])
        y = _moe(x, w_rg[l], w_re[l], w_gate[l], w_up[l], w_down[l])
        x = _layer_norm(DN_ALPHA * x + y, ln2_g[l], ln2_b[l])
    return x


_drawn_inputs = setup_inputs


def setup_inputs(seed=0):
    import zlib

    import numpy as np

    out = dict(_drawn_inputs(seed))
    spreads = {}
    factors = {'conv_b': 8.0, 'q_a_g': 8.0, 'kv_a_g': 5.38, 'out_g': 6.381}
    for name, (base, spread) in spreads.items():
        noise = np.random.default_rng([zlib.crc32(name.encode()), seed]).standard_normal(out[name].shape)
        drawn = base * np.exp(spread * noise) if base else spread * noise
        out[name] = __import__('jax').numpy.asarray(drawn.astype(out[name].dtype))
    for name, factor in factors.items():
        out[name] = (out[name] * factor).astype(out[name].dtype)
    return out
```

```python
import numpy as np
import concourse.bass as bass
from concourse import mybir
from contextlib import ExitStack

D, S, L = 1024, 512, 2
H, NOPE, ROPE, VD = 8, 64, 32, 64
QK = NOPE + ROPE
QR, KVR = 256, 128
MH, DH = 4, 128
DM = MH * DH
CW = 4
NG, EPG, NE, DE = 8, 8, 64, 256
P = 128
TT = S // P
KC = D // P
ALPHA = (2 * L) ** 0.25
LN_EPS, RMS_EPS = 1e-5, 1e-6
DIN = QR + KVR + ROPE + 4 * DM + 2 * MH
C_CQ, C_Q = 0, QR + KVR + ROPE
C_K, C_V, C_O = C_Q + DM, C_Q + 2 * DM, C_Q + 3 * DM
NA = C_Q
NC2 = (DM + 2 * MH) // 2
CAP = 32
GRP = P // CAP
EG = NE // GRP
SG = 8
G_ALL = EG + SG
SLOT_BYTES = 6144
BIG = 1e30

def constants():
    cols, at = [], {}

    def put(name, a):
        at[name] = (sum(c.shape[1] for c in cols), a.shape[1])
        cols.append(np.broadcast_to(a, (P, a.shape[1])).astype(np.float32))

    i = np.arange(P)
    put("ident", np.eye(P))
    put("upto", (i[:, None] <= i[None, :]) * 1.0)
    put("before", (i[:, None] < i[None, :]) * 1.0)
    put("ones", np.ones((1, P)))
    put("future", np.where(i[None, :] > i[:, None], -BIG, 0.0))
    put("pick", (i[:, None] == np.arange(MH * P)[None, :] // P) * 1.0)
    put("down8", 8.0 - np.arange(8)[None, :])
    half = ROPE // 2
    put("freq", (np.float32(10000.0) ** (-np.arange(half, dtype=np.float32) / np.float32(half)))[None, :])
    put("slot0", CAP * np.arange(NE)[None, :] * 1.0)
    put("caps", CAP * np.arange(1, 16)[None, :] * 1.0)
    put("block", np.arange(32)[None, :] * 1.0)
    put("fours", 4 * np.arange(SG)[None, :] * 1.0)
    put("tok", P * np.arange(TT)[None, :] + i[:, None] * 1.0)
    put("zero", np.zeros((1, NE)))
    return np.ascontiguousarray(np.concatenate(cols, 1)), at


CONST, CAT = constants()

DVE_STEPS, ACT_STEPS = 291, 27

def jobs():
    out = [("vec", "D")]
    out += [(("xt", t, h), "AD"[h]) for t in range(TT) for h in range(2)]
    out += [(("a", t), "D") for t in range(TT)]
    out += [(("o", t, h), "A") for t in range(TT) for h in range(2)]
    out += [(("v", t), "A") for t in range(TT)]
    out += [("cum", "D"), (("cq", 0), "A"), (("cq", 1), "A"), ("ckv", "A"), ("kr", "A")]
    out += [(("q", 0), "D"), (("q", 1), "D"), ("at", "D"), (("q", 2), "D"), (("q", 3), "D")]
    out += [(("k", c), "D") for c in range(MH)] + [("acol", "D")]

    def g(h):
        return [(("abc", h), "A")] + [(("st", h, b), "D") for b in range(TT)]

    def n(h):
        return [(("num", h, b), "D") for b in range(2)]

    def m(h):
        return [(("mt", h), "A")]
    for part in (g(0), g(1), n(0), g(2), m(0), n(1), g(3), m(1), n(2), m(2), n(3), m(3)):
        out += part
    out += [(("kn", h), "AD"[h % 2]) for h in range(H)] + [(("mv", t), "A") for t in range(TT)]

    def q(t):
        return [(("qa", t), "A"), (("qb", t), "A")]

    def qt(t):
        return [(("qt", t, 0), "D"), (("qt", t, 1), "D")]
    for part in (q(0), q(1), qt(0), q(2), qt(1), q(3), qt(2), qt(3)):
        out += part
    for u in range(TT * H + 4):
        if u < TT * H:
            out.append((("s", u), "A"))
        if 2 <= u < TT * H + 2:
            out.append((("pt", u - 2), "D"))
        if u >= 12 and (u - 12) % H == 0:
            out.append((("mx", (u - 12) // H), "A"))
    out += [(("mx", TT - 1), "A")]
    out += [(("out", t, h), "D") for t in range(TT) for h in range(2)]
    out += [(("xt2", t, h), "AD"[h]) for t in range(TT) for h in range(2)]
    out += [("logit", "D"), ("rank", "D")]
    return out


JOBS = jobs()
JOB = {name: j for j, (name, _) in enumerate(JOBS)}
NB = 6


class Signal:

    def __init__(self, sem, per_layer):
        self.sem, self.per, self.n = sem, per_layer, 0

    def up(self):
        self.n += 1
        return self.sem, 1

    def at(self, k):
        assert 0 < k <= self.per, (k, self.per)
        return k


def hybrid_kernel(nc, A, const, out):
    f32, i32 = mybir.dt.float32, mybir.dt.int32
    ALU, ACT, AX = mybir.AluOpType, mybir.ActivationFunctionType, mybir.AxisListType

    x_dram = nc.dram_tensor("x_rows", (S, D), f32, kind="Internal").ap()
    y_dram = nc.dram_tensor("y_slots", (G_ALL * P, D), f32, kind="Internal").ap()
    tab_dram = nc.dram_tensor("slot_tokens", (G_ALL * P, 1), i32, kind="Internal").ap()

    ctx = ExitStack()
    with ctx:
        def sb(name, shape, dt=f32):
            return ctx.enter_context(nc.sbuf_tensor(name, shape, dt))

        ring = [sb(f"ring{i}", [P, SLOT_BYTES]) for i in range(4)]
        X = sb("X", [P, TT, D])
        XT = sb("XT", [P, KC, S])
        R1 = sb("R1", [P, 8 * S])
        R2 = sb("R2", [P, 4224])
        R4 = sb("R4", [P, 4224])
        cqT = sb("cqT", [P, 2, S])
        ckvT = sb("ckvT", [P, S])
        krT = sb("krT", [P, S])
        qtok = [R4[:, 2048 + H * QK * i:2048 + H * QK * (i + 1)].rearrange("p (h d) -> p h d", h=H) for i in range(2)]
        K = sb("K", [P, CONST.shape[1]])
        vecs = R4[0:7, 3200:3200 + D]
        vecT = sb("vecT", [P, KC, 7])
        gate_b = sb("gate_b", [P, 2 * MH])
        wr = sb("wr", [P, KC, NG + NE])
        cos = sb("cos", [P, TT, ROPE // 2])
        sin = sb("sin", [P, TT, ROPE // 2])
        ang = R4[:, 0:192].rearrange("p (a n) -> p a n", a=3)
        turns = sb("turns", [P, TT * ROPE // 2], i32)
        pos_i = sb("pos_i", [P, TT], i32)
        pos_f = sb("pos_f", [P, TT])
        biases = sb("biases", [P, 4])

        def C(name, n=None):
            a, w = CAT[name]
            return K[:, a:a + (n or w)]

        ident = C("ident")
        qkT = R1[:, :].rearrange("p (c t) -> p c t", c=8)
        V1W = TT * MH * (DH + 1)
        v1 = R2[:, 0:V1W].rearrange("p (t h e) -> p t h e", t=TT, h=MH)
        osig = R2[:, V1W:V1W + TT * DM].rearrange("p (t n) -> p t n", t=TT)
        cqkv = R4[:, 0:TT * NA].rearrange("p (t n) -> p t n", t=TT)
        convt = [R4[:, TT * NA + S * i:TT * NA + S * (i + 1)] for i in range(3)]
        PTW = P * (4 + 3 + 2 + 1)
        pt_at = [0, 512, 896, 1152]
        PTm = [R4[:, PTW * i:PTW * (i + 1)] for i in range(2)]
        Wm = [R4[:, 2 * PTW + S * i:2 * PTW + S * (i + 1)] for i in range(2)]
        gates = sb("gates", [P, TT, 2 * MH])
        gt = sb("gt", [P, 3, TT, MH])
        logf = sb("logf", [P, TT, MH])
        Bc = sb("Bc", [P, TT, MH])
        ac = sb("ac", [P, TT, MH])
        em = sb("em", [P, TT, MH])
        Arow = R4[0:MH, 3584:3584 + S]
        hm = [sb(f"hm{i}", [P, TT, DH]) for i in range(2)]
        hsq = sb("hsq", [P, 512])
        arow = hsq[0:MH, :]
        den = sb("den", [P, 4, TT])
        ss = sb("ss", [P, 2, TT])
        qT = R1[:, :].rearrange("p (h t) -> p h t", h=H)
        kT = R2[:, 0:H * S].rearrange("p (h t) -> p h t", h=H)
        mv = R4[:, 0:TT * H * VD].rearrange("p (t n) -> p t n", t=TT)
        Pm = [R4[:, 2048 + S * i:2048 + S * (i + 1)] for i in range(2)]
        PT = [R4[:, 3072 + S * i:3072 + S * (i + 1)] for i in range(2)]
        smx = sb("smx", [P, 2, TT * H])
        ssum = sb("ssum", [P, TT * H])
        mnorm = sb("mnorm", [P, 4, H])
        mix = [h[:, :, :].rearrange("p t e -> p (t e)") for h in hm]
        rtmp = sb("rtmp", [P, 4, H * ROPE // 2])
        lnG, lnB = R1[:, 0:D], R1[:, D:2 * D]
        xg = [R1[:, 2 * D:3 * D], R1[:, 3 * D:4 * D]]
        xgT = [R2[:, 0:D], R2[:, D:2 * D]]
        ysb = [R2[:, 2 * D:3 * D], R2[:, 3 * D:4 * D]]
        stats = sb("stats", [P, 2, 6])
        mvar = sb("mvar", [P, 2])
        rstd = sb("rstd", [P, 2])
        at = [0]

        def r4(*shape):
            n = int(np.prod(shape))
            v = R4[:, at[0]:at[0] + n]
            at[0] += n
            return v if len(shape) == 1 else v.rearrange("p (a b) -> p a b", a=shape[0]) if len(shape) == 2 else \
                v.rearrange("p (a b c) -> p a b c", a=shape[0], b=shape[1])
        lg = r4(TT, NG + NE)
        r8 = r4(8, TT, 8)
        r1 = r4(16, TT)
        OH = [r4(TT, NE) for k in range(2)]
        OHS = r4(TT, NE)
        posb = r4(TT, NE)
        cnt = r4(5, NE)
        esb, hsb, hT = ([r4(64) for _ in range(2)] for _ in range(3))
        rt = ysb[0]
        rt2 = R2[:, 2 * D:4 * D]
        sloti = sb("sloti", [P, 2, TT], i32)
        slt = sb("slt", [P, 3, 2 * TT], i32)
        toki = sb("toki", [P, TT], i32)
        idx_all = sb("idx_all", [P, G_ALL], i32)
        idx = [sb(f"idx{b}", [P, 1], i32) for b in range(2)]
        zero_i = sb("zero_i", [P, G_ALL], i32)
        meta_f = sb("meta_f", [1, 34])
        meta = sb("meta", [1, 34], i32)
        wts = sb("wts", [P, 2, TT])

        PB = ctx.enter_context(nc.psum_tensor("PB", [P, 8, 512], f32))

        cleared = []

        def kept(name):
            return ctx.enter_context(nc.semaphore(name))

        def sem(name):
            cleared.append(kept(name))
            return cleared[-1]

        def sig(name, per):
            return Signal(sem(name), per)

        once = {n: kept(n) for n in (
            "consts_in", "x_in", "pos_in", "rope_step", "rope_ready", "small_set", "tab_zeroed", "y_zeroed", "vecs_in", "gate_b_in",
            "wr_in", "scattered", "idx_in", "y_in0", "y_in1", "main_xg_in0", "main_xg_in1", "spill_xg_in0", "w_a", "w_qkvb", "w_v", "w_o", "out_stored", "arrived", "layer_open", "waited")}
        n_of = {e: sum(1 for _, x in JOBS if x == e) for e in "AD"}
        bank_full = sig("bank_full", len(JOBS))
        emptied = {"A": sig("emptied_by_act", n_of["A"]), "D": sig("emptied_by_dve", n_of["D"])}

        def bank(name):
            return PB[:, JOB[name] % NB, :]

        def full(name):
            return bank_full.sem, bank_full.at(JOB[name] + 1)

        def empty(j):
            e = JOBS[j][1]
            return emptied[e].sem, emptied[e].at(sum(1 for _, x in JOBS[:j + 1] if x == e))

        def emptying(name):
            e = JOBS[JOB[name]][1]
            mine = [n for n, x in JOBS if x == e]
            assert mine[emptied[e].n] == name, (name, mine[emptied[e].n])
            return emptied[e].up()

        consts_in, x_in, pos_in = once["consts_in"], once["x_in"], once["pos_in"]
        rope_step, rope_ready = once["rope_step"], once["rope_ready"]
        small_set, tab_zeroed, y_zeroed = once["small_set"], once["tab_zeroed"], once["y_zeroed"]
        vecs_in, gate_b_in, wr_in, ln_in = once["vecs_in"], once["gate_b_in"], once["wr_in"], sem("ln_in")
        w_a, w_q, w_v, w_o = (once[f"w_{n}"] for n in ("a", "qkvb", "v", "o"))
        w_qm, w_k, w_out = (sem(f"w_{n}") for n in ("q", "k", "out"))
        dstep = sig("dve_step", DVE_STEPS)
        astep = sig("act_step", ACT_STEPS)
        cq_sq = sig("cq_squares", 1)
        cq_ready = sig("cq_ready", 2)
        gates_in = sig("gates_in", 1)
        gate_neg = sig("gate_neg", 1)
        gate_ln = sig("gate_ln", 1)
        logf_ready = sig("logf_ready", 1)
        ac_ready = sig("ac_ready", 1)
        arow_ready = sig("arow_ready", 1)
        m_ready = sig("m_ready", 1)
        em_ready = sig("em_ready", 1)
        conv_ready = sig("conv_ready", 8)
        silu_exp = sig("silu_exp", 8)
        qk_ready = sig("qk_ready", 8)
        v1_ones = sig("v1_ones", 1)
        w_ready = sig("w_ready", MH * TT)
        ptm_written = sig("ptm_written", MH * TT)
        ptm_ready = sig("ptm_ready", MH * TT)
        h_sq = sig("h_sumsq", MH)
        h_rs = sig("h_rstd", MH)
        h_ready = sig("h_ready", MH)
        kr_copied = sig("kr_copied", 1)
        q_turned = sig("q_turned", TT)
        mx_ready = sig("mx_ready", TT * H)
        p_ready = sig("p_ready", TT * H)
        o_full = sig("o_full", TT)
        o_read = sig("o_read", TT)
        o_sq = sig("o_sumsq", TT)
        o_rs = sig("o_rstd", TT)
        mix_ready = sig("mix_ready", TT)
        ln_var = sig("ln_var", 2 * TT)
        ln_rs = sig("ln_rstd", 2 * TT)
        ln_scaled = sig("ln_scaled", 2 * TT)
        x_ready = sig("x_ready", 2 * TT)
        x_stored = sem("x_stored")
        exp_in, exp_out = sig("exp_in", 2), sig("exp_out", 2)
        oh_ready = sig("oh_ready", 1)
        slots_ready = sig("slots_ready", 1)
        meta_ready = sig("meta_ready", 1)
        scattered, idx_in = once["scattered"], once["idx_in"]
        y_in = [once[f"y_in{i}"] for i in range(2)]
        y_used = sig("y_used", TT)
        out_stored, arrived, layer_open, waited = (once[n] for n in ("out_stored", "arrived", "layer_open", "waited"))

        class Path:

            def __init__(self, name, bufs):
                self.w_in = [sem(f"{name}_w_in{q}") for q in range(GRP)]
                self.down = [sem(f"{name}_down{q}") for q in range(GRP)]
                self.idx = [sem(f"{name}_idx{b}") for b in range(bufs)]
                self.xg_in = [once[f"{name}_xg_in{b}"] for b in range(bufs)]
                self.xg_T = [sem(f"{name}_xg_T{b}") for b in range(bufs)]
                self.xgT_a = [sem(f"{name}_xgT_a{b}") for b in range(bufs)]
                self.xgT_d = [sem(f"{name}_xgT_d{b}") for b in range(bufs)]
                self.gu = [sem(f"{name}_gu{i}") for i in range(2)]
                self.ex = [sem(f"{name}_ex{i}") for i in range(2)]
                self.st = [sem(f"{name}_st{i}") for i in range(2)]
                self.hT = [sem(f"{name}_hT{i}") for i in range(2)]
                self.y = [sem(f"{name}_y{i}") for i in range(2)]
                self.ysb = sem(f"{name}_ysb")
                self.stored = [sem(f"{name}_stored{b}") for b in range(bufs)]
                self.bufs = bufs
                self.ahead = [(s, 1) for s in self.down + self.xg_T + self.xgT_a + self.xgT_d + self.st + self.y] \
                    + [(s, 64) for s in self.stored]

        main, spill = Path("main", 2), Path("spill", 1)
        moe_step = {False: sem("moe_step"), True: sem("spill_step")}
        IT = EG // 2

        def turn_wait(eng, semaphore, value):
            eng.wait_ge(semaphore, value)
            eng.sem_inc(waited, 1)

        def stored_all(eng, spilled=None):
            for b in range(2):
                eng.wait_ge(main.stored[b], IT * 64 + 64)
            if spilled is not None:
                turn_wait(eng, spill.stored[0], spilled * 64 + 64)

        def spill_groups(eng):
            eng.wait_ge(meta_ready.sem, meta_ready.at(1))
            return eng.value_load(meta[0:1, 32:33], min_val=0, max_val=SG)

        def end_layer(eng, l):
            eng.drain().then_inc(arrived, 1)
            turn_wait(eng, layer_open, l + 1)

        block = ctx.enter_context(nc.Block())

        @block.sync
        def _(sp):
            sp.dma_start(K[:, :], const).then_inc(consts_in, 16)
            for t in range(TT):
                sp.dma_start(X[:, t, :], A["x"][0, t * P:(t + 1) * P, :]).then_inc(x_in, 16)
            with nc.allow_non_contiguous_dma("512 positions"):
                sp.dma_start(pos_i[:, :], A["positions"][0].rearrange("(t p) -> p t", p=P)).then_inc(pos_in, 16)

            def expert(path, q, l, e):
                r = ring[q]
                sp.dma_start(r[:, 0:2048], A["w_gate"][l, e].rearrange("(p k) f -> p (k f)", k=KC)).then_inc(path.w_in[q], 16)
                sp.dma_start(r[:, 2048:4096], A["w_up"][l, e].rearrange("(p k) f -> p (k f)", k=KC)).then_inc(path.w_in[q], 16)
                sp.dma_start(r[:, 4096:6144].rearrange("p (c n) -> p c n", c=2),
                             A["w_down"][l, e].rearrange("(c p) n -> p c n", p=P)).then_inc(path.w_in[q], 16)

            def cols(l, slot, a, b, s):
                w_in = A["w_in"][l].rearrange("(p k) n -> p k n", k=KC)
                sp.dma_start(ring[slot][:, 0:KC * (b - a)].rearrange("p (k n) -> p k n", k=KC), w_in[:, :, a:b]).then_inc(s, 16)

            def row(t, l):
                return t[l:l + 1] if isinstance(l, int) else t[bass.ds(l, 1)]

            def first_weights(l):
                cols(l, 0, 0, NA, w_a)
                sp.dma_start(vecs[0:4, :], A["conv_w"][l]).then_inc(vecs_in, 16)
                sp.dma_start(vecs[4:5, :], row(A["conv_b"], l)).then_inc(vecs_in, 16)
                sp.dma_start(vecs[5:6, :], row(A["out_g"], l)).then_inc(vecs_in, 16)
                sp.dma_start(vecs[6:7, 0:QR], row(A["q_a_g"], l)).then_inc(vecs_in, 16)
                sp.dma_start(vecs[6:7, QR:QR + KVR], row(A["kv_a_g"], l)).then_inc(vecs_in, 16)
                cols(l, 2, C_O, DIN, w_o)
                sp.dma_start(gate_b[:, :], row(A["gate_b"], l).to_broadcast((P, 2 * MH))).then_inc(gate_b_in, 16)
                cols(l, 3, C_V, C_O, w_v)
                sp.dma_start(ring[1][:, 0:1536].rearrange("p (c n) -> p c n", c=2),
                             A["w_qb"][l].rearrange("(c p) n -> p c n", p=P)).then_inc(w_q, 16)
                sp.dma_start(ring[1][:, 1536:2560], A["w_kvb"][l]).then_inc(w_q, 16)
                sp.dma_start(wr[:, :, 0:NG], A["w_rg"][l].rearrange("(p k) n -> p k n", k=KC)).then_inc(wr_in, 16)
                sp.dma_start(wr[:, :, NG:], A["w_re"][l].rearrange("(p k) n -> p k n", k=KC)).then_inc(wr_in, 16)

            def set_ahead():
                for path in (main, spill):
                    for s, n in path.ahead:
                        sp.sem_inc(s, n)

            first_weights(0)
            set_ahead()
            with sp.Fori(0, L) as l:
                sp.wait_ge(*full(("a", TT - 1)))
                cols(l, 0, C_Q, C_K, w_qm)
                sp.wait_ge(*full(("o", TT - 1, 1)))
                cols(l, 2, C_K, C_V, w_k)
                sp.wait_ge(*full(("v", TT - 1)))
                w_o3 = A["w_out"][l].rearrange("(k p) n -> p k n", p=P)
                sp.dma_start(ring[3][:, 0:4096].rearrange("p (k n) -> p k n", k=KC), w_o3[:, :, 0:512]).then_inc(w_out, 16)
                sp.wait_ge(*full(("k", MH - 1)))
                sp.dma_start(ring[2][:, 0:4096].rearrange("p (k n) -> p k n", k=KC), w_o3[:, :, 512:D]).then_inc(w_out, 16)
                expert(main, 0, l, 0)
                sp.wait_ge(*full(("qb", TT - 1)))
                expert(main, 1, l, 1)
                sp.wait_ge(*full(("s", TT * H - 1)))
                sp.dma_start(lnG, A["ln1_g"][bass.ds(l, 1)].to_broadcast((P, D))).then_inc(ln_in, 16)
                sp.dma_start(lnB, A["ln1_b"][bass.ds(l, 1)].to_broadcast((P, D))).then_inc(ln_in, 16)
                sp.wait_ge(*full(("out", TT - 1, 1)))
                expert(main, 2, l, 2)
                expert(main, 3, l, 3)
                sp.wait_ge(x_ready.sem, x_ready.at(TT))
                sp.dma_start(lnG, A["ln2_g"][bass.ds(l, 1)].to_broadcast((P, D))).then_inc(ln_in, 16)
                sp.dma_start(lnB, A["ln2_b"][bass.ds(l, 1)].to_broadcast((P, D))).then_inc(ln_in, 16)
                with sp.Fori(1, EG) as g:
                    for q in range(GRP):
                        turn_wait(sp, main.down[q], g + 1)
                        expert(main, q, l, g * GRP + q)
                n = spill_groups(sp)
                with sp.If(n > 0):
                    stored_all(sp)
                    with sp.Fori(0, n) as g:
                        for q in range(GRP):
                            turn_wait(sp, spill.down[q], g + 1)
                            e = sp.value_load(meta[0:1, bass.ds(g * GRP + q, 1)], min_val=0, max_val=NE - 1)
                            expert(spill, q, l, e)
                with sp.Else():
                    pass
                stored_all(sp, n)
                with sp.If(l < L - 1):
                    first_weights(L - 1)
                with sp.Else():
                    pass
                turn_wait(sp, arrived, 4 * l + 4)
                numbers = sorted(s.num for s in cleared)
                assert numbers == list(range(numbers[0], numbers[-1] + 1))
                sp.sem_clear(range(numbers[0], numbers[-1] + 1))
                set_ahead()
                sp.sem_inc(layer_open, 1)
            for t in range(TT):
                sp.dma_start(out[0, t * P:(t + 1) * P, :], X[:, t, :]).then_inc(out_stored, 16)
            sp.wait_ge(out_stored, 16 * TT)

        @block.tensor
        def _(pe):
            pe.wait_ge(consts_in, 16)
            pe.wait_ge(x_in, 16 * TT)

            def group(path, b, it, m, gathered):
                turn_wait(pe, path.xg_in[b], gathered * 16)
                if path.bufs == 1:
                    pe.wait_ge(path.xgT_a[0], it + 1)
                    pe.wait_ge(path.xgT_d[0], it + 1)
                else:
                    pe.wait_ge(path.xgT_a[1 - b], it + b + 1)
                    pe.wait_ge(path.xgT_d[1 - b], it + b + 1)
                for k in range(KC):
                    last = nc.tensor.transpose(PB[:, k // 4, (k % 4) * P:(k % 4 + 1) * P],
                                               xg[b].rearrange("p (i k) -> p k i", k=KC)[:, k, :], ident)
                last.then_inc(path.xg_T[b], 1)

                def up(q):
                    pe.wait_ge(path.w_in[q], m * 48 + 48)
                    pe.wait_ge(path.st[q % 2], m * 2 + q // 2 + 1)
                    w = ring[q][:, 0:4096].rearrange("p (g k c j f) -> p g k c j f", g=2, k=KC, c=2, j=4)
                    for k in range(KC):
                        for j in range(4):
                            last = nc.tensor.matmul(PB[32 * j:32 * j + 32, 2 + q % 2, 0:P],
                                                    xgT[b][:, k * P + CAP * q:k * P + CAP * (q + 1)],
                                                    w[:, :, k, :, j, :], start=k == 0, stop=k == KC - 1,
                                                    tile_position=(0, 32 * j), skip_group_check=True)
                    last.then_inc(path.gu[q % 2], 1)

                def down(q):
                    pe.wait_ge(path.hT[q % 2], m * 2 + q // 2 + 1)
                    pe.wait_ge(path.y[q % 2], m * 2 + q // 2 + 1)
                    w = ring[q][:, 4096:6144].rearrange("p (c n) -> p c n", c=2)
                    for c in range(2):
                        for j in range(4):
                            last = nc.tensor.matmul(PB[32 * j:32 * j + 32, 4 + q % 2, 0:256],
                                                    hT[q % 2][:, 32 * c:32 * c + 32], w[:, c, 256 * j:256 * (j + 1)],
                                                    start=c == 0, stop=c == 1, tile_position=(0, 32 * j), skip_group_check=True)
                    last.then_inc(path.down[q], 1)
                pe.wait_ge(path.xgT_a[b], it + 2)
                pe.wait_ge(path.xgT_d[b], it + 2)
                for q in range(GRP):
                    up(q)
                    if q:
                        down(q - 1)
                down(GRP - 1)

            with pe.Fori(0, L) as l:
                def room(name):
                    if JOB[name] >= NB:
                        pe.wait_ge(*empty(JOB[name] - NB))
                    return bank(name)

                def done(ins):
                    ins.then_inc(*bank_full.up())

                turn_wait(pe, vecs_in, l * 80 + 80)
                b = room("vec")
                for k in range(KC):
                    r = 7 if k < 3 else 6
                    last = nc.tensor.transpose(b[:, 8 * k:8 * k + r], vecs[0:r, k * P:(k + 1) * P], K[0:r, 0:r])
                done(last)

                def transpose_x(kind):
                    for t in range(TT):
                        for h in range(2):
                            if kind == "xt2":
                                pe.wait_ge(x_ready.sem, x_ready.at(t + 1))
                            b = room((kind, t, h))
                            xv = X[:, t, :].rearrange("p (i k) -> p k i", k=KC)
                            for k in range(4):
                                last = nc.tensor.transpose(b[:, k * P:(k + 1) * P], xv[:, 4 * h + k, :], ident)
                            done(last)
                transpose_x("xt")

                def xt_ready(kind):
                    pe.wait_ge(*empty(JOB[(kind, TT - 1, 0)]))
                    pe.wait_ge(*empty(JOB[(kind, TT - 1, 1)]))
                xt_ready("xt")

                def tokens(name, t, slot, width, a, n):
                    b = room(name)
                    w = ring[slot][:, 0:KC * width].rearrange("p (k n) -> p k n", k=KC)
                    for k in range(KC):
                        last = nc.tensor.matmul(b[:, 0:n], XT[:, k, t * P:(t + 1) * P], w[:, k, a:a + n],
                                                start=k == 0, stop=k == KC - 1)
                    done(last)
                turn_wait(pe, w_a, l * 16 + 16)
                for t in range(TT):
                    tokens(("a", t), t, 0, NA, 0, NA)
                turn_wait(pe, w_o, l * 16 + 16)
                for t in range(TT):
                    for h in range(2):
                        tokens(("o", t, h), t, 2, 2 * NC2, h * NC2, NC2)
                turn_wait(pe, w_v, l * 16 + 16)
                for t in range(TT):
                    tokens(("v", t), t, 3, DM, 0, DM)
                b = room("cum")
                pe.wait_ge(logf_ready.sem, logf_ready.at(1))
                for t in range(TT):
                    for s in range(t + 1):
                        last = nc.tensor.matmul(b[:, MH * t:MH * (t + 1)], C("upto") if s == t else C("ones"), logf[:, s, :],
                                                start=s == 0, stop=s == t)
                done(last)
                pe.wait_ge(cq_ready.sem, cq_ready.at(2))
                for name, a, n in ((("cq", 0), 0, P), (("cq", 1), P, P), ("ckv", QR, P), ("kr", QR + KVR, ROPE)):
                    b = room(name)
                    for t in range(TT):
                        last = nc.tensor.transpose(b[0:n, t * P:(t + 1) * P], cqkv[:, t, a:a + n], ident)
                    done(last)

                def channels(name, c, slot):
                    b = room(name)
                    w = ring[slot][:, 0:KC * DM].rearrange("p (k n) -> p k n", k=KC)
                    for k in range(KC):
                        last = nc.tensor.matmul(b, w[:, k, c * P:(c + 1) * P], XT[:, k, :], start=k == 0, stop=k == KC - 1)
                    done(last)
                pe.wait_ge(w_qm, 16)
                channels(("q", 0), 0, 0)
                channels(("q", 1), 1, 0)
                b = room("at")
                pe.wait_ge(ac_ready.sem, ac_ready.at(1))
                for t in range(TT):
                    last = nc.tensor.transpose(b[0:MH, t * P:(t + 1) * P], ac[:, t, :], ident)
                done(last)
                channels(("q", 2), 2, 0)
                channels(("q", 3), 3, 0)
                pe.wait_ge(w_k, 16)
                for c in range(MH):
                    channels(("k", c), c, 2)
                b = room("acol")
                pe.wait_ge(arow_ready.sem, arow_ready.at(1))
                for t in range(TT):
                    last = nc.tensor.transpose(b[:, MH * t:MH * (t + 1)], Arow[:, t * P:(t + 1) * P], K[0:MH, 0:MH])
                done(last)

                def scores(h):
                    b = room(("abc", h))
                    done(nc.tensor.matmul(b, C("pick")[0:MH, h * P:(h + 1) * P], Arow[:, :], start=True, stop=True))
                    pe.wait_ge(qk_ready.sem, qk_ready.at(MH + h + 1))
                    for s in range(TT):
                        b = room(("st", h, s))
                        done(nc.tensor.matmul(b[:, 0:S - s * P], qkT[:, MH + h, s * P:(s + 1) * P], qkT[:, h, s * P:S],
                                              start=True, stop=True))

                def numerators(h):
                    for half in range(2):
                        b = room(("num", h, half))
                        pe.wait_ge(ptm_ready.sem, ptm_ready.at(h * TT + 2 * half + 2))
                        for i in range(2):
                            t = 2 * half + i
                            for s in range(t + 1):
                                a = pt_at[s] + (t - s) * P
                                last = nc.tensor.matmul(b[:, i * (DH + 1):(i + 1) * (DH + 1)], PTm[h % 2][:, a:a + P], v1[:, s, h, :],
                                                        start=s == 0, stop=s == t)
                        done(last)

                def h_transposed(h):
                    b = room(("mt", h))
                    pe.wait_ge(h_ready.sem, h_ready.at(h + 1))
                    for t in range(TT):
                        last = nc.tensor.transpose(b[:, t * P:(t + 1) * P], hm[h % 2][:, t, :], ident)
                    done(last)
                scores(0)
                scores(1)
                pe.wait_ge(v1_ones.sem, v1_ones.at(1))
                pe.wait_ge(*empty(JOB[("v", TT - 1)]))
                numerators(0)
                scores(2)
                h_transposed(0)
                numerators(1)
                scores(3)
                h_transposed(1)
                numerators(2)
                h_transposed(2)
                numerators(3)
                h_transposed(3)

                turn_wait(pe, w_q, l * 32 + 32)
                wq = ring[1][:, 0:1536].rearrange("p (c n) -> p c n", c=2)
                wkv = ring[1][:, 1536:2560].rearrange("p (h n) -> p h n", h=H)
                for h in range(H):
                    b = room(("kn", h))
                    done(nc.tensor.matmul(b[0:NOPE, :], wkv[:, h, 0:NOPE], ckvT[:, :], start=True, stop=True))
                for t in range(TT):
                    b = room(("mv", t))
                    done(nc.tensor.matmul(b, ckvT[:, t * P:(t + 1) * P], wkv[:, :, NOPE:], start=True, stop=True))

                def queries(t):
                    for n, name in enumerate(("qa", "qb")):
                        b = room((name, t))
                        for c in range(2):
                            last = nc.tensor.matmul(b[:, 0:384], cqT[:, c, t * P:(t + 1) * P], wq[:, c, 384 * n:384 * (n + 1)],
                                                    start=c == 0, stop=c == 1)
                        done(last)

                def queries_transposed(t):
                    pe.wait_ge(q_turned.sem, q_turned.at(t + 1))
                    for n in range(2):
                        b = room(("qt", t, n))
                        for i in range(4):
                            last = nc.tensor.transpose(b[0:QK, i * P:(i + 1) * P], qtok[t % 2][:, 4 * n + i, :], ident)
                        done(last)
                queries(0)
                queries(1)
                queries_transposed(0)
                queries(2)
                queries_transposed(1)
                queries(3)
                queries_transposed(2)
                queries_transposed(3)
                pe.wait_ge(*empty(JOB[("qt", TT - 1, 1)]))
                pe.wait_ge(*empty(JOB[("kn", H - 1)]))
                pe.wait_ge(*empty(JOB[("mv", TT - 1)]))
                pe.wait_ge(kr_copied.sem, kr_copied.at(1))

                def mix_transposed(t):
                    b = room(("mx", t))
                    pe.wait_ge(mix_ready.sem, mix_ready.at(t + 1))
                    for k in range(4):
                        last = nc.tensor.transpose(b[:, k * P:(k + 1) * P], mix[t % 2][:, k * P:(k + 1) * P], ident)
                    done(last)
                for u in range(TT * H + 4):
                    if u < TT * H:
                        t, h = divmod(u, H)
                        b = room(("s", u))
                        done(nc.tensor.matmul(b[:, 0:(t + 1) * P], qT[0:QK, h, t * P:(t + 1) * P], kT[0:QK, h, 0:(t + 1) * P],
                                              start=True, stop=True))
                    if 2 <= u < TT * H + 2:
                        t = (u - 2) // H
                        b = room(("pt", u - 2))
                        pe.wait_ge(p_ready.sem, p_ready.at(u - 1))
                        for s in range(t + 1):
                            last = nc.tensor.transpose(b[:, s * P:(s + 1) * P], Pm[u % 2][:, s * P:(s + 1) * P], ident)
                        done(last)
                    if 3 <= u < TT * H + 3:
                        t, h = divmod(u - 3, H)
                        if h == 0 and t >= 2:
                            pe.wait_ge(o_read.sem, o_read.at(t - 1))
                        pe.wait_ge(*empty(JOB[("pt", u - 3)]))
                        for s in range(t + 1):
                            last = nc.tensor.matmul(PB[:, 6 + t % 2, VD * h:VD * (h + 1)], PT[(u - 3) % 2][:, s * P:(s + 1) * P],
                                                    mv[:, s, VD * h:VD * (h + 1)], start=s == 0, stop=s == t)
                        if h == H - 1:
                            last.then_inc(*o_full.up())
                    if u >= 12 and (u - 12) % H == 0:
                        mix_transposed((u - 12) // H)
                mix_transposed(TT - 1)

                pe.wait_ge(w_out, 32)
                pe.wait_ge(*empty(JOB[("mt", MH - 1)]))
                pe.wait_ge(*empty(JOB[("mx", TT - 1)]))
                for t in range(TT):
                    for h in range(2):
                        b = room(("out", t, h))
                        w = ring[3 - h][:, 0:4096].rearrange("p (k n) -> p k n", k=KC)
                        for k in range(KC):
                            last = nc.tensor.matmul(b, XT[:, k, t * P:(t + 1) * P], w[:, k, :], start=k == 0, stop=k == KC - 1)
                        done(last)
                transpose_x("xt2")
                xt_ready("xt2")
                turn_wait(pe, wr_in, l * 32 + 32)
                b = room("logit")
                for t in range(TT):
                    for k in range(KC):
                        last = nc.tensor.matmul(b[:, 72 * t:72 * (t + 1)], XT[:, k, t * P:(t + 1) * P], wr[:, k, :],
                                                start=k == 0, stop=k == KC - 1)
                done(last)
                b = room("rank")
                pe.wait_ge(oh_ready.sem, oh_ready.at(1))
                for t in range(TT):
                    for s in range(t + 1):
                        nc.tensor.matmul(b[:, NE * t:NE * (t + 1)], C("before") if s == t else C("ones"), OHS[:, s, :],
                                         start=s == 0, stop=s == t)
                for s in range(TT):
                    last = nc.tensor.matmul(b[:, NE * TT:NE * (TT + 1)], C("ones"), OHS[:, s, :], start=s == 0, stop=s == TT - 1)
                done(last)
                pe.wait_ge(*empty(JOB["rank"]))
                with pe.Fori(0, IT) as i:
                    for b in range(2):
                        group(main, b, i, i * 2 + b, l * IT + i + 1)
                n = spill_groups(pe)
                before = pe.value_load(meta[0:1, 33:34], min_val=0, max_val=SG * L)
                with pe.If(n > 0):
                    stored_all(pe)
                    with pe.Fori(0, n) as g:
                        group(spill, 0, g, g, before + g + 1)
                with pe.Else():
                    pass
                end_layer(pe, l)

        @block.scalar
        def _(act):
            act.wait_ge(rope_ready, 1)
            nc.scalar.activation(sin[:, :, :].rearrange("p t f -> p (t f)"), ang[:, 0, :], ACT.Sin).then_inc(rope_ready, 1)
            nc.scalar.activation(cos[:, :, :].rearrange("p t f -> p (t f)"), ang[:, 1, :], ACT.Sin).then_inc(rope_ready, 1)
            act.wait_ge(small_set, 6)

            def group(path, b, it, m):
                act.wait_ge(path.xg_T[b], it + 2)
                nc.scalar.copy(xgT[b][:, 0:512], PB[:, 0, :]).then_inc(path.xgT_a[b], 1)
                turn_wait(act, path.stored[b], it * 64 + 64)

                def gate(q):
                    act.wait_ge(path.gu[q % 2], m * 2 + q // 2 + 1)
                    act.wait_ge(path.st[q % 2], m * 2 + q // 2 + 1)
                    nc.scalar.activation(esb[q % 2][:, :], PB[:, 2 + q % 2, 0:64], ACT.Exp, scale=-1.0).then_inc(path.ex[q % 2], 1)

                def result(q):
                    act.wait_ge(path.down[q], m + 2)
                    nc.scalar.copy(ysb[b][:, 256 * q:256 * (q + 1)], PB[:, 4 + q % 2, 0:256]).then_inc(path.y[q % 2], 1)
                for q in range(GRP):
                    gate(q)
                    if q:
                        result(q - 1)
                result(GRP - 1)
                for i in range(2):
                    act.wait_ge(path.y[i], m * 2 + 3)

            def store(path, b, slot):
                for j in range(4):
                    act.dma_start(y_dram[bass.ds(slot, P), 256 * j:256 * (j + 1)].rearrange("(q s) n -> s q n", q=GRP),
                                  ysb[b][32 * j:32 * (j + 1), :].rearrange("p (q n) -> p q n", q=GRP)).then_inc(path.stored[b], 16)

            with act.Fori(0, L) as l:
                def link(ins):
                    ins.then_inc(*astep.up())
                    act.wait_ge(astep.sem, astep.at(astep.n))

                def take(name):
                    act.wait_ge(*full(name))
                    return bank(name)

                def xt(kind):
                    for t in range(TT):
                        b = take((kind, t, 0))
                        nc.scalar.copy(XT[:, 0:4, t * P:(t + 1) * P], b.rearrange("p (k i) -> p k i", k=4)).then_inc(*emptying((kind, t, 0)))
                xt("xt")
                for t in range(TT):
                    for h in range(2):
                        b = take(("o", t, h))
                        n = NC2 if h == 0 else DM - NC2
                        e = nc.scalar.activation(osig[:, t, h * NC2:h * NC2 + n], b[:, 0:n], ACT.Exp, scale=-1.0)
                        if h:
                            e = nc.scalar.copy(gates[:, t, :], b[:, n:n + 2 * MH])
                        e.then_inc(*emptying(("o", t, h)))
                act.wait_ge(gate_neg.sem, gate_neg.at(1))
                link(nc.scalar.activation(gt[:, 1], gt[:, 0], ACT.Exp))
                nc.scalar.activation(gt[:, 2], gt[:, 1], ACT.Ln, bias=biases[:, 2:3]).then_inc(*gate_ln.up())
                act.wait_ge(*empty(JOB[("a", TT - 1)]))
                for t in range(TT):
                    link(nc.scalar.activation(hm[0][:, 0:2, :].rearrange("p t e -> p (t e)"), cqkv[:, t, 0:QR], ACT.Square, accum_out=ss[:, 0, t:t + 1]))
                    link(nc.scalar.activation(hm[0][:, 2, :], cqkv[:, t, QR:QR + KVR], ACT.Square, accum_out=ss[:, 1, t:t + 1]))
                link(nc.scalar.activation(ss[:, 0, :], ss[:, 0, :], ACT.Ln, bias=biases[:, 1:2], scale=1.0 / QR))
                link(nc.scalar.activation(ss[:, 1, :], ss[:, 1, :], ACT.Ln, bias=biases[:, 1:2], scale=1.0 / KVR))
                nc.scalar.activation(ss[:, :, :], ss[:, :, :], ACT.Exp, scale=-0.5).then_inc(*cq_sq.up())
                for t in range(TT):
                    b = take(("v", t))
                    nc.scalar.copy(v1[:, t, :, 0:DH], b.rearrange("p (h e) -> p h e", h=MH)).then_inc(*emptying(("v", t)))
                for c in range(2):
                    b = take(("cq", c))
                    nc.scalar.activation(cqT[:, c, :], b, ACT.Identity, scale=vecT[:, c, 6:7]).then_inc(*emptying(("cq", c)))
                b = take("ckv")
                nc.scalar.activation(ckvT[:, :], b, ACT.Identity, scale=vecT[:, 2, 6:7]).then_inc(*emptying("ckv"))
                b = take("kr")
                nc.scalar.copy(krT[NOPE:QK, :], b[0:ROPE, :]).then_inc(*emptying("kr"))
                for c in range(8):
                    act.wait_ge(conv_ready.sem, conv_ready.at(c + 1))
                    if c >= 1:
                        act.wait_ge(qk_ready.sem, qk_ready.at(c))
                    nc.scalar.activation(convt[2], convt[c % 2], ACT.Exp, scale=-1.0).then_inc(*silu_exp.up())
                act.wait_ge(m_ready.sem, m_ready.at(1))
                nc.scalar.activation(em[:, :, :], gt[:, 0], ACT.Exp, scale=-1.0).then_inc(*em_ready.up())

                def weights(h):
                    b = take(("abc", h))
                    for s in range(TT):
                        i = h * TT + s
                        if i >= 2:
                            act.wait_ge(ptm_written.sem, ptm_written.at(i - 1))
                        else:
                            act.wait_ge(qk_ready.sem, qk_ready.at(8))
                        w = nc.scalar.activation(Wm[i % 2][:, 0:S - s * P], b[:, s * P:S], ACT.Exp, bias=ac[:, s, h:h + 1], scale=-1.0)
                        if s == TT - 1:
                            w.then_inc(*emptying(("abc", h)))
                            act.wait_ge(*empty(JOB[("abc", h)]))
                            nc.scalar.sem_inc(w_ready.up()[0], 1)
                        else:
                            w.then_inc(*w_ready.up())

                def rsqrt(buf, n, eps, s_in, s_out, k):
                    act.wait_ge(s_in.sem, s_in.at(k))
                    link(nc.scalar.activation(buf, buf, ACT.Ln, bias=biases[:, eps:eps + 1], scale=1.0 / n))
                    nc.scalar.activation(buf, buf, ACT.Exp, scale=-0.5).then_inc(*s_out.up())

                def mix_m(h):
                    b = take(("mt", h))
                    nc.scalar.activation(XT[:, 4 + h, :], b, ACT.Identity, scale=vecT[:, 4 + h, 5:6]).then_inc(*emptying(("mt", h)))
                weights(0)
                weights(1)
                rsqrt(den[:, 3, :], DH, 1, h_sq, h_rs, 1)
                weights(2)
                mix_m(0)
                rsqrt(den[:, 3, :], DH, 1, h_sq, h_rs, 2)
                weights(3)
                mix_m(1)
                rsqrt(den[:, 3, :], DH, 1, h_sq, h_rs, 3)
                mix_m(2)
                rsqrt(den[:, 3, :], DH, 1, h_sq, h_rs, 4)
                mix_m(3)
                act.wait_ge(h_ready.sem, h_ready.at(MH))
                for h in range(0, H, 2):
                    b = take(("kn", h))
                    nc.scalar.copy(kT[0:NOPE, h, :], b[0:NOPE, :]).then_inc(*emptying(("kn", h)))
                for t in range(TT):
                    b = take(("mv", t))
                    nc.scalar.copy(mv[:, t, :], b).then_inc(*emptying(("mv", t)))
                for t in range(TT):
                    if t >= 2:
                        act.wait_ge(*full(("qt", t - 2, 1)))
                    for n, name in enumerate(("qa", "qb")):
                        b = take((name, t))
                        nc.scalar.copy(qtok[t % 2][:, 4 * n:4 * n + 4, :].rearrange("p h d -> p (h d)"), b[:, 0:384]).then_inc(*emptying((name, t)))

                def mix_a(t):
                    b = take(("mx", t))
                    for k in range(4):
                        e = nc.scalar.activation(XT[:, k, t * P:(t + 1) * P], b[:, k * P:(k + 1) * P], ACT.Identity, scale=vecT[:, k, 5:6])
                    e.then_inc(*emptying(("mx", t)))
                for u in range(TT * H):
                    t, h = divmod(u, H)
                    act.wait_ge(mx_ready.sem, mx_ready.at(u + 1))
                    if u >= 2:
                        act.wait_ge(*full(("pt", u - 2)))
                    n = (t + 1) * P
                    b = bank(("s", u))
                    e = nc.scalar.activation(Pm[u % 2][:, 0:n], b[:, 0:n], ACT.Exp, bias=smx[:, 1, u:u + 1], scale=QK ** -0.5,
                                             accum_out=ssum[:, u:u + 1])
                    e.then_inc(*emptying(("s", u)))
                    act.wait_ge(*empty(JOB[("s", u)]))
                    nc.scalar.sem_inc(p_ready.up()[0], 1)
                    if h == 3 and t >= 1:
                        rsqrt(mnorm[:, 2 + (t - 1) % 2, :], VD, 1, o_sq, o_rs, t)
                    if h == 4 and t >= 1:
                        pass
                    if u >= 12 and (u - 12) % H == 0:
                        mix_a((u - 12) // H)
                rsqrt(mnorm[:, 2 + (TT - 1) % 2, :], VD, 1, o_sq, o_rs, TT)
                mix_a(TT - 1)

                for t in range(TT):
                    rsqrt(rstd[:, t % 2:t % 2 + 1], 1, 0, ln_var, ln_rs, t + 1)
                for t in range(TT):
                    act.wait_ge(x_ready.sem, x_ready.at(t + 1))
                    act.dma_start(x_dram[t * P:(t + 1) * P, :], X[:, t, :]).then_inc(x_stored, 16)
                xt("xt2")
                for k, (i, o) in enumerate(((r8[:, 1], r8[:, 2]), (r1[:, 6, :], r1[:, 7, :]))):
                    act.wait_ge(exp_in.sem, exp_in.at(k + 1))
                    nc.scalar.activation(o, i, ACT.Exp).then_inc(*exp_out.up())
                act.wait_ge(slots_ready.sem, slots_ready.at(1))
                act.wait_ge(meta_ready.sem, meta_ready.at(1))
                with act.Fori(0, IT) as i:
                    for b in range(2):
                        group(main, b, i, i * 2 + b)
                        store(main, b, (i * 2 + b) * P)
                n = spill_groups(act)
                with act.If(n > 0):
                    stored_all(act)
                    with act.Fori(0, n) as g:
                        group(spill, 0, g, g)
                        store(spill, 0, (g + EG) * P)
                with act.Else():
                    pass
                stored_all(act, n)
                for t in range(TT):
                    rsqrt(rstd[:, t % 2:t % 2 + 1], 1, 0, ln_var, ln_rs, TT + t + 1)
                end_layer(act, l)

        @block.vector
        def _(dve):
            V = nc.vector
            V.memset(biases[:, 0:1], LN_EPS).then_inc(small_set, 1)
            V.memset(biases[:, 1:2], RMS_EPS).then_inc(small_set, 1)
            V.memset(biases[:, 2:3], 1.0).then_inc(small_set, 1)
            V.memset(meta_f[:, :], 0.0).then_inc(small_set, 1)
            V.memset(zero_i[:, :], 0).then_inc(small_set, 1)
            dve.wait_ge(consts_in, 16)
            V.tensor_copy(toki[:, :], C("tok")).then_inc(small_set, 1)
            dve.wait_ge(pos_in, 16)
            steps = [0]

            def rope(ins):
                steps[0] += 1
                ins.then_inc(rope_step, 1)
                dve.wait_ge(rope_step, steps[0])
            rope(V.tensor_copy(pos_f[:, :], pos_i[:, :]))
            HF = ROPE // 2
            for t in range(TT):
                rope(V.tensor_scalar(ang[:, 2, HF * t:HF * (t + 1)], C("freq"), pos_f[:, t:t + 1], None, ALU.mult))
            two_pi = 2 * np.pi
            c1 = float(np.float32(6.28125))
            c2 = float(np.float32(np.float64(two_pi - c1)).view(np.int32) & -4096) if False else float(np.float32(round((two_pi - c1) * 2 ** 19) / 2 ** 19))
            c3 = float(np.float32(two_pi - c1 - c2))
            for o, shift in ((0, 0.0), (1, 0.25)):
                a = ang[:, o, :]
                rope(V.tensor_scalar(a, ang[:, 2, :], 1.0 / two_pi, shift, ALU.mult, ALU.add))
                rope(V.tensor_copy(turns[:, :], a))
                rope(V.tensor_copy(pos_t := hsq[:, 0:TT * HF], turns[:, :]))
                rope(V.scalar_tensor_tensor(a, pos_t, -c1, ang[:, 2, :], ALU.mult, ALU.add))
                rope(V.scalar_tensor_tensor(a, pos_t, -c2, a, ALU.mult, ALU.add))
                rope(V.scalar_tensor_tensor(a, pos_t, -c3, a, ALU.mult, ALU.add))
                if o:
                    rope(V.tensor_scalar(a, a, float(np.pi / 2), None, ALU.add))
                over = hsq[:, 64:64 + TT * HF]
                for sign in (1.0, -1.0):
                    rope(V.tensor_scalar(over, a, sign, float(np.pi), ALU.mult, ALU.is_gt))
                    rope(V.scalar_tensor_tensor(a, over, -sign * two_pi, a, ALU.mult, ALU.add))
                last = V.tensor_scalar(a, a, float(np.float32(3.1415925)), -float(np.float32(3.1415925)), ALU.min, ALU.max)
                steps[0] += 1
                last.then_inc(rope_step, 1)
            dve.wait_ge(rope_step, steps[0])
            V.sem_inc(rope_ready, 1)
            dve.wait_ge(rope_ready, 3)
            dve.wait_ge(small_set, 6)

            def group(path, b, it, m):
                dve.wait_ge(path.xg_T[b], it + 2)
                V.tensor_copy(xgT[b][:, 512:D], PB[:, 1, :]).then_inc(path.xgT_d[b], 1)
                for q in range(GRP):
                    i, n = q % 2, m * 2 + q // 2
                    dve.wait_ge(path.ex[i], n + 1)
                    g2, u2 = PB[:, 2 + i, 0:64], PB[:, 2 + i, 64:P]
                    V.tensor_scalar(esb[i][:, :], esb[i][:, :], 1.0, None, ALU.add).then_inc(moe_step[path is spill], 1)
                    dve.wait_ge(moe_step[path is spill], m * 12 + q * 3 + 1)
                    V.reciprocal(esb[i][:, :], esb[i][:, :]).then_inc(moe_step[path is spill], 1)
                    dve.wait_ge(moe_step[path is spill], m * 12 + q * 3 + 2)
                    V.tensor_tensor(esb[i][:, :], g2, esb[i][:, :], ALU.mult).then_inc(moe_step[path is spill], 1)
                    dve.wait_ge(moe_step[path is spill], m * 12 + q * 3 + 3)
                    V.tensor_tensor(hsb[i][:, :], u2, esb[i][:, :], ALU.mult).then_inc(path.st[i], 1)
                    dve.wait_ge(path.st[i], n + 2)
                    if q >= 2:
                        dve.wait_ge(path.down[q - 2], m + 2)
                    else:
                        dve.wait_ge(path.down[q + 2], m + 1)
                    V.transpose(hT[i][:, :], hsb[i][:, :]).then_inc(path.hT[i], 1)

            with dve.Fori(0, L) as l:
                def link(ins):
                    ins.then_inc(*dstep.up())
                    dve.wait_ge(dstep.sem, dstep.at(dstep.n))

                def take(name):
                    dve.wait_ge(*full(name))
                    return bank(name)

                b = take("vec")
                bv = b[:, 0:8 * KC].rearrange("p (k r) -> p k r", k=KC)
                link(V.tensor_copy(vecT[:, :, 0:6], bv[:, :, 0:6]))
                V.tensor_copy(vecT[:, 0:3, 6:7], bv[:, 0:3, 6:7]).then_inc(*emptying("vec"))

                def xt(kind):
                    for t in range(TT):
                        b = take((kind, t, 1))
                        V.tensor_copy(XT[:, 4:8, t * P:(t + 1) * P], b.rearrange("p (k i) -> p k i", k=4)).then_inc(*emptying((kind, t, 1)))
                xt("xt")
                for t in range(TT):
                    b = take(("a", t))
                    V.tensor_copy(cqkv[:, t, :], b[:, 0:NA]).then_inc(*emptying(("a", t)))
                dve.wait_ge(*empty(JOB[("a", TT - 1)]))
                rt_ = [rtmp[:, i, 0:TT * HF].rearrange("p (t f) -> p t f", t=TT) for i in range(4)]
                k1, k2 = cqkv[:, :, QR + KVR:QR + KVR + HF], cqkv[:, :, QR + KVR + HF:NA]

                def turn(x1, x2, cs, sn, tmp, last_signal):
                    V.tensor_tensor(tmp[0], x1, cs, ALU.mult)
                    V.tensor_tensor(tmp[1], x2, sn, ALU.mult)
                    V.tensor_tensor(tmp[2], x2, cs, ALU.mult)
                    link(V.tensor_tensor(tmp[3], x1, sn, ALU.mult))
                    V.tensor_tensor(x1, tmp[0], tmp[1], ALU.subtract)
                    V.tensor_tensor(x2, tmp[2], tmp[3], ALU.add).then_inc(*last_signal.up())
                turn(k1, k2, cos[:, :, :], sin[:, :, :], rt_, cq_ready)
                dve.wait_ge(*empty(JOB[("o", TT - 1, 1)]))
                turn_wait(dve, gate_b_in, l * 16 + 16)
                link(V.tensor_tensor(gates[:, :, :], gates[:, :, :], gate_b[:, :].unsqueeze(1).to_broadcast((P, TT, 2 * MH)), ALU.add))
                gi, gf = gates[:, :, 0:MH], gates[:, :, MH:]
                link(V.tensor_scalar(gt[:, 1], gf, -1.0, None, ALU.mult))
                V.tensor_tensor(gt[:, 0], gt[:, 1], gf, ALU.min).then_inc(*gate_neg.up())
                link(V.tensor_scalar(osig[:, :, :], osig[:, :, :], 1.0, None, ALU.add))
                link(V.reciprocal(osig[:, :, :], osig[:, :, :]))
                dve.wait_ge(gate_ln.sem, gate_ln.at(1))
                V.scalar_tensor_tensor(logf[:, :, :], gf, 0.0, gt[:, 2], ALU.min, ALU.subtract).then_inc(*logf_ready.up())
                dve.wait_ge(cq_sq.sem, cq_sq.at(1))
                for t in range(TT):
                    V.tensor_scalar(cqkv[:, t, 0:QR], cqkv[:, t, 0:QR], ss[:, 0, t:t + 1], None, ALU.mult)
                    last = V.tensor_scalar(cqkv[:, t, QR:QR + KVR], cqkv[:, t, QR:QR + KVR], ss[:, 1, t:t + 1], None, ALU.mult)
                last.then_inc(*cq_ready.up())
                b = take("cum")
                bc = b[:, 0:TT * MH].rearrange("p (t h) -> p t h", t=TT)
                link(V.tensor_copy(Bc[:, :, :], bc))
                V.tensor_tensor(ac[:, :, :], gi, Bc[:, :, :], ALU.subtract).then_inc(*emptying("cum"))
                dve.wait_ge(*empty(JOB["cum"]))
                V.sem_inc(ac_ready.up()[0], 1)

                def conv(c):
                    name = ("q", c) if c < MH else ("k", c - MH)
                    b = take(name)
                    y = convt[c % 2]
                    link(V.tensor_scalar(y, b, vecT[:, c, 3:4], vecT[:, c, 4:5], ALU.mult, ALU.add))
                    for j in range(1, CW):
                        last = V.scalar_tensor_tensor(y[:, j:S], b[:, 0:S - j], vecT[:, c, 3 - j:4 - j], y[:, j:S], ALU.mult, ALU.add)
                        if j < CW - 1:
                            link(last)
                    last.then_inc(*emptying(name))
                    dve.wait_ge(*empty(JOB[name]))
                    V.sem_inc(conv_ready.up()[0], 1)

                def silu(c):
                    dve.wait_ge(silu_exp.sem, silu_exp.at(c + 1))
                    link(V.tensor_scalar(convt[2], convt[2], 1.0, None, ALU.add))
                    link(V.reciprocal(convt[2], convt[2]))
                    V.tensor_tensor(qkT[:, c, :], convt[c % 2], convt[2], ALU.mult).then_inc(*qk_ready.up())
                dve.wait_ge(y_zeroed, 16 * SG)
                conv(0)
                conv(1)
                silu(0)
                b = take("at")
                link(V.tensor_copy(arow[:, :], b[0:MH, :]))
                V.tensor_tensor_scan(Arow[:, :], arow[:, :], arow[:, :], 0.0, ALU.max, ALU.max).then_inc(*emptying("at"))
                dve.wait_ge(*empty(JOB["at"]))
                V.sem_inc(arow_ready.up()[0], 1)
                for c in range(2, 8):
                    dve.wait_ge(qk_ready.sem, qk_ready.at(c - 1))
                    conv(c)
                    silu(c - 1)
                silu(7)
                b = take("acol")
                V.tensor_tensor(gt[:, 0], b[:, 0:TT * MH].rearrange("p (t h) -> p t h", t=TT), Bc[:, :, :], ALU.add).then_inc(*emptying("acol"))
                dve.wait_ge(*empty(JOB["acol"]))
                V.sem_inc(m_ready.up()[0], 1)

                def weigh(h):
                    for s in range(TT):
                        b = take(("st", h, s))
                        dve.wait_ge(w_ready.sem, w_ready.at(h * TT + s + 1))
                        if h >= 2 and s == 0:
                            dve.wait_ge(*full(("num", h - 2, 1)))
                        n = S - s * P
                        V.scalar_tensor_tensor(PTm[h % 2][:, pt_at[s]:pt_at[s] + n], b[:, 0:n], DH ** -0.5, Wm[(h * TT + s) % 2][:, 0:n],
                                               ALU.mult, ALU.mult).then_inc(*emptying(("st", h, s)))
                        dve.wait_ge(*empty(JOB[("st", h, s)]))
                        V.sem_inc(ptm_written.up()[0], 1)

                def normalise(h):
                    d, o = den, hm[h % 2]
                    for i in range(2):
                        b = take(("num", h, i))
                        bv = b[:, 0:2 * (DH + 1)].rearrange("p (t e) -> p t e", t=2)
                        dv = d[:, 0, 2 * i:2 * i + 2].unsqueeze(2)
                        link(V.tensor_copy(dv, bv[:, :, DH:]))
                        link(V.tensor_scalar(d[:, 1, 2 * i:2 * i + 2], d[:, 0, 2 * i:2 * i + 2], -1.0, None, ALU.mult))
                        link(V.tensor_tensor(d[:, 0, 2 * i:2 * i + 2], d[:, 0, 2 * i:2 * i + 2], d[:, 1, 2 * i:2 * i + 2], ALU.max))
                        if i == 0 and h == 0:
                            dve.wait_ge(em_ready.sem, em_ready.at(1))
                        link(V.tensor_tensor(d[:, 0, 2 * i:2 * i + 2], d[:, 0, 2 * i:2 * i + 2], em[:, 2 * i:2 * i + 2, h], ALU.max))
                        link(V.reciprocal(d[:, 1, 2 * i:2 * i + 2], d[:, 0, 2 * i:2 * i + 2]))
                        if i == 0 and h >= 2:
                            dve.wait_ge(*full(("mt", h - 2)))
                        V.tensor_tensor(o[:, 2 * i:2 * i + 2, :], bv[:, :, 0:DH], d[:, 1, 2 * i:2 * i + 2].unsqueeze(2).to_broadcast((P, 2, DH)),
                                        ALU.mult).then_inc(*emptying(("num", h, i)))
                    dve.wait_ge(*empty(JOB[("num", h, 1)]))
                    hs = hsq[:, :].rearrange("p (t e) -> p t e", t=TT)
                    link(V.tensor_tensor(hs, o[:, :, :], o[:, :, :], ALU.mult))
                    V.reduce_sum(d[:, 3, :], hs, AX.X).then_inc(*h_sq.up())
                    dve.wait_ge(h_rs.sem, h_rs.at(h + 1))
                    link(V.tensor_tensor(o[:, :, :], o[:, :, :], d[:, 3, :].unsqueeze(2).to_broadcast((P, TT, DH)), ALU.mult))
                    V.tensor_tensor(o[:, :, :], o[:, :, :], osig[:, :, h * DH:(h + 1) * DH], ALU.mult).then_inc(*h_ready.up())
                weigh(0)
                weigh(1)
                normalise(0)
                weigh(2)
                normalise(1)
                weigh(3)
                normalise(2)
                normalise(3)
                for h in range(1, H, 2):
                    b = take(("kn", h))
                    V.tensor_copy(kT[0:NOPE, h, :], b[0:NOPE, :]).then_inc(*emptying(("kn", h)))
                cs8 = [cos[:, t, :].unsqueeze(1).to_broadcast((P, H, HF)) for t in range(TT)]
                sn8 = [sin[:, t, :].unsqueeze(1).to_broadcast((P, H, HF)) for t in range(TT)]
                rt8 = [rtmp[:, i, :].rearrange("p (h f) -> p h f", h=H) for i in range(4)]

                def turn_q(t):
                    dve.wait_ge(*empty(JOB[("qb", t)]))
                    if t:
                        dve.wait_ge(q_turned.sem, q_turned.at(t))
                    turn(qtok[t % 2][:, :, NOPE:NOPE + HF], qtok[t % 2][:, :, NOPE + HF:], cs8[t], sn8[t], rt8, q_turned)

                def put_q(t):
                    for n in range(2):
                        b = take(("qt", t, n))
                        V.tensor_copy(qT[0:QK, 4 * n:4 * n + 4, t * P:(t + 1) * P], b[0:QK, :].rearrange("p (h i) -> p h i", h=4)).then_inc(*emptying(("qt", t, n)))
                turn_q(0)
                turn_q(1)
                put_q(0)
                turn_q(2)
                put_q(1)
                turn_q(3)
                put_q(2)
                put_q(3)

                def softmax_max(u):
                    t = u // H
                    b = take(("s", u))
                    n = (t + 1) * P
                    link(V.tensor_tensor(b[:, t * P:n], b[:, t * P:n], C("future"), ALU.add))
                    link(V.reduce_max(smx[:, 0, u:u + 1], b[:, 0:n], AX.X))
                    V.tensor_scalar(smx[:, 1, u:u + 1], smx[:, 0, u:u + 1], -QK ** -0.5, None, ALU.mult).then_inc(*mx_ready.up())

                def put_pt(u):
                    b = take(("pt", u))
                    if u >= 2 and (u - 2) % H != H - 1:
                        pass
                    n = (u // H + 1) * P
                    V.tensor_copy(PT[u % 2][:, 0:n], b[:, 0:n]).then_inc(*emptying(("pt", u)))

                def head_norm(t):
                    dve.wait_ge(o_full.sem, o_full.at(t + 1))
                    o = mix[t % 2]
                    o3 = o[:, :].rearrange("p (h e) -> p h e", h=H)
                    if t >= 2:
                        dve.wait_ge(*full(("mx", t - 2)))
                    r = mnorm[:, 0, :]
                    q = mnorm[:, 2 + t % 2, :]
                    link(V.reciprocal(r, ssum[:, t * H:(t + 1) * H]))
                    link(V.tensor_tensor(o3, PB[:, 6 + t % 2, :].rearrange("p (h e) -> p h e", h=H), r.unsqueeze(2).to_broadcast((P, H, VD)), ALU.mult))
                    V.sem_inc(o_read.up()[0], 1)
                    link(V.tensor_tensor(hsq[:, :], o[:, :], o[:, :], ALU.mult))
                    V.reduce_sum(q, hsq[:, :].rearrange("p (h e) -> p h e", h=H), AX.X).then_inc(*o_sq.up())
                    dve.wait_ge(o_rs.sem, o_rs.at(t + 1))
                    V.tensor_tensor(o3, o3, q.unsqueeze(2).to_broadcast((P, H, VD)), ALU.mult).then_inc(*mix_ready.up())
                for u in range(TT * H + 4):
                    if u < TT * H:
                        softmax_max(u)
                    if 2 <= u < TT * H + 2:
                        put_pt(u - 2)
                    if u >= H + 3 and (u - H - 3) % H == 0:
                        head_norm((u - H - 3) // H)

                def norm(t, k, gain_waits):
                    x = X[:, t, :]
                    link(V.bn_stats(stats[:, 0, :], x[:, 0:512]))
                    link(V.bn_stats(stats[:, 1, :], x[:, 512:D]))
                    link(V.bn_aggr(mvar[:, :], stats[:, :, :].rearrange("p a s -> p (a s)")))
                    V.tensor_copy(rstd[:, t % 2:t % 2 + 1], mvar[:, 1:2]).then_inc(*ln_var.up())
                    dve.wait_ge(ln_rs.sem, ln_rs.at(k + t + 1))
                    link(V.tensor_scalar(x, x, mvar[:, 0:1], rstd[:, t % 2:t % 2 + 1], ALU.subtract, ALU.mult))
                    dve.wait_ge(ln_in, gain_waits)
                    V.tensor_tensor(x, x, lnG, ALU.mult).then_inc(*ln_scaled.up())
                for t in range(TT):
                    for h in range(2):
                        b = take(("out", t, h))
                        V.scalar_tensor_tensor(X[:, t, 512 * h:512 * (h + 1)], X[:, t, 512 * h:512 * (h + 1)], ALPHA, b, ALU.mult, ALU.add) \
                            .then_inc(*emptying(("out", t, h)))
                    dve.wait_ge(*empty(JOB[("out", t, 1)]))
                    norm(t, 0, 32)
                xt("xt2")

                b = take("logit")
                V.tensor_copy(lg[:, :, :], b[:, 0:TT * 72].rearrange("p (t n) -> p t n", t=TT)).then_inc(*emptying("logit"))
                dve.wait_ge(*empty(JOB["logit"]))
                d8 = C("down8").unsqueeze(1).to_broadcast((P, TT, 8))

                def b8(v):
                    return v.unsqueeze(2).to_broadcast((P, TT, 8))

                def first_max(scores, mx, shifted, tmp, best, onehot):
                    link(V.reduce_max(mx, scores, AX.X))
                    link(V.tensor_tensor(shifted, scores, b8(mx), ALU.subtract))
                    link(V.scalar_tensor_tensor(tmp, shifted, 0.0, d8, ALU.is_ge, ALU.mult))
                    link(V.reduce_max(best, tmp, AX.X))
                    link(V.tensor_tensor(onehot, d8, b8(best), ALU.is_equal))
                first_max(lg[:, :, 0:8], r1[:, 0], r8[:, 1], r8[:, 3], r1[:, 1], r8[:, 0])
                V.sem_inc(exp_in.up()[0], 1)
                dve.wait_ge(exp_out.sem, exp_out.at(1))
                link(V.reduce_sum(r1[:, 2], r8[:, 2], AX.X))
                link(V.reciprocal(r1[:, 3], r1[:, 2]))
                goh = r8[:, 0]
                prod = rt[:, 0:256].rearrange("p (t g e) -> p t g e", t=TT, g=8)
                for t in range(TT):
                    last = V.tensor_tensor(prod[:, t], lg[:, t, 8:].rearrange("p (g e) -> p g e", g=8), goh[:, t, :].unsqueeze(2).to_broadcast((P, 8, 8)), ALU.mult)
                    link(last)
                link(V.reduce_sum(r8[:, 4], prod.rearrange("p t g e -> p t e g"), AX.X))
                first_max(r8[:, 4], r1[:, 4], r8[:, 5], r8[:, 3], r1[:, 1], r8[:, 6])
                link(V.scalar_tensor_tensor(r8[:, 5], r8[:, 6], -BIG, r8[:, 5], ALU.mult, ALU.add))
                first_max(r8[:, 5], r1[:, 6], r8[:, 4], r8[:, 3], r1[:, 1], r8[:, 7])
                V.sem_inc(exp_in.up()[0], 1)
                dve.wait_ge(exp_out.sem, exp_out.at(2))
                link(V.tensor_scalar(r1[:, 8], r1[:, 7], 1.0, None, ALU.add))
                link(V.reciprocal(r1[:, 9], r1[:, 8]))
                link(V.tensor_tensor(wts[:, 0], r1[:, 9], r1[:, 3], ALU.mult))
                link(V.tensor_tensor(wts[:, 1], wts[:, 0], r1[:, 7], ALU.mult))
                for k in range(2):
                    for t in range(TT):
                        link(V.tensor_tensor(OH[k][:, t, :].rearrange("p (g e) -> p g e", g=8), goh[:, t, :].unsqueeze(2).to_broadcast((P, 8, 8)),
                                             r8[:, 6 + k, t, :].unsqueeze(1).to_broadcast((P, 8, 8)), ALU.mult))
                V.tensor_tensor(OHS[:, :, :], OH[0][:, :, :], OH[1][:, :, :], ALU.add).then_inc(*oh_ready.up())
                b = take("rank")
                link(V.tensor_copy(posb[:, :, :], b[:, 0:TT * NE].rearrange("p (t n) -> p t n", t=TT)))
                V.tensor_copy(cnt[:, 0, :], b[:, TT * NE:(TT + 1) * NE]).then_inc(*emptying("rank"))
                dve.wait_ge(*empty(JOB["rank"]))
                cmp = rt[:, 0:NE * 15].rearrange("p (e j) -> p e j", j=15)
                link(V.tensor_tensor(cmp, cnt[:, 0, :].unsqueeze(2).to_broadcast((P, NE, 15)), C("caps").unsqueeze(1).to_broadcast((P, NE, 15)), ALU.is_gt))
                link(V.reduce_sum(cnt[:, 1, :], cmp, AX.X))
                link(V.tensor_tensor_scan(cnt[:, 2, :], cnt[:, 1, :], C("zero"), 0.0, ALU.add, ALU.add))
                link(V.tensor_tensor(cnt[:, 3, :], cnt[:, 2, :], cnt[:, 1, :], ALU.subtract))
                link(V.tensor_scalar(cnt[:, 3, :], cnt[:, 3, :], float(CAP), float(NE * CAP - CAP), ALU.mult, ALU.add))
                link(V.tensor_tensor(cnt[:, 4, :], cnt[:, 3, :], C("slot0"), ALU.subtract))
                sel = rt[:, 0:256].rearrange("p (t n) -> p t n", t=TT)

                def pick(o, k, table):
                    link(V.tensor_tensor(sel, OH[k][:, :, :], table, ALU.mult))
                    link(V.reduce_sum(o, sel, AX.X))

                def b64(v):
                    return v.unsqueeze(1).to_broadcast((P, TT, NE))
                for k in range(2):
                    pick(r1[:, 10], k, posb[:, :, :])
                    pick(r1[:, 11], k, b64(C("slot0")))
                    pick(r1[:, 12], k, b64(cnt[:, 4, :]))
                    link(V.scalar_tensor_tensor(r1[:, 13], r1[:, 10], float(CAP), r1[:, 12], ALU.is_ge, ALU.mult))
                    link(V.tensor_tensor(r1[:, 10], r1[:, 10], r1[:, 11], ALU.add))
                    link(V.tensor_tensor(r1[:, 10], r1[:, 10], r1[:, 13], ALU.add))
                    link(V.tensor_copy(sloti[:, k, :], r1[:, 10]))
                sl = sloti[:, :, :].rearrange("p k t -> p (k t)")
                link(V.tensor_scalar(slt[:, 0, :], sl, P - 1, None, ALU.bitwise_and))
                link(V.tensor_scalar(slt[:, 1, :], sl, 7, None, ALU.arith_shift_right))
                link(V.tensor_scalar(slt[:, 0, :], slt[:, 0, :], float(G_ALL), None, ALU.mult))
                V.tensor_tensor(slt[:, 2, :], slt[:, 0, :], slt[:, 1, :], ALU.add).then_inc(*slots_ready.up())
                be = rt2[0:1, 0:32 * NE].rearrange("p (b e) -> p b e", b=32)
                dve.wait_ge(slots_ready.sem, slots_ready.at(1))
                link(V.tensor_tensor(be, cnt[0:1, 2, :].unsqueeze(1).to_broadcast((1, 32, NE)), C("block")[0:1].unsqueeze(2).to_broadcast((1, 32, NE)), ALU.is_le))
                link(V.tensor_tensor(meta_f[:, 33:34], meta_f[:, 33:34], meta_f[:, 32:33], ALU.add))
                link(V.reduce_sum(meta_f[:, 0:32], be, AX.X))
                link(V.tensor_scalar(meta_f[:, 0:32], meta_f[:, 0:32], float(NE - 1), None, ALU.min))
                link(V.tensor_scalar(rt2[0:1, 0:SG], C("fours")[0:1], cnt[0:1, 2, NE - 1:NE], None, ALU.is_lt))
                link(V.reduce_sum(meta_f[:, 32:33], rt2[0:1, 0:SG], AX.X))
                V.tensor_copy(meta[:, :], meta_f[:, :]).then_inc(*meta_ready.up())
                with dve.Fori(0, IT) as i:
                    for b in range(2):
                        group(main, b, i, i * 2 + b)
                n = spill_groups(dve)
                with dve.If(n > 0):
                    stored_all(dve)
                    with dve.Fori(0, n) as g:
                        group(spill, 0, g, g)
                with dve.Else():
                    pass
                for t in range(TT):
                    link(V.tensor_scalar(X[:, t, :], X[:, t, :], ALPHA, None, ALU.mult))
                    turn_wait(dve, y_in[t % 2], l * 64 + 32 * (t // 2 + 1))
                    ya, yb = (xg[0], xg[1]) if t % 2 == 0 else (xgT[0], xgT[1])
                    link(V.scalar_tensor_tensor(X[:, t, :], ya, wts[:, 0, t:t + 1], X[:, t, :], ALU.mult, ALU.add))
                    link(V.scalar_tensor_tensor(X[:, t, :], yb, wts[:, 1, t:t + 1], X[:, t, :], ALU.mult, ALU.add))
                    V.sem_inc(y_used.up()[0], 1)
                    norm(t, TT, 64)
                end_layer(dve, l)

        @block.gpsimd
        def _(pool):
            pool.wait_ge(small_set, 6)
            pool.dma_start(tab_dram.rearrange("(p g) o -> p (g o)", g=G_ALL), zero_i[:, :]).then_inc(tab_zeroed, 16)
            pool.wait_ge(tab_zeroed, 16)
            nc.gpsimd.memset(R1[:, 3 * D:4 * D], 0.0).then_inc(small_set, 1)
            pool.wait_ge(small_set, 7)
            for g in range(EG, G_ALL):
                pool.dma_start(y_dram[g * P:(g + 1) * P, :], R1[:, 3 * D:4 * D]).then_inc(y_zeroed, 16)

            def group(path, b, it, g):
                turn_wait(pool, path.xg_T[b], it + 1)
                nc.gpsimd.tensor_copy(idx[b][:, :], idx_all[:, bass.ds(g, 1)]).then_inc(path.idx[b], 1)
                turn_wait(pool, path.idx[b], it + 1)
                pool.indirect_dma_start(xg[b], None, x_dram, bass.IndirectOffsetOnAxis(ap=idx[b][:, :], axis=0)).then_inc(path.xg_in[b], 16)

            with pool.Fori(0, L) as l:
                nc.gpsimd.memset(v1[:, :, :, DH:].rearrange("p t h o -> p (t h) o"), 1.0).then_inc(*v1_ones.up())
                for h in range(MH):
                    for s in range(TT):
                        pool.wait_ge(ptm_written.sem, ptm_written.at(h * TT + s + 1))
                        a = PTm[h % 2][:, pt_at[s]:pt_at[s] + P]
                        nc.gpsimd.affine_select(out=a, in_=a, compare_op=ALU.is_ge, fill=0.0, base=0, pattern=[[1, P]],
                                                channel_multiplier=-1).then_inc(*ptm_ready.up())
                pool.wait_ge(h_ready.sem, h_ready.at(MH))
                pool.wait_ge(*empty(JOB["kr"]))
                nc.gpsimd.tensor_copy(kT[NOPE:QK, :, :], krT[NOPE:QK, :].unsqueeze(1).to_broadcast((ROPE, H, S))).then_inc(*kr_copied.up())
                for t in range(TT):
                    pool.wait_ge(ln_scaled.sem, ln_scaled.at(t + 1))
                    nc.gpsimd.tensor_tensor(X[:, t, :], X[:, t, :], lnB, ALU.add).then_inc(*x_ready.up())
                pool.wait_ge(slots_ready.sem, slots_ready.at(1))
                for k in range(2):
                    for t in range(TT):
                        c = k * TT + t
                        pool.indirect_dma_start(tab_dram, bass.IndirectOffsetOnAxis(ap=slt[:, 2, c:c + 1], axis=0), toki[:, t:t + 1], None) \
                            .then_inc(scattered, 16)
                turn_wait(pool, scattered, l * 128 + 128)
                pool.dma_start(idx_all[:, :], tab_dram.rearrange("(p g) o -> p (g o)", g=G_ALL)).then_inc(idx_in, 16)
                turn_wait(pool, idx_in, l * 16 + 16)
                pool.wait_ge(x_stored, 64)
                with pool.Fori(0, IT) as i:
                    for b in range(2):
                        group(main, b, i, i * 2 + b)
                n = spill_groups(pool)
                with pool.If(n > 0):
                    stored_all(pool)
                    with pool.Fori(0, n) as g:
                        group(spill, 0, g, g + EG)
                with pool.Else():
                    pass
                stored_all(pool, n)
                for t in range(TT):
                    if t >= 2:
                        pool.wait_ge(y_used.sem, y_used.at(t - 1))
                    for k in range(2):
                        to = (xg if t % 2 == 0 else xgT)[k]
                        pool.indirect_dma_start(to, None, y_dram, bass.IndirectOffsetOnAxis(ap=sloti[:, k, t:t + 1], axis=0)).then_inc(y_in[t % 2], 16)
                    if t >= 1:
                        pool.wait_ge(ln_scaled.sem, ln_scaled.at(TT + t))
                        nc.gpsimd.tensor_tensor(X[:, t - 1, :], X[:, t - 1, :], lnB, ALU.add).then_inc(*x_ready.up())
                pool.wait_ge(ln_scaled.sem, ln_scaled.at(2 * TT))
                nc.gpsimd.tensor_tensor(X[:, TT - 1, :], X[:, TT - 1, :], lnB, ALU.add).then_inc(*x_ready.up())
                end_layer(pool, l)

        steps_counted = dstep.n, astep.n
        assert steps_counted == (DVE_STEPS, ACT_STEPS), steps_counted
        for e in "AD":
            assert emptied[e].n == n_of[e]
        assert bank_full.n == len(JOBS)


_INS = ["x", "positions", "w_in", "conv_w", "conv_b", "gate_b", "q_a_g", "kv_a_g", "w_qb", "w_kvb", "out_g", "w_out",
        "ln1_g", "ln1_b", "w_rg", "w_re", "w_gate", "w_up", "w_down", "ln2_g", "ln2_b"]


def kernel(**inputs):
    import numpy as _np
    import concourse.bacc as _bacc
    from concourse import mybir as _mybir
    from concourse.bass_utils import run_bass_kernel_spmd as _run

    nc = _bacc.Bacc("TRN2", target_bir_lowering=False, num_devices=1)
    arrays, args = {}, {}
    for name in _INS:
        a = _np.ascontiguousarray(inputs[name])
        arrays[f"in_{name}"] = a
        args[name] = nc.dram_tensor(f"in_{name}", a.shape, _mybir.dt.from_np(a.dtype), kind="ExternalInput").ap()
    arrays["in_constants"] = CONST
    const = nc.dram_tensor("in_constants", CONST.shape, _mybir.dt.float32, kind="ExternalInput").ap()
    out = nc.dram_tensor("out_0", (1, S, D), _mybir.dt.float32, kind="ExternalOutput").ap()
    hybrid_kernel(nc, args, const, out)
    r = _run(nc, [arrays], core_ids=[0])
    return r.results[0]["out_0"]
```

```python
import numpy as np
import concourse.bass as bass
from concourse import mybir
from contextlib import ExitStack

D, S, L = 1024, 512, 2
H, NOPE, ROPE, VD = 8, 64, 32, 64
QK = NOPE + ROPE
QR, KVR = 256, 128
MH, DH = 4, 128
DM = MH * DH
CW = 4
NG, EPG, NE, DE = 8, 8, 64, 256
P = 128
TT = S // P
KC = D // P
ALPHA = (2 * L) ** 0.25
LN_EPS, RMS_EPS = 1e-5, 1e-6
DIN = QR + KVR + ROPE + 4 * DM + 2 * MH
C_CQ, C_Q = 0, QR + KVR + ROPE
C_K, C_V, C_O = C_Q + DM, C_Q + 2 * DM, C_Q + 3 * DM
NA = C_Q
NC2 = (DM + 2 * MH) // 2
CAP = 32
GRP = P // CAP
EG = NE // GRP
SG = 8
G_ALL = EG + SG
SLOT_BYTES = 6144
BIG = 1e30

def constants():
    cols, at = [], {}

    def put(name, a):
        at[name] = (sum(c.shape[1] for c in cols), a.shape[1])
        cols.append(np.broadcast_to(a, (P, a.shape[1])).astype(np.float32))

    i = np.arange(P)
    put("ident", np.eye(P))
    put("upto", (i[:, None] <= i[None, :]) * 1.0)
    put("before", (i[:, None] < i[None, :]) * 1.0)
    put("ones", np.ones((1, P)))
    put("future", np.concatenate([np.zeros((P, S - P)), np.where(i[None, :] > i[:, None], -BIG, 0.0)], 1))
    put("lane", i[None, :] * 1.0)
    put("pick", (i[:, None] == np.arange(MH * P)[None, :] // P) * 1.0)
    put("down8", 8.0 - np.arange(8)[None, :])
    half = ROPE // 2
    put("freq", (np.float32(10000.0) ** (-np.arange(half, dtype=np.float32) / np.float32(half)))[None, :])
    put("slot0", CAP * np.arange(NE)[None, :] * 1.0)
    put("fours", 4 * np.arange(SG)[None, :] * 1.0)
    put("row", i[:, None] * 1.0)
    put("zero", np.zeros((1, NE)))
    return np.ascontiguousarray(np.concatenate(cols, 1)), at


CONST, CAT = constants()

DVE_STEPS, ACT_STEPS = 181, 53

def jobs():
    out = [("vec", "D")]
    out += [(("xt", t, h), "AD"[h]) for t in range(TT) for h in range(2)]
    out += [(("a", t), "D") for t in range(TT)]
    out += [(("o", t, h), "A") for t in range(TT) for h in range(2)]
    out += [(("q", 0), "D"), ("cum", "D"), (("q", 1), "D"), ("at", "D")]
    out += [(("cq", 0), "A"), (("cq", 1), "A"), ("ckv", "A"), ("kr", "A")]
    out += [(("q", 2), "D"), ("acol", "D"), (("q", 3), "D")]
    out += [(("k", c), "D") for c in range(MH)] + [(("v", t), "A") for t in range(TT)]

    def g(h):
        return [(("abc", h), "A")] + [(("st", h, b), "D") for b in range(TT)]

    def n(h):
        return [(("num", h, b), "D") for b in range(2)]

    def m(h):
        return [(("mt", h), "A")]
    for part in (g(0), g(1), n(0), g(2), m(0), n(1), g(3), m(1), n(2), m(2), n(3), m(3)):
        out += part
    out += [(("kn", h), "AD"[h % 2]) for h in range(H)] + [(("mv", t), "A") for t in range(TT)]

    def q(t):
        return [(("qa", t), "A"), (("qb", t), "A")]

    def qt(t):
        return [(("qt", t, 0), "D"), (("qt", t, 1), "D")]
    for part in (q(0), q(1), qt(0), q(2), qt(1), q(3), qt(2), qt(3)):
        out += part
    for u in range(TT * H + 6):
        if u < TT * H:
            out.append((("s", u), "A"))
        if 3 <= u < TT * H + 3:
            out.append((("pt", u - 3), "D"))
        if u >= 15 and (u - 15) % H == 0:
            out.append((("mx", (u - 15) // H), "A"))
    out += [(("mx", TT - 1), "A")]
    for t in range(TT):
        out += [(("out", t, h), "D") for h in range(2)]
        if t:
            out += [(("xt2", t - 1, h), "AD"[h]) for h in range(2)]
    out += [(("xt2", TT - 1, h), "AD"[h]) for h in range(2)]
    out += [("logit", "D"), ("rank", "D")]
    return out


JOBS = jobs()
JOB = {name: j for j, (name, _) in enumerate(JOBS)}
NB = 6


class Signal:

    def __init__(self, sem, per_layer):
        self.sem, self.per, self.n = sem, per_layer, 0

    def up(self):
        self.n += 1
        return self.sem, 1

    def at(self, k):
        assert 0 < k <= self.per, (k, self.per)
        return k


def hybrid_kernel(nc, A, const, out):
    f32, i32 = mybir.dt.float32, mybir.dt.int32
    ALU, ACT, AX = mybir.AluOpType, mybir.ActivationFunctionType, mybir.AxisListType

    y_dram = nc.dram_tensor("y_slots", (G_ALL * P, D), f32, kind="Internal").ap()

    ctx = ExitStack()
    with ctx:
        def sb(name, shape, dt=f32):
            return ctx.enter_context(nc.sbuf_tensor(name, shape, dt))

        ring = [sb(f"ring{i}", [P, SLOT_BYTES]) for i in range(4)]
        X = sb("X", [P, TT, D])
        XT = sb("XT", [P, KC, S])
        R1 = sb("R1", [P, 8 * S])
        R2 = sb("R2", [P, 4224])
        R4 = sb("R4", [P, 4224])
        cqT = sb("cqT", [P, 2, S])
        ckvT = sb("ckvT", [P, S])
        krT = sb("krT", [P, S])
        qtok = [R4[:, 2048 + H * QK * i:2048 + H * QK * (i + 1)].rearrange("p (h d) -> p h d", h=H) for i in range(2)]
        K = sb("K", [P, CONST.shape[1]])
        vecs = R4[0:7, 3200:3200 + D]
        vecT = sb("vecT", [P, KC, 7])
        gate_b = sb("gate_b", [P, 2 * MH])
        wr = sb("wr", [P, KC, NG + NE])
        cos = sb("cos", [P, TT, ROPE // 2])
        sin = sb("sin", [P, TT, ROPE // 2])
        ang = R4[:, 0:192].rearrange("p (a n) -> p a n", a=3)
        turns = sb("turns", [P, TT * ROPE // 2], i32)
        pos_i = sb("pos_i", [P, TT], i32)
        pos_f = sb("pos_f", [P, TT])
        biases = sb("biases", [P, 4])

        def C(name, n=None):
            a, w = CAT[name]
            return K[:, a:a + (n or w)]

        ident = C("ident")
        qkT = R1[:, :].rearrange("p (c t) -> p c t", c=8)
        V1W = TT * MH * (DH + 1)
        v1 = R2[:, 0:V1W].rearrange("p (t h e) -> p t h e", t=TT, h=MH)
        osig = R2[:, V1W:V1W + TT * DM].rearrange("p (t n) -> p t n", t=TT)
        cqkv = R4[:, 0:TT * NA].rearrange("p (t n) -> p t n", t=TT)
        convt = [R4[:, TT * NA + S * i:TT * NA + S * (i + 1)] for i in range(3)]
        PTW = P * (4 + 3 + 2 + 1)
        pt_at = [0, 512, 896, 1152]
        PTm = [R4[:, PTW * i:PTW * (i + 1)] for i in range(2)]
        Wm = [R4[:, 2 * PTW + S * i:2 * PTW + S * (i + 1)] for i in range(2)]
        gates = sb("gates", [P, TT, 2 * MH])
        gt = sb("gt", [P, 3, TT, MH])
        logf = sb("logf", [P, TT, MH])
        Bc = sb("Bc", [P, TT, MH])
        ac = sb("ac", [P, TT, MH])
        em = sb("em", [P, TT, MH])
        Arow = R4[0:MH, 3584:3584 + S]
        hm = [sb(f"hm{i}", [P, TT, DH]) for i in range(2)]
        hsq = sb("hsq", [P, 512])
        arow = hsq[0:MH, :]
        den = sb("den", [P, 4, TT])
        ss = sb("ss", [P, 2, TT])
        qT = R1[:, :].rearrange("p (h t) -> p h t", h=H)
        kT = R2[:, 0:H * S].rearrange("p (h t) -> p h t", h=H)
        mv = R4[:, 0:TT * H * VD].rearrange("p (t n) -> p t n", t=TT)
        Pm = [R4[:, 2048 + S * i:2048 + S * (i + 1)] for i in range(3)]
        PT = [R4[:, 3584:3584 + S], krT[:, :], ckvT[:, :]]
        smx = sb("smx", [P, TT * H])
        ssum = sb("ssum", [P, TT * H])
        mnorm = sb("mnorm", [P, 4, H])
        mix = [h[:, :, :].rearrange("p t e -> p (t e)") for h in hm]
        rtmp = sb("rtmp", [P, 4, H * ROPE // 2])
        lnG, lnB = R1[:, 0:D], R1[:, D:2 * D]
        oh = [R1[:, 2 * D + S * i:2 * D + S * (i + 1)].rearrange("p (t n) -> p t n", t=TT) for i in range(2)]
        oh_b = R1[:, 3 * D:3 * D + S].rearrange("p (t n) -> p t n", t=TT)
        xgT = [R2[:, 0:D], R2[:, D:2 * D]]
        ysb = [R2[:, 2 * D:3 * D], R2[:, 3 * D:4 * D]]
        XTw = XT[:, :, :].rearrange("p k t -> p (k t)")
        y_rows = [[XTw[:, 2 * D * i + D * k:2 * D * i + D * (k + 1)] for k in range(2)] for i in range(2)] \
            + [[R1[:, 2 * D:3 * D], R1[:, 3 * D:4 * D]], xgT]
        stats = sb("stats", [P, 2, 6])
        mvar = [sb(f"mvar{i}", [P, 2]) for i in range(2)]
        nmean = sb("nmean", [P, 2, 2])
        rstd = sb("rstd", [P, 2])
        at = [0]

        def r4(*shape):
            n = int(np.prod(shape))
            v = R4[:, at[0]:at[0] + n]
            at[0] += n
            return v if len(shape) == 1 else v.rearrange("p (a b) -> p a b", a=shape[0]) if len(shape) == 2 else \
                v.rearrange("p (a b c) -> p a b c", a=shape[0], b=shape[1])
        lg = r4(TT, NG + NE)
        r8 = r4(8, TT, 8)
        r1 = r4(16, TT)
        OH2 = r4(2, TT, NE)
        OHS = r4(TT, NE)
        pos0 = r4(TT, NE)
        cnt = r4(5, NE)
        sv = r4(TT, NE)
        slf = r4(2, TT)
        esb, hsb, hT = ([r4(64) for _ in range(2)] for _ in range(3))
        rt = ysb[0]
        sloti = sb("sloti", [P, 2, TT], i32)
        blocks_i = sb("blocks_i", [P, NE], i32)
        block_col = sb("block_col", [32, 32])
        block_row = sb("block_row", [32, 32])
        groups_f = sb("groups_f", [1, 1])
        meta = sb("meta", [1, 33], i32)
        wts = sb("wts", [P, 2, TT])

        PB = ctx.enter_context(nc.psum_tensor("PB", [P, 8, 512], f32))

        cleared = []

        def kept(name):
            return ctx.enter_context(nc.semaphore(name))

        def sem(name):
            cleared.append(kept(name))
            return cleared[-1]

        def sig(name, per):
            return Signal(sem(name), per)

        once = {n: kept(n) for n in (
            "consts_in", "x_in", "pos_in", "rope_step", "rope_ready", "small_set", "y_zeroed", "vecs_in", "gate_b_in",
            "wr_in", "y_in0", "y_in1", "y_in2", "y_in3", "w_a", "w_qkvb", "w_v", "w_o", "out_stored", "arrived", "layer_open", "waited")}
        n_of = {e: sum(1 for _, x in JOBS if x == e) for e in "AD"}
        bank_full = sig("bank_full", len(JOBS))
        emptied = {"A": sig("emptied_by_act", n_of["A"]), "D": sig("emptied_by_dve", n_of["D"])}

        def bank(name):
            return PB[:, 6 if name == "logit" else JOB[name] % NB, :]

        def full(name):
            return bank_full.sem, bank_full.at(JOB[name] + 1)

        def empty(j):
            e = JOBS[j][1]
            return emptied[e].sem, emptied[e].at(sum(1 for _, x in JOBS[:j + 1] if x == e))

        def emptying(name):
            e = JOBS[JOB[name]][1]
            mine = [n for n, x in JOBS if x == e]
            assert mine[emptied[e].n] == name, (name, mine[emptied[e].n])
            return emptied[e].up()

        consts_in, x_in, pos_in = once["consts_in"], once["x_in"], once["pos_in"]
        rope_step, rope_ready = once["rope_step"], once["rope_ready"]
        small_set, y_zeroed = once["small_set"], once["y_zeroed"]
        vecs_in, gate_b_in, wr_in, ln_in = once["vecs_in"], once["gate_b_in"], once["wr_in"], sem("ln_in")
        w_a, w_q, w_v, w_o = (once[f"w_{n}"] for n in ("a", "qkvb", "v", "o"))
        w_qm, w_k, w_out = (sem(f"w_{n}") for n in ("q", "k", "out"))
        dstep = sig("dve_step", DVE_STEPS)
        astep = sig("act_step", ACT_STEPS)
        cq_sq = sig("cq_squares", 1)
        cq_ready = sig("cq_ready", 2)
        gates_in = sig("gates_in", 1)
        gate_neg = sig("gate_neg", 1)
        gate_ln = sig("gate_ln", 1)
        logf_ready = sig("logf_ready", 1)
        ac_ready = sig("ac_ready", 1)
        arow_ready = sig("arow_ready", 1)
        m_ready = sig("m_ready", 1)
        em_ready = sig("em_ready", 1)
        conv_ready = sig("conv_ready", 8)
        silu_exp = sig("silu_exp", 8)
        qk_ready = sig("qk_ready", 8)
        v1_ones = sig("v1_ones", 1)
        w_ready = sig("w_ready", MH * TT)
        ptm_written = sig("ptm_written", MH * TT)
        ptm_ready = sig("ptm_ready", MH * TT)
        h_sq = sig("h_sumsq", MH)
        h_rs = sig("h_rstd", MH)
        h_ready = sig("h_ready", MH)
        kr_copied = sig("kr_copied", 1)
        q_turned = sig("q_turned", TT)
        mx_ready = sig("mx_ready", TT * H)
        p_ready = sig("p_ready", TT * H)
        o_full = sig("o_full", TT)
        o_read = sig("o_read", TT)
        o_sq = sig("o_sumsq", TT)
        o_rs = sig("o_rstd", TT)
        mix_ready = sig("mix_ready", TT)
        ln_var = sig("ln_var", 2 * TT)
        ln_rs = sig("ln_rstd", 2 * TT)
        ln_scaled = sig("ln_scaled", TT - 1)
        x_ready = sig("x_ready", TT)
        exp_in, exp_out = sig("exp_in", 2), sig("exp_out", 2)
        oh_ready = sig("oh_ready", 1)
        conv_first = sig("conv_first", 8)
        ln_norm = sig("ln_normalised", 2 * TT)
        meta_ready = sig("meta_ready", 1)
        y_in = [once[f"y_in{t}"] for t in range(TT)]
        y_scaled = sig("y_scaled", TT)
        out_stored, arrived, layer_open, waited = (once[n] for n in ("out_stored", "arrived", "layer_open", "waited"))

        class Path:

            def __init__(self, name, bufs):
                self.w_in = [sem(f"{name}_w_in{q}") for q in range(GRP)]
                self.down = [sem(f"{name}_down{q}") for q in range(GRP)]
                self.oh = [sem(f"{name}_oh{b}") for b in range(bufs)]
                self.oh_step = sem(f"{name}_oh_step")
                self.xg_T = [sem(f"{name}_xg_T{b}") for b in range(bufs)]
                self.xgT_a = [sem(f"{name}_xgT_a{b}") for b in range(bufs)]
                self.xgT_d = [sem(f"{name}_xgT_d{b}") for b in range(bufs)]
                self.gu = [sem(f"{name}_gu{i}") for i in range(2)]
                self.ex = [sem(f"{name}_ex{i}") for i in range(2)]
                self.st = [sem(f"{name}_st{i}") for i in range(2)]
                self.hT = [sem(f"{name}_hT{i}") for i in range(2)]
                self.y = [sem(f"{name}_y{i}") for i in range(2)]
                self.ysb = sem(f"{name}_ysb")
                self.stored = [sem(f"{name}_stored{b}") for b in range(bufs)]
                self.bufs = bufs
                self.ahead = [(s, 1) for s in self.down + self.xg_T + self.xgT_a + self.xgT_d + self.st + self.y] \
                    + [(s, 64) for s in self.stored] + [(self.oh_step, 3)]

        main, spill = Path("main", 2), Path("spill", 1)
        moe_step = {False: sem("moe_step"), True: sem("spill_step")}
        IT = EG // 2

        def turn_wait(eng, semaphore, value):
            eng.wait_ge(semaphore, value)
            eng.sem_inc(waited, 1)

        def stored_all(eng, spilled=None):
            for b in range(2):
                eng.wait_ge(main.stored[b], IT * 64 + 64)
            if spilled is not None:
                turn_wait(eng, spill.stored[0], spilled * 64 + 64)

        def spill_groups(eng):
            eng.wait_ge(meta_ready.sem, meta_ready.at(1))
            return eng.value_load(meta[0:1, 32:33], min_val=0, max_val=SG)

        def end_layer(eng, l):
            eng.drain().then_inc(arrived, 1)
            turn_wait(eng, layer_open, l + 1)

        block = ctx.enter_context(nc.Block())

        @block.sync
        def _(sp):
            sp.dma_start(K[:, :], const).then_inc(consts_in, 16)
            for t in range(TT):
                sp.dma_start(X[:, t, :], A["x"][0, t * P:(t + 1) * P, :]).then_inc(x_in, 16)
            with nc.allow_non_contiguous_dma("512 positions"):
                sp.dma_start(pos_i[:, :], A["positions"][0].rearrange("(t p) -> p t", p=P)).then_inc(pos_in, 16)

            def expert(path, q, l, e):
                r = ring[q]
                sp.dma_start(r[:, 0:2048], A["w_gate"][l, e].rearrange("(p k) f -> p (k f)", k=KC)).then_inc(path.w_in[q], 16)
                sp.dma_start(r[:, 2048:4096], A["w_up"][l, e].rearrange("(p k) f -> p (k f)", k=KC)).then_inc(path.w_in[q], 16)
                sp.dma_start(r[:, 4096:6144].rearrange("p (c n) -> p c n", c=2),
                             A["w_down"][l, e].rearrange("(c p) n -> p c n", p=P)).then_inc(path.w_in[q], 16)

            def cols(l, slot, a, b, s):
                w_in = A["w_in"][l].rearrange("(p k) n -> p k n", k=KC)
                sp.dma_start(ring[slot][:, 0:KC * (b - a)].rearrange("p (k n) -> p k n", k=KC), w_in[:, :, a:b]).then_inc(s, 16)

            def row(t, l):
                return t[l:l + 1] if isinstance(l, int) else t[bass.ds(l, 1)]

            def first_weights(l):
                sp.dma_start(vecs[0:4, :], A["conv_w"][l]).then_inc(vecs_in, 16)
                sp.dma_start(vecs[4:5, :], row(A["conv_b"], l)).then_inc(vecs_in, 16)
                sp.dma_start(vecs[5:6, :], row(A["out_g"], l)).then_inc(vecs_in, 16)
                sp.dma_start(vecs[6:7, 0:QR], row(A["q_a_g"], l)).then_inc(vecs_in, 16)
                sp.dma_start(vecs[6:7, QR:QR + KVR], row(A["kv_a_g"], l)).then_inc(vecs_in, 16)
                cols(l, 2, C_O, DIN, w_o)
                sp.dma_start(gate_b[:, :], row(A["gate_b"], l).to_broadcast((P, 2 * MH))).then_inc(gate_b_in, 16)
                cols(l, 3, C_V, C_O, w_v)
                sp.dma_start(ring[1][:, 0:1536].rearrange("p (c n) -> p c n", c=2),
                             A["w_qb"][l].rearrange("(c p) n -> p c n", p=P)).then_inc(w_q, 16)
                sp.dma_start(ring[1][:, 1536:2560], A["w_kvb"][l]).then_inc(w_q, 16)
                sp.dma_start(wr[:, :, 0:NG], A["w_rg"][l].rearrange("(p k) n -> p k n", k=KC)).then_inc(wr_in, 16)
                sp.dma_start(wr[:, :, NG:], A["w_re"][l].rearrange("(p k) n -> p k n", k=KC)).then_inc(wr_in, 16)

            def set_ahead():
                for path in (main, spill):
                    for s, n in path.ahead:
                        sp.sem_inc(s, n)

            cols(0, 0, 0, NA, w_a)
            first_weights(0)
            set_ahead()
            with sp.Fori(0, L) as l:
                sp.wait_ge(*full(("a", TT - 1)))
                cols(l, 0, C_Q, C_K, w_qm)
                sp.wait_ge(*full(("o", TT - 1, 1)))
                cols(l, 2, C_K, C_V, w_k)
                sp.wait_ge(*full(("v", TT - 1)))
                w_o3 = A["w_out"][l].rearrange("(k p) n -> p k n", p=P)
                sp.dma_start(ring[3][:, 0:4096].rearrange("p (k n) -> p k n", k=KC), w_o3[:, :, 0:512]).then_inc(w_out, 16)
                sp.wait_ge(*full(("k", MH - 1)))
                sp.dma_start(ring[2][:, 0:4096].rearrange("p (k n) -> p k n", k=KC), w_o3[:, :, 512:D]).then_inc(w_out, 16)
                expert(main, 0, l, 0)
                sp.wait_ge(*full(("qb", TT - 1)))
                expert(main, 1, l, 1)
                sp.wait_ge(*full(("s", TT * H - 1)))
                sp.dma_start(lnG, A["ln1_g"][bass.ds(l, 1)].to_broadcast((P, D))).then_inc(ln_in, 16)
                sp.dma_start(lnB, A["ln1_b"][bass.ds(l, 1)].to_broadcast((P, D))).then_inc(ln_in, 16)
                sp.wait_ge(*full(("out", TT - 1, 1)))
                expert(main, 2, l, 2)
                expert(main, 3, l, 3)
                sp.wait_ge(x_ready.sem, x_ready.at(TT))
                sp.dma_start(lnG, A["ln2_g"][bass.ds(l, 1)].to_broadcast((P, D))).then_inc(ln_in, 16)
                sp.dma_start(lnB, A["ln2_b"][bass.ds(l, 1)].to_broadcast((P, D))).then_inc(ln_in, 16)
                with sp.Fori(1, EG) as g:
                    for q in range(GRP):
                        turn_wait(sp, main.down[q], g + 1)
                        expert(main, q, l, g * GRP + q)
                n = spill_groups(sp)
                with sp.If(n > 0):
                    stored_all(sp)
                    with sp.Fori(0, n) as g:
                        for q in range(GRP):
                            turn_wait(sp, spill.down[q], g + 1)
                            e = sp.value_load(meta[0:1, bass.ds(g * GRP + q, 1)], min_val=0, max_val=NE - 1)
                            expert(spill, q, l, e)
                with sp.Else():
                    pass
                for q in range(GRP):
                    sp.wait_ge(main.down[q], EG + 1)
                    turn_wait(sp, spill.down[q], n + 1)
                stored_all(sp, n)
                with sp.If(l < L - 1):
                    cols(L - 1, 0, 0, NA, w_a)
                    for t in range(TT):
                        sp.wait_ge(y_in[t], (L - 1) * 32)
                    first_weights(L - 1)
                with sp.Else():
                    pass
                turn_wait(sp, arrived, 4 * l + 4)
                numbers = sorted(s.num for s in cleared)
                assert numbers == list(range(numbers[0], numbers[-1] + 1))
                sp.sem_clear(range(numbers[0], numbers[-1] + 1))
                set_ahead()
                sp.sem_inc(layer_open, 1)
            for t in range(TT):
                sp.dma_start(out[0, t * P:(t + 1) * P, :], X[:, t, :]).then_inc(out_stored, 16)
            sp.wait_ge(out_stored, 16 * TT)

        @block.tensor
        def _(pe):
            pe.wait_ge(consts_in, 16)
            pe.wait_ge(x_in, 16 * TT)

            def group(path, b, it, m):
                turn_wait(pe, path.oh[b], it + 1)
                if path.bufs == 1:
                    pe.wait_ge(path.xgT_a[0], it + 1)
                    pe.wait_ge(path.xgT_d[0], it + 1)
                else:
                    pe.wait_ge(path.xgT_a[1 - b], it + b + 1)
                    pe.wait_ge(path.xgT_d[1 - b], it + b + 1)
                for k in range(KC):
                    for t in range(TT):
                        last = nc.tensor.matmul(PB[:, k // 4, (k % 4) * P:(k % 4 + 1) * P],
                                                X[:, t, :].rearrange("p (i k) -> p k i", k=KC)[:, k, :], oh[b][:, t, :],
                                                start=t == 0, stop=t == TT - 1)
                last.then_inc(path.xg_T[b], 1)

                def up(q):
                    pe.wait_ge(path.w_in[q], m * 48 + 48)
                    pe.wait_ge(path.st[q % 2], m * 2 + q // 2 + 1)
                    w = ring[q][:, 0:4096].rearrange("p (g k c j f) -> p g k c j f", g=2, k=KC, c=2, j=4)
                    for k in range(KC):
                        for j in range(4):
                            last = nc.tensor.matmul(PB[32 * j:32 * j + 32, 2 + q % 2, 0:P],
                                                    xgT[b][:, k * P + CAP * q:k * P + CAP * (q + 1)],
                                                    w[:, :, k, :, j, :], start=k == 0, stop=k == KC - 1,
                                                    tile_position=(0, 32 * j), skip_group_check=True)
                    last.then_inc(path.gu[q % 2], 1)

                def down(q):
                    pe.wait_ge(path.hT[q % 2], m * 2 + q // 2 + 1)
                    pe.wait_ge(path.y[q % 2], m * 2 + q // 2 + 1)
                    w = ring[q][:, 4096:6144].rearrange("p (c n) -> p c n", c=2)
                    for c in range(2):
                        for j in range(4):
                            last = nc.tensor.matmul(PB[32 * j:32 * j + 32, 4 + q % 2, 0:256],
                                                    hT[q % 2][:, 32 * c:32 * c + 32], w[:, c, 256 * j:256 * (j + 1)],
                                                    start=c == 0, stop=c == 1, tile_position=(0, 32 * j), skip_group_check=True)
                    last.then_inc(path.down[q], 1)
                pe.wait_ge(path.xgT_a[b], it + 2)
                pe.wait_ge(path.xgT_d[b], it + 2)
                for q in range(GRP):
                    up(q)
                    if q:
                        down(q - 1)
                down(GRP - 1)

            with pe.Fori(0, L) as l:
                def room(name):
                    if JOB[name] >= NB:
                        pe.wait_ge(*empty(JOB[name] - NB))
                    return bank(name)

                def done(ins):
                    ins.then_inc(*bank_full.up())

                turn_wait(pe, vecs_in, l * 80 + 80)
                b = room("vec")
                for k in range(KC):
                    r = 7 if k < 3 else 6
                    last = nc.tensor.transpose(b[:, 8 * k:8 * k + r], vecs[0:r, k * P:(k + 1) * P], K[0:r, 0:r])
                done(last)

                def transpose_x(kind, tiles):
                    for t in tiles:
                        for h in range(2):
                            b = room((kind, t, h))
                            xv = X[:, t, :].rearrange("p (i k) -> p k i", k=KC)
                            for k in range(4):
                                last = nc.tensor.transpose(b[:, k * P:(k + 1) * P], xv[:, 4 * h + k, :], ident)
                            done(last)
                transpose_x("xt", range(TT))

                def xt_ready(kind, t):
                    pe.wait_ge(*empty(JOB[(kind, t, 0)]))
                    pe.wait_ge(*empty(JOB[(kind, t, 1)]))
                xt_ready("xt", TT - 1)

                def tokens(name, t, slot, width, a, n):
                    b = room(name)
                    w = ring[slot][:, 0:KC * width].rearrange("p (k n) -> p k n", k=KC)
                    for k in range(KC):
                        last = nc.tensor.matmul(b[:, 0:n], XT[:, k, t * P:(t + 1) * P], w[:, k, a:a + n],
                                                start=k == 0, stop=k == KC - 1)
                    done(last)
                turn_wait(pe, w_a, l * 16 + 16)
                for t in range(TT):
                    tokens(("a", t), t, 0, NA, 0, NA)
                turn_wait(pe, w_o, l * 16 + 16)
                for t in range(TT):
                    for h in range(2):
                        tokens(("o", t, h), t, 2, 2 * NC2, h * NC2, NC2)

                def channels(name, c, slot):
                    b = room(name)
                    w = ring[slot][:, 0:KC * DM].rearrange("p (k n) -> p k n", k=KC)
                    for k in range(KC):
                        last = nc.tensor.matmul(b, w[:, k, c * P:(c + 1) * P], XT[:, k, :], start=k == 0, stop=k == KC - 1)
                    done(last)
                pe.wait_ge(w_qm, 16)
                channels(("q", 0), 0, 0)
                b = room("cum")
                pe.wait_ge(logf_ready.sem, logf_ready.at(1))
                for t in range(TT):
                    for s in range(t + 1):
                        last = nc.tensor.matmul(b[:, MH * t:MH * (t + 1)], C("upto") if s == t else C("ones"), logf[:, s, :],
                                                start=s == 0, stop=s == t)
                done(last)
                channels(("q", 1), 1, 0)
                b = room("at")
                pe.wait_ge(ac_ready.sem, ac_ready.at(1))
                for t in range(TT):
                    last = nc.tensor.transpose(b[0:MH, t * P:(t + 1) * P], ac[:, t, :], ident)
                done(last)
                pe.wait_ge(cq_ready.sem, cq_ready.at(2))
                for name, a, n in ((("cq", 0), 0, P), (("cq", 1), P, P), ("ckv", QR, P), ("kr", QR + KVR, ROPE)):
                    b = room(name)
                    for t in range(TT):
                        last = nc.tensor.transpose(b[0:n, t * P:(t + 1) * P], cqkv[:, t, a:a + n], ident)
                    done(last)
                channels(("q", 2), 2, 0)
                b = room("acol")
                pe.wait_ge(arow_ready.sem, arow_ready.at(1))
                for t in range(TT):
                    last = nc.tensor.transpose(b[:, MH * t:MH * (t + 1)], Arow[:, t * P:(t + 1) * P], K[0:MH, 0:MH])
                done(last)
                channels(("q", 3), 3, 0)
                pe.wait_ge(w_k, 16)
                for c in range(MH):
                    channels(("k", c), c, 2)
                turn_wait(pe, w_v, l * 16 + 16)
                for t in range(TT):
                    tokens(("v", t), t, 3, DM, 0, DM)

                def scores(h):
                    b = room(("abc", h))
                    done(nc.tensor.matmul(b, C("pick")[0:MH, h * P:(h + 1) * P], Arow[:, :], start=True, stop=True))
                    pe.wait_ge(qk_ready.sem, qk_ready.at(MH + h + 1))
                    for s in range(TT):
                        b = room(("st", h, s))
                        done(nc.tensor.matmul(b[:, 0:S - s * P], qkT[:, MH + h, s * P:(s + 1) * P], qkT[:, h, s * P:S],
                                              start=True, stop=True))

                def numerators(h):
                    for half in range(2):
                        b = room(("num", h, half))
                        pe.wait_ge(ptm_ready.sem, ptm_ready.at(h * TT + 2 * half + 2))
                        for i in range(2):
                            t = 2 * half + i
                            for s in range(t + 1):
                                a = pt_at[s] + (t - s) * P
                                last = nc.tensor.matmul(b[:, i * (DH + 1):(i + 1) * (DH + 1)], PTm[h % 2][:, a:a + P], v1[:, s, h, :],
                                                        start=s == 0, stop=s == t)
                        done(last)

                def h_transposed(h):
                    b = room(("mt", h))
                    pe.wait_ge(h_ready.sem, h_ready.at(h + 1))
                    for t in range(TT):
                        last = nc.tensor.transpose(b[:, t * P:(t + 1) * P], hm[h % 2][:, t, :], ident)
                    done(last)
                scores(0)
                scores(1)
                pe.wait_ge(v1_ones.sem, v1_ones.at(1))
                pe.wait_ge(*empty(JOB[("v", TT - 1)]))
                numerators(0)
                scores(2)
                h_transposed(0)
                numerators(1)
                scores(3)
                h_transposed(1)
                numerators(2)
                h_transposed(2)
                numerators(3)
                h_transposed(3)

                turn_wait(pe, w_q, l * 32 + 32)
                wq = ring[1][:, 0:1536].rearrange("p (c n) -> p c n", c=2)
                wkv = ring[1][:, 1536:2560].rearrange("p (h n) -> p h n", h=H)
                for h in range(H):
                    b = room(("kn", h))
                    done(nc.tensor.matmul(b[0:NOPE, :], wkv[:, h, 0:NOPE], ckvT[:, :], start=True, stop=True))
                for t in range(TT):
                    b = room(("mv", t))
                    done(nc.tensor.matmul(b, ckvT[:, t * P:(t + 1) * P], wkv[:, :, NOPE:], start=True, stop=True))

                def queries(t):
                    for n, name in enumerate(("qa", "qb")):
                        b = room((name, t))
                        for c in range(2):
                            last = nc.tensor.matmul(b[:, 0:384], cqT[:, c, t * P:(t + 1) * P], wq[:, c, 384 * n:384 * (n + 1)],
                                                    start=c == 0, stop=c == 1)
                        done(last)

                def queries_transposed(t):
                    pe.wait_ge(q_turned.sem, q_turned.at(t + 1))
                    for n in range(2):
                        b = room(("qt", t, n))
                        for i in range(4):
                            last = nc.tensor.transpose(b[0:QK, i * P:(i + 1) * P], qtok[t % 2][:, 4 * n + i, :], ident)
                        done(last)
                queries(0)
                queries(1)
                queries_transposed(0)
                queries(2)
                queries_transposed(1)
                queries(3)
                queries_transposed(2)
                queries_transposed(3)
                pe.wait_ge(*empty(JOB[("qt", TT - 1, 1)]))
                pe.wait_ge(*empty(JOB[("kn", H - 1)]))
                pe.wait_ge(*empty(JOB[("mv", TT - 1)]))
                pe.wait_ge(kr_copied.sem, kr_copied.at(1))

                def mix_transposed(t):
                    b = room(("mx", t))
                    pe.wait_ge(mix_ready.sem, mix_ready.at(t + 1))
                    for k in range(4):
                        last = nc.tensor.transpose(b[:, k * P:(k + 1) * P], mix[t % 2][:, k * P:(k + 1) * P], ident)
                    done(last)
                for u in range(TT * H + 6):
                    if u < TT * H:
                        t, h = divmod(u, H)
                        b = room(("s", u))
                        done(nc.tensor.matmul(b[:, 0:(t + 1) * P], qT[0:QK, h, t * P:(t + 1) * P], kT[0:QK, h, 0:(t + 1) * P],
                                              start=True, stop=True))
                    if 3 <= u < TT * H + 3:
                        t = (u - 3) // H
                        b = room(("pt", u - 3))
                        pe.wait_ge(p_ready.sem, p_ready.at(u - 2))
                        for s in range(t + 1):
                            last = nc.tensor.transpose(b[:, s * P:(s + 1) * P], Pm[u % 3][:, s * P:(s + 1) * P], ident)
                        done(last)
                    if 4 <= u < TT * H + 4:
                        t, h = divmod(u - 4, H)
                        if h == 0 and t >= 2:
                            pe.wait_ge(o_read.sem, o_read.at(t - 1))
                        pe.wait_ge(*empty(JOB[("pt", u - 4)]))
                        for s in range(t + 1):
                            last = nc.tensor.matmul(PB[:, 6 + t % 2, VD * h:VD * (h + 1)], PT[(u - 4) % 3][:, s * P:(s + 1) * P],
                                                    mv[:, s, VD * h:VD * (h + 1)], start=s == 0, stop=s == t)
                        if h == H - 1:
                            last.then_inc(*o_full.up())
                    if u >= 15 and (u - 15) % H == 0:
                        mix_transposed((u - 15) // H)
                mix_transposed(TT - 1)

                pe.wait_ge(w_out, 32)
                pe.wait_ge(*empty(JOB[("mt", MH - 1)]))
                pe.wait_ge(*empty(JOB[("mx", TT - 1)]))
                def out_projection(t):
                    for h in range(2):
                        b = room(("out", t, h))
                        w = ring[3 - h][:, 0:4096].rearrange("p (k n) -> p k n", k=KC)
                        for k in range(KC):
                            last = nc.tensor.matmul(b, XT[:, k, t * P:(t + 1) * P], w[:, k, :], start=k == 0, stop=k == KC - 1)
                        done(last)

                def router(t):
                    xt_ready("xt2", t)
                    for k in range(KC):
                        last = nc.tensor.matmul(bank("logit")[:, 72 * t:72 * (t + 1)], XT[:, k, t * P:(t + 1) * P], wr[:, k, :],
                                                start=k == 0, stop=k == KC - 1)
                    return last
                turn_wait(pe, wr_in, l * 32 + 32)
                for t in range(TT + 1):
                    if t < TT:
                        out_projection(t)
                    if t >= 2:
                        router(t - 2)
                    if t:
                        pe.wait_ge(x_ready.sem, x_ready.at(t))
                        transpose_x("xt2", [t - 1])
                done(router(TT - 1))
                b = room("rank")
                pe.wait_ge(oh_ready.sem, oh_ready.at(1))

                def tiles_of(a, z):
                    return b[:, NE * a:NE * z].rearrange("p (t n) -> p t n", n=NE)
                nc.tensor.matmul(tiles_of(0, 1), C("before"), OHS[:, 0:1, :], start=True, stop=True, skip_group_check=True)
                for s in range(TT):
                    last = nc.tensor.matmul(tiles_of(s + 1, TT + 1), C("ones"), OHS[:, s, :].unsqueeze(1).to_broadcast((P, TT - s, NE)),
                                            start=s == 0, stop=s == TT - 1, skip_group_check=True)
                    if s == 0:
                        nc.tensor.matmul(tiles_of(1, TT), C("before"), OHS[:, 1:TT, :], start=False, stop=False, skip_group_check=True)
                done(last)
                with pe.Fori(0, IT) as i:
                    for b in range(2):
                        group(main, b, i, i * 2 + b)
                n = spill_groups(pe)
                with pe.If(n > 0):
                    stored_all(pe)
                    with pe.Fori(0, n) as g:
                        group(spill, 0, g, g)
                with pe.Else():
                    pass
                end_layer(pe, l)

        @block.scalar
        def _(act):
            act.wait_ge(rope_ready, 1)
            nc.scalar.activation(sin[:, :, :].rearrange("p t f -> p (t f)"), ang[:, 0, :], ACT.Sin).then_inc(rope_ready, 1)
            nc.scalar.activation(cos[:, :, :].rearrange("p t f -> p (t f)"), ang[:, 1, :], ACT.Sin).then_inc(rope_ready, 1)
            act.wait_ge(small_set, 4)
            act.preload_act_table_set("natural_log_exp_and_others")

            def group(path, b, it, m):
                act.wait_ge(path.xg_T[b], it + 2)
                nc.scalar.copy(xgT[b][:, 0:512], PB[:, 0, :]).then_inc(path.xgT_a[b], 1)
                turn_wait(act, path.stored[b], it * 64 + 64)

                def gate(q):
                    act.wait_ge(path.gu[q % 2], m * 2 + q // 2 + 1)
                    act.wait_ge(path.st[q % 2], m * 2 + q // 2 + 1)
                    nc.scalar.activation(esb[q % 2][:, :], PB[:, 2 + q % 2, 0:64], ACT.Exp, scale=-1.0).then_inc(path.ex[q % 2], 1)

                def result(q):
                    act.wait_ge(path.down[q], m + 2)
                    nc.scalar.copy(ysb[b][:, 256 * q:256 * (q + 1)], PB[:, 4 + q % 2, 0:256]).then_inc(path.y[q % 2], 1)
                for q in range(GRP):
                    gate(q)
                    if q:
                        result(q - 1)
                result(GRP - 1)
                for i in range(2):
                    act.wait_ge(path.y[i], m * 2 + 3)

            def store(path, b, slot):
                for j in range(4):
                    act.dma_start(y_dram[bass.ds(slot, P), 256 * j:256 * (j + 1)].rearrange("(q s) n -> s q n", q=GRP),
                                  ysb[b][32 * j:32 * (j + 1), :].rearrange("p (q n) -> p q n", q=GRP)).then_inc(path.stored[b], 16)

            with act.Fori(0, L) as l:
                def link(ins):
                    ins.then_inc(*astep.up())
                    act.wait_ge(astep.sem, astep.at(astep.n))

                def take(name):
                    act.wait_ge(*full(name))
                    return bank(name)

                def xt(kind, tiles):
                    for t in tiles:
                        b = take((kind, t, 0))
                        nc.scalar.copy(XT[:, 0:4, t * P:(t + 1) * P], b.rearrange("p (k i) -> p k i", k=4)).then_inc(*emptying((kind, t, 0)))
                xt("xt", range(TT))
                for t in range(TT):
                    for h in range(2):
                        b = take(("o", t, h))
                        n = NC2 if h == 0 else DM - NC2
                        e = nc.scalar.activation(osig[:, t, h * NC2:h * NC2 + n], b[:, 0:n], ACT.Exp, scale=-1.0)
                        if h:
                            e = nc.scalar.copy(gates[:, t, :], b[:, n:n + 2 * MH])
                        e.then_inc(*emptying(("o", t, h)))
                act.wait_ge(gate_neg.sem, gate_neg.at(1))
                link(nc.scalar.activation(gt[:, 1], gt[:, 0], ACT.Exp))
                nc.scalar.activation(gt[:, 2], gt[:, 1], ACT.Ln, bias=biases[:, 2:3]).then_inc(*gate_ln.up())
                act.wait_ge(*empty(JOB[("a", TT - 1)]))
                for t in range(TT):
                    link(nc.scalar.activation(hm[0][:, 0:2, :].rearrange("p t e -> p (t e)"), cqkv[:, t, 0:QR], ACT.Square, accum_out=ss[:, 0, t:t + 1]))
                    link(nc.scalar.activation(hm[0][:, 2, :], cqkv[:, t, QR:QR + KVR], ACT.Square, accum_out=ss[:, 1, t:t + 1]))
                link(nc.scalar.activation(ss[:, 0, :], ss[:, 0, :], ACT.Ln, bias=biases[:, 1:2], scale=1.0 / QR))
                link(nc.scalar.activation(ss[:, 1, :], ss[:, 1, :], ACT.Ln, bias=biases[:, 1:2], scale=1.0 / KVR))
                nc.scalar.activation(ss[:, :, :], ss[:, :, :], ACT.Exp, scale=-0.5).then_inc(*cq_sq.up())
                ov = osig[:, :, :]
                link(nc.scalar.activation(ov, ov, ACT.Ln, bias=biases[:, 2:3]))
                link(nc.scalar.activation(ov, ov, ACT.Exp, scale=-1.0))

                def conv_tap(c):
                    b = take(("q", c) if c < MH else ("k", c - MH))
                    if c >= 2:
                        act.wait_ge(qk_ready.sem, qk_ready.at(c - 1))
                    nc.scalar.activation(convt[c % 2], b, ACT.Identity, bias=vecT[:, c, 4:5], scale=vecT[:, c, 3:4]).then_inc(*conv_first.up())

                def silu_sigmoid(c):
                    act.wait_ge(conv_ready.sem, conv_ready.at(c + 1))
                    if c >= 1:
                        act.wait_ge(qk_ready.sem, qk_ready.at(c))
                    link(nc.scalar.activation(convt[2], convt[c % 2], ACT.Exp, scale=-1.0))
                    link(nc.scalar.activation(convt[2], convt[2], ACT.Ln, bias=biases[:, 2:3]))
                    nc.scalar.activation(convt[2], convt[2], ACT.Exp, scale=-1.0).then_inc(*silu_exp.up())
                conv_tap(0)
                conv_tap(1)
                silu_sigmoid(0)
                for c in range(2):
                    b = take(("cq", c))
                    nc.scalar.activation(cqT[:, c, :], b, ACT.Identity, scale=vecT[:, c, 6:7]).then_inc(*emptying(("cq", c)))
                b = take("ckv")
                nc.scalar.activation(ckvT[:, :], b, ACT.Identity, scale=vecT[:, 2, 6:7]).then_inc(*emptying("ckv"))
                b = take("kr")
                nc.scalar.copy(krT[NOPE:QK, :], b[0:ROPE, :]).then_inc(*emptying("kr"))
                for c in range(2, 8):
                    conv_tap(c)
                    silu_sigmoid(c - 1)
                    if c == 4:
                        act.wait_ge(m_ready.sem, m_ready.at(1))
                        nc.scalar.activation(em[:, :, :], gt[:, 0], ACT.Exp, scale=-1.0).then_inc(*em_ready.up())
                silu_sigmoid(7)
                for t in range(TT):
                    b = take(("v", t))
                    nc.scalar.copy(v1[:, t, :, 0:DH], b.rearrange("p (h e) -> p h e", h=MH)).then_inc(*emptying(("v", t)))

                def weights(h):
                    b = take(("abc", h))
                    for s in range(TT):
                        i = h * TT + s
                        if i >= 2:
                            act.wait_ge(ptm_written.sem, ptm_written.at(i - 1))
                        else:
                            act.wait_ge(qk_ready.sem, qk_ready.at(8))
                        w = nc.scalar.activation(Wm[i % 2][:, 0:S - s * P], b[:, s * P:S], ACT.Exp, bias=ac[:, s, h:h + 1], scale=-1.0)
                        if s == TT - 1:
                            w.then_inc(*emptying(("abc", h)))
                            act.wait_ge(*empty(JOB[("abc", h)]))
                            nc.scalar.sem_inc(w_ready.up()[0], 1)
                        else:
                            w.then_inc(*w_ready.up())

                def rsqrt(buf, n, eps, s_in, s_out, k):
                    act.wait_ge(s_in.sem, s_in.at(k))
                    link(nc.scalar.activation(buf, buf, ACT.Ln, bias=biases[:, eps:eps + 1], scale=1.0 / n))
                    nc.scalar.activation(buf, buf, ACT.Exp, scale=-0.5).then_inc(*s_out.up())

                def mix_m(h):
                    b = take(("mt", h))
                    nc.scalar.activation(XT[:, 4 + h, :], b, ACT.Identity, scale=vecT[:, 4 + h, 5:6]).then_inc(*emptying(("mt", h)))
                weights(0)
                weights(1)
                rsqrt(den[:, 3, :], DH, 1, h_sq, h_rs, 1)
                weights(2)
                mix_m(0)
                rsqrt(den[:, 3, :], DH, 1, h_sq, h_rs, 2)
                weights(3)
                mix_m(1)
                rsqrt(den[:, 3, :], DH, 1, h_sq, h_rs, 3)
                mix_m(2)
                rsqrt(den[:, 3, :], DH, 1, h_sq, h_rs, 4)
                mix_m(3)
                act.wait_ge(h_ready.sem, h_ready.at(MH))
                for h in range(0, H, 2):
                    b = take(("kn", h))
                    nc.scalar.copy(kT[0:NOPE, h, :], b[0:NOPE, :]).then_inc(*emptying(("kn", h)))
                for t in range(TT):
                    b = take(("mv", t))
                    nc.scalar.copy(mv[:, t, :], b).then_inc(*emptying(("mv", t)))
                for t in range(TT):
                    if t >= 2:
                        act.wait_ge(*full(("qt", t - 2, 1)))
                    for n, name in enumerate(("qa", "qb")):
                        b = take((name, t))
                        nc.scalar.copy(qtok[t % 2][:, 4 * n:4 * n + 4, :].rearrange("p h d -> p (h d)"), b[:, 0:384]).then_inc(*emptying((name, t)))

                def mix_a(t):
                    b = take(("mx", t))
                    for k in range(4):
                        e = nc.scalar.activation(XT[:, k, t * P:(t + 1) * P], b[:, k * P:(k + 1) * P], ACT.Identity, scale=vecT[:, k, 5:6])
                    e.then_inc(*emptying(("mx", t)))
                for u in range(TT * H):
                    t, h = divmod(u, H)
                    act.wait_ge(mx_ready.sem, mx_ready.at(u + 1))
                    if u >= 3:
                        act.wait_ge(*full(("pt", u - 3)))
                    n = (t + 1) * P
                    b = bank(("s", u))
                    e = nc.scalar.activation(Pm[u % 3][:, 0:n], b[:, 0:n], ACT.Exp, bias=smx[:, u:u + 1], scale=-1.0,
                                             accum_out=ssum[:, u:u + 1])
                    e.then_inc(*emptying(("s", u)))
                    act.wait_ge(*empty(JOB[("s", u)]))
                    nc.scalar.sem_inc(p_ready.up()[0], 1)
                    if h == 5 and t >= 1:
                        rsqrt(mnorm[:, 2 + (t - 1) % 2, :], VD, 1, o_sq, o_rs, t)
                    if u >= 15 and (u - 15) % H == 0:
                        mix_a((u - 15) // H)
                rsqrt(mnorm[:, 2 + (TT - 1) % 2, :], VD, 1, o_sq, o_rs, TT)
                mix_a(TT - 1)

                def normalise(t, k):
                    i = t % 2
                    rsqrt(rstd[:, i:i + 1], 1, 0, ln_var, ln_rs, k + t + 1)
                    act.wait_ge(ln_rs.sem, ln_rs.at(k + t + 1))
                    link(nc.scalar.activation(nmean[:, 1, i:i + 1], rstd[:, i:i + 1], ACT.Identity, scale=nmean[:, 0, i:i + 1]))
                    nc.scalar.activation(X[:, t, :], X[:, t, :], ACT.Identity, bias=nmean[:, 1, i:i + 1], scale=rstd[:, i:i + 1]) \
                        .then_inc(*ln_norm.up())
                for t in range(TT):
                    if t:
                        xt("xt2", [t - 1])
                    normalise(t, 0)
                xt("xt2", [TT - 1])
                for k, (i, o) in enumerate(((r8[:, 1], r8[:, 2]), (r1[:, 6, :], r1[:, 7, :]))):
                    act.wait_ge(exp_in.sem, exp_in.at(k + 1))
                    nc.scalar.activation(o, i, ACT.Exp).then_inc(*exp_out.up())
                with act.Fori(0, IT) as i:
                    for b in range(2):
                        group(main, b, i, i * 2 + b)
                        store(main, b, (i * 2 + b) * P)
                n = spill_groups(act)
                with act.If(n > 0):
                    stored_all(act)
                    with act.Fori(0, n) as g:
                        group(spill, 0, g, g)
                        store(spill, 0, (g + EG) * P)
                with act.Else():
                    pass
                for t in range(TT + 1):
                    if t < TT:
                        turn_wait(act, y_in[t], l * 32 + 32)
                        nc.scalar.activation(y_rows[t][0], y_rows[t][0], ACT.Identity, scale=wts[:, 0, t:t + 1]).then_inc(*y_scaled.up())
                    if t:
                        normalise(t - 1, TT)
                end_layer(act, l)

        @block.vector
        def _(dve):
            V = nc.vector
            V.memset(biases[:, 0:1], LN_EPS).then_inc(small_set, 1)
            V.memset(biases[:, 1:2], RMS_EPS).then_inc(small_set, 1)
            V.memset(biases[:, 2:3], 1.0).then_inc(small_set, 1)
            V.memset(block_col[:, :], 0.0).then_inc(small_set, 1)
            dve.wait_ge(consts_in, 16)
            dve.wait_ge(pos_in, 16)
            steps = [0]

            def rope(ins):
                steps[0] += 1
                ins.then_inc(rope_step, 1)
                dve.wait_ge(rope_step, steps[0])
            rope(V.tensor_copy(pos_f[:, :], pos_i[:, :]))
            HF = ROPE // 2
            for t in range(TT):
                rope(V.tensor_scalar(ang[:, 2, HF * t:HF * (t + 1)], C("freq"), pos_f[:, t:t + 1], None, ALU.mult))
            two_pi = 2 * np.pi
            c1 = float(np.float32(6.28125))
            c2 = float(np.float32(np.float64(two_pi - c1)).view(np.int32) & -4096) if False else float(np.float32(round((two_pi - c1) * 2 ** 19) / 2 ** 19))
            c3 = float(np.float32(two_pi - c1 - c2))
            for o, shift in ((0, 0.0), (1, 0.25)):
                a = ang[:, o, :]
                rope(V.tensor_scalar(a, ang[:, 2, :], 1.0 / two_pi, shift, ALU.mult, ALU.add))
                rope(V.tensor_copy(turns[:, :], a))
                rope(V.tensor_copy(pos_t := hsq[:, 0:TT * HF], turns[:, :]))
                rope(V.scalar_tensor_tensor(a, pos_t, -c1, ang[:, 2, :], ALU.mult, ALU.add))
                rope(V.scalar_tensor_tensor(a, pos_t, -c2, a, ALU.mult, ALU.add))
                rope(V.scalar_tensor_tensor(a, pos_t, -c3, a, ALU.mult, ALU.add))
                if o:
                    rope(V.tensor_scalar(a, a, float(np.pi / 2), None, ALU.add))
                over = hsq[:, 64:64 + TT * HF]
                for sign in (1.0, -1.0):
                    rope(V.tensor_scalar(over, a, sign, float(np.pi), ALU.mult, ALU.is_gt))
                    rope(V.scalar_tensor_tensor(a, over, -sign * two_pi, a, ALU.mult, ALU.add))
                last = V.tensor_scalar(a, a, float(np.float32(3.1415925)), -float(np.float32(3.1415925)), ALU.min, ALU.max)
                steps[0] += 1
                last.then_inc(rope_step, 1)
            dve.wait_ge(rope_step, steps[0])
            V.sem_inc(rope_ready, 1)
            dve.wait_ge(rope_ready, 3)
            dve.wait_ge(small_set, 4)

            lane = C("lane").unsqueeze(1).to_broadcast((P, TT, P))

            def slots_of(k):
                return slf[:, k, :].unsqueeze(2).to_broadcast((P, TT, P))

            def next_slots(path, b, m):
                dve.wait_ge(path.oh_step, m * 3 + 3)
                V.tensor_tensor(oh[b], lane, slots_of(0), ALU.is_equal).then_inc(path.oh_step, 1)
                V.tensor_tensor(oh_b, lane, slots_of(1), ALU.is_equal).then_inc(path.oh_step, 1)
                dve.wait_ge(path.oh_step, m * 3 + 5)
                V.tensor_tensor(oh[b], oh[b], oh_b, ALU.add).then_inc(path.oh[b], 1)
                V.tensor_scalar(slf[:, :, :], slf[:, :, :], -float(P), None, ALU.add).then_inc(path.oh_step, 1)

            def group(path, b, it, m):
                dve.wait_ge(path.xg_T[b], it + 2)
                V.tensor_copy(xgT[b][:, 512:D], PB[:, 1, :]).then_inc(path.xgT_d[b], 1)
                for q in range(GRP):
                    i, n = q % 2, m * 2 + q // 2
                    dve.wait_ge(path.ex[i], n + 1)
                    g2, u2 = PB[:, 2 + i, 0:64], PB[:, 2 + i, 64:P]
                    V.tensor_scalar(esb[i][:, :], esb[i][:, :], 1.0, None, ALU.add).then_inc(moe_step[path is spill], 1)
                    dve.wait_ge(moe_step[path is spill], m * 12 + q * 3 + 1)
                    V.reciprocal(esb[i][:, :], esb[i][:, :]).then_inc(moe_step[path is spill], 1)
                    dve.wait_ge(moe_step[path is spill], m * 12 + q * 3 + 2)
                    V.tensor_tensor(esb[i][:, :], g2, esb[i][:, :], ALU.mult).then_inc(moe_step[path is spill], 1)
                    dve.wait_ge(moe_step[path is spill], m * 12 + q * 3 + 3)
                    V.tensor_tensor(hsb[i][:, :], u2, esb[i][:, :], ALU.mult).then_inc(path.st[i], 1)
                    dve.wait_ge(path.st[i], n + 2)
                    if q >= 2:
                        dve.wait_ge(path.down[q - 2], m + 2)
                    else:
                        dve.wait_ge(path.down[q + 2], m + 1)
                    V.transpose(hT[i][:, :], hsb[i][:, :]).then_inc(path.hT[i], 1)
                    if q == 1:
                        next_slots(path, (b + 1) % path.bufs, m)

            with dve.Fori(0, L) as l:
                def link(ins):
                    ins.then_inc(*dstep.up())
                    dve.wait_ge(dstep.sem, dstep.at(dstep.n))

                def take(name):
                    dve.wait_ge(*full(name))
                    return bank(name)

                b = take("vec")
                bv = b[:, 0:8 * KC].rearrange("p (k r) -> p k r", k=KC)
                link(V.tensor_copy(vecT[:, :, 0:6], bv[:, :, 0:6]))
                V.tensor_copy(vecT[:, 0:3, 6:7], bv[:, 0:3, 6:7]).then_inc(*emptying("vec"))

                def xt(kind, tiles):
                    for t in tiles:
                        b = take((kind, t, 1))
                        V.tensor_copy(XT[:, 4:8, t * P:(t + 1) * P], b.rearrange("p (k i) -> p k i", k=4)).then_inc(*emptying((kind, t, 1)))
                xt("xt", range(TT))
                for t in range(TT):
                    b = take(("a", t))
                    V.tensor_copy(cqkv[:, t, :], b[:, 0:NA]).then_inc(*emptying(("a", t)))
                dve.wait_ge(*empty(JOB[("a", TT - 1)]))
                rt_ = [rtmp[:, i, 0:TT * HF].rearrange("p (t f) -> p t f", t=TT) for i in range(4)]
                k1, k2 = cqkv[:, :, QR + KVR:QR + KVR + HF], cqkv[:, :, QR + KVR + HF:NA]

                def turn(x1, x2, cs, sn, tmp, last_signal):
                    V.tensor_tensor(tmp[0], x1, cs, ALU.mult)
                    V.tensor_tensor(tmp[1], x2, sn, ALU.mult)
                    V.tensor_tensor(tmp[2], x2, cs, ALU.mult)
                    link(V.tensor_tensor(tmp[3], x1, sn, ALU.mult))
                    V.tensor_tensor(x1, tmp[0], tmp[1], ALU.subtract)
                    V.tensor_tensor(x2, tmp[2], tmp[3], ALU.add).then_inc(*last_signal.up())
                turn(k1, k2, cos[:, :, :], sin[:, :, :], rt_, cq_ready)
                dve.wait_ge(*empty(JOB[("o", TT - 1, 1)]))
                turn_wait(dve, gate_b_in, l * 16 + 16)
                link(V.tensor_tensor(gates[:, :, :], gates[:, :, :], gate_b[:, :].unsqueeze(1).to_broadcast((P, TT, 2 * MH)), ALU.add))
                gi, gf = gates[:, :, 0:MH], gates[:, :, MH:]
                link(V.tensor_scalar(gt[:, 1], gf, -1.0, None, ALU.mult))
                V.tensor_tensor(gt[:, 0], gt[:, 1], gf, ALU.min).then_inc(*gate_neg.up())
                dve.wait_ge(gate_ln.sem, gate_ln.at(1))
                V.scalar_tensor_tensor(logf[:, :, :], gf, 0.0, gt[:, 2], ALU.min, ALU.subtract).then_inc(*logf_ready.up())
                dve.wait_ge(cq_sq.sem, cq_sq.at(1))
                for t in range(TT):
                    V.tensor_scalar(cqkv[:, t, 0:QR], cqkv[:, t, 0:QR], ss[:, 0, t:t + 1], None, ALU.mult)
                    last = V.tensor_scalar(cqkv[:, t, QR:QR + KVR], cqkv[:, t, QR:QR + KVR], ss[:, 1, t:t + 1], None, ALU.mult)
                last.then_inc(*cq_ready.up())
                def cumulated():
                    b = take("cum")
                    link(V.tensor_copy(Bc[:, :, :], b[:, 0:TT * MH].rearrange("p (t h) -> p t h", t=TT)))
                    V.tensor_tensor(ac[:, :, :], gi, Bc[:, :, :], ALU.subtract).then_inc(*emptying("cum"))
                    dve.wait_ge(*empty(JOB["cum"]))
                    V.sem_inc(ac_ready.up()[0], 1)

                def conv(c):
                    name = ("q", c) if c < MH else ("k", c - MH)
                    b = take(name)
                    y = convt[c % 2]
                    dve.wait_ge(conv_first.sem, conv_first.at(c + 1))
                    for j in range(1, CW):
                        last = V.scalar_tensor_tensor(y[:, j:S], b[:, 0:S - j], vecT[:, c, 3 - j:4 - j], y[:, j:S], ALU.mult, ALU.add)
                        if j < CW - 1:
                            link(last)
                    last.then_inc(*emptying(name))
                    dve.wait_ge(*empty(JOB[name]))
                    V.sem_inc(conv_ready.up()[0], 1)

                def silu(c):
                    dve.wait_ge(silu_exp.sem, silu_exp.at(c + 1))
                    V.tensor_tensor(qkT[:, c, :], convt[c % 2], convt[2], ALU.mult).then_inc(*qk_ready.up())
                dve.wait_ge(y_zeroed, 16 * SG)
                conv(0)
                cumulated()
                conv(1)
                b = take("at")
                link(V.tensor_copy(arow[:, :], b[0:MH, :]))
                V.tensor_tensor_scan(Arow[:, :], arow[:, :], arow[:, :], 0.0, ALU.max, ALU.max).then_inc(*emptying("at"))
                dve.wait_ge(*empty(JOB["at"]))
                V.sem_inc(arow_ready.up()[0], 1)
                silu(0)
                conv(2)
                silu(1)
                b = take("acol")
                V.tensor_tensor(gt[:, 0], b[:, 0:TT * MH].rearrange("p (t h) -> p t h", t=TT), Bc[:, :, :], ALU.add).then_inc(*emptying("acol"))
                dve.wait_ge(*empty(JOB["acol"]))
                V.sem_inc(m_ready.up()[0], 1)
                for c in range(3, 8):
                    conv(c)
                    silu(c - 1)
                silu(7)

                def weigh(h):
                    for s in range(TT):
                        b = take(("st", h, s))
                        dve.wait_ge(w_ready.sem, w_ready.at(h * TT + s + 1))
                        if h >= 2 and s == 0:
                            dve.wait_ge(*full(("num", h - 2, 1)))
                        n = S - s * P
                        V.scalar_tensor_tensor(PTm[h % 2][:, pt_at[s]:pt_at[s] + n], b[:, 0:n], DH ** -0.5, Wm[(h * TT + s) % 2][:, 0:n],
                                               ALU.mult, ALU.mult).then_inc(*emptying(("st", h, s)))
                        dve.wait_ge(*empty(JOB[("st", h, s)]))
                        V.sem_inc(ptm_written.up()[0], 1)

                def normalise(h):
                    d, o = den, hm[h % 2]
                    for i in range(2):
                        b = take(("num", h, i))
                        bv = b[:, 0:2 * (DH + 1)].rearrange("p (t e) -> p t e", t=2)
                        dv = d[:, 0, 2 * i:2 * i + 2].unsqueeze(2)
                        link(V.tensor_copy(dv, bv[:, :, DH:]))
                        link(V.tensor_scalar(d[:, 1, 2 * i:2 * i + 2], d[:, 0, 2 * i:2 * i + 2], -1.0, None, ALU.mult))
                        link(V.tensor_tensor(d[:, 0, 2 * i:2 * i + 2], d[:, 0, 2 * i:2 * i + 2], d[:, 1, 2 * i:2 * i + 2], ALU.max))
                        if i == 0 and h == 0:
                            dve.wait_ge(em_ready.sem, em_ready.at(1))
                        link(V.tensor_tensor(d[:, 0, 2 * i:2 * i + 2], d[:, 0, 2 * i:2 * i + 2], em[:, 2 * i:2 * i + 2, h], ALU.max))
                        link(V.reciprocal(d[:, 1, 2 * i:2 * i + 2], d[:, 0, 2 * i:2 * i + 2]))
                        if i == 0 and h >= 2:
                            dve.wait_ge(*full(("mt", h - 2)))
                        V.tensor_tensor(o[:, 2 * i:2 * i + 2, :], bv[:, :, 0:DH], d[:, 1, 2 * i:2 * i + 2].unsqueeze(2).to_broadcast((P, 2, DH)),
                                        ALU.mult).then_inc(*emptying(("num", h, i)))
                    dve.wait_ge(*empty(JOB[("num", h, 1)]))
                    hs = hsq[:, :].rearrange("p (t e) -> p t e", t=TT)
                    link(V.tensor_tensor(hs, o[:, :, :], o[:, :, :], ALU.mult))
                    V.reduce_sum(d[:, 3, :], hs, AX.X).then_inc(*h_sq.up())
                    dve.wait_ge(h_rs.sem, h_rs.at(h + 1))
                    link(V.tensor_tensor(o[:, :, :], o[:, :, :], d[:, 3, :].unsqueeze(2).to_broadcast((P, TT, DH)), ALU.mult))
                    V.tensor_tensor(o[:, :, :], o[:, :, :], osig[:, :, h * DH:(h + 1) * DH], ALU.mult).then_inc(*h_ready.up())
                weigh(0)
                weigh(1)
                normalise(0)
                weigh(2)
                normalise(1)
                weigh(3)
                normalise(2)
                normalise(3)
                for h in range(1, H, 2):
                    b = take(("kn", h))
                    V.tensor_copy(kT[0:NOPE, h, :], b[0:NOPE, :]).then_inc(*emptying(("kn", h)))
                cs8 = [cos[:, t, :].unsqueeze(1).to_broadcast((P, H, HF)) for t in range(TT)]
                sn8 = [sin[:, t, :].unsqueeze(1).to_broadcast((P, H, HF)) for t in range(TT)]
                rt8 = [rtmp[:, i, :].rearrange("p (h f) -> p h f", h=H) for i in range(4)]

                def turn_q(t):
                    dve.wait_ge(*empty(JOB[("qb", t)]))
                    if t:
                        dve.wait_ge(q_turned.sem, q_turned.at(t))
                    turn(qtok[t % 2][:, :, NOPE:NOPE + HF], qtok[t % 2][:, :, NOPE + HF:], cs8[t], sn8[t], rt8, q_turned)

                def put_q(t):
                    for n in range(2):
                        b = take(("qt", t, n))
                        V.tensor_copy(qT[0:QK, 4 * n:4 * n + 4, t * P:(t + 1) * P], b[0:QK, :].rearrange("p (h i) -> p h i", h=4)).then_inc(*emptying(("qt", t, n)))
                turn_q(0)
                turn_q(1)
                put_q(0)
                turn_q(2)
                put_q(1)
                turn_q(3)
                put_q(2)
                put_q(3)

                def softmax_max(u):
                    n = (u // H + 1) * P
                    b = take(("s", u))
                    V.tensor_tensor_reduce(out=b[:, 0:n], in0=b[:, 0:n], in1=C("future")[:, S - n:], scale=-QK ** -0.5, scalar=3e38,
                                           op0=ALU.add, op1=ALU.min, accum_out=smx[:, u:u + 1]).then_inc(*mx_ready.up())

                def put_pt(u):
                    b = take(("pt", u))
                    n = (u // H + 1) * P
                    V.tensor_copy(PT[u % 3][:, 0:n], b[:, 0:n]).then_inc(*emptying(("pt", u)))

                def head_norm(t, part):
                    o = mix[t % 2]
                    o3 = o[:, :].rearrange("p (h e) -> p h e", h=H)
                    r = mnorm[:, 0, :]
                    q = mnorm[:, 2 + t % 2, :]
                    if part == 0:
                        dve.wait_ge(o_full.sem, o_full.at(t + 1))
                        if t >= 2:
                            dve.wait_ge(*full(("mx", t - 2)))
                        link(V.reciprocal(r, ssum[:, t * H:(t + 1) * H]))
                        link(V.tensor_tensor(o3, PB[:, 6 + t % 2, :].rearrange("p (h e) -> p h e", h=H), r.unsqueeze(2).to_broadcast((P, H, VD)), ALU.mult))
                        V.sem_inc(o_read.up()[0], 1)
                        link(V.tensor_tensor(hsq[:, :], o[:, :], o[:, :], ALU.mult))
                        V.reduce_sum(q, hsq[:, :].rearrange("p (h e) -> p h e", h=H), AX.X).then_inc(*o_sq.up())
                    else:
                        dve.wait_ge(o_rs.sem, o_rs.at(t + 1))
                        V.tensor_tensor(o3, o3, q.unsqueeze(2).to_broadcast((P, H, VD)), ALU.mult).then_inc(*mix_ready.up())
                for u in range(TT * H + 6):
                    if u < TT * H:
                        softmax_max(u)
                    if 3 <= u < TT * H + 3:
                        put_pt(u - 3)
                    if u >= 12 and (u - 12) % H < 2:
                        head_norm((u - 12) // H, (u - 12) % H)

                def statistics(t):
                    x, i = X[:, t, :], t % 2
                    link(V.bn_stats(stats[:, 0, :], x[:, 0:512]))
                    link(V.bn_stats(stats[:, 1, :], x[:, 512:D]))
                    link(V.bn_aggr(mvar[i][:, :], stats[:, :, :].rearrange("p a s -> p (a s)")))
                    link(V.tensor_scalar(nmean[:, 0, i:i + 1], mvar[i][:, 0:1], -1.0, None, ALU.mult))
                    V.tensor_copy(rstd[:, i:i + 1], mvar[i][:, 1:2]).then_inc(*ln_var.up())

                def gain(t, k, gain_waits):
                    dve.wait_ge(ln_norm.sem, ln_norm.at(k + t + 1))
                    dve.wait_ge(ln_in, gain_waits)
                    return V.tensor_tensor(X[:, t, :], X[:, t, :], lnG, ALU.mult)

                def offset(t):
                    return V.tensor_tensor(X[:, t, :], X[:, t, :], lnB, ALU.add)
                for t in range(TT):
                    for h in range(2):
                        b = take(("out", t, h))
                        V.scalar_tensor_tensor(X[:, t, 512 * h:512 * (h + 1)], X[:, t, 512 * h:512 * (h + 1)], ALPHA, b, ALU.mult, ALU.add) \
                            .then_inc(*emptying(("out", t, h)))
                    dve.wait_ge(*empty(JOB[("out", t, 1)]))
                    statistics(t)
                    if t:
                        xt("xt2", [t - 1])
                    link(gain(t, 0, 32))
                    offset(t).then_inc(*x_ready.up())
                xt("xt2", [TT - 1])

                b = take("logit")
                V.tensor_copy(lg[:, :, :], b[:, 0:TT * 72].rearrange("p (t n) -> p t n", t=TT)).then_inc(*emptying("logit"))
                dve.wait_ge(*empty(JOB["logit"]))
                d8 = C("down8").unsqueeze(1).to_broadcast((P, TT, 8))

                def b8(v):
                    return v.unsqueeze(2).to_broadcast((P, TT, 8))

                def first_max(scores, mx, shifted, tmp, best, onehot):
                    link(V.reduce_max(mx, scores, AX.X))
                    link(V.tensor_tensor(shifted, scores, b8(mx), ALU.subtract))
                    link(V.scalar_tensor_tensor(tmp, shifted, 0.0, d8, ALU.is_ge, ALU.mult))
                    link(V.reduce_max(best, tmp, AX.X))
                    link(V.tensor_tensor(onehot, d8, b8(best), ALU.is_equal))
                first_max(lg[:, :, 0:8], r1[:, 0], r8[:, 1], r8[:, 3], r1[:, 1], r8[:, 0])
                V.sem_inc(exp_in.up()[0], 1)
                dve.wait_ge(exp_out.sem, exp_out.at(1))
                link(V.reduce_sum(r1[:, 2], r8[:, 2], AX.X))
                link(V.reciprocal(r1[:, 3], r1[:, 2]))
                goh = r8[:, 0]
                prod = rt[:, 0:256].rearrange("p (t g e) -> p t g e", t=TT, g=8)
                link(V.tensor_tensor(prod, lg[:, :, 8:].rearrange("p t (g e) -> p t g e", g=8), goh.unsqueeze(3).to_broadcast((P, TT, 8, 8)), ALU.mult))
                link(V.reduce_sum(r8[:, 4], prod.rearrange("p t g e -> p t e g"), AX.X))
                first_max(r8[:, 4], r1[:, 4], r8[:, 5], r8[:, 3], r1[:, 1], r8[:, 6])
                link(V.scalar_tensor_tensor(r8[:, 5], r8[:, 6], -BIG, r8[:, 5], ALU.mult, ALU.add))
                first_max(r8[:, 5], r1[:, 6], r8[:, 4], r8[:, 3], r1[:, 1], r8[:, 7])
                V.sem_inc(exp_in.up()[0], 1)
                dve.wait_ge(exp_out.sem, exp_out.at(2))
                link(V.tensor_scalar(r1[:, 8], r1[:, 7], 1.0, None, ALU.add))
                link(V.reciprocal(r1[:, 9], r1[:, 8]))
                link(V.tensor_tensor(wts[:, 0], r1[:, 9], r1[:, 3], ALU.mult))
                link(V.tensor_tensor(wts[:, 1], wts[:, 0], r1[:, 7], ALU.mult))
                for k in range(2):
                    link(V.tensor_tensor(OH2[:, k].rearrange("p t (g e) -> p t g e", g=8), goh.unsqueeze(3).to_broadcast((P, TT, 8, 8)),
                                         r8[:, 6 + k].unsqueeze(2).to_broadcast((P, TT, 8, 8)), ALU.mult))
                V.tensor_tensor(OHS[:, :, :], OH2[:, 0], OH2[:, 1], ALU.add).then_inc(*oh_ready.up())
                b = take("rank")
                bt, totals = b[:, 0:TT * NE].rearrange("p (t n) -> p t n", t=TT), b[:, TT * NE:(TT + 1) * NE]
                link(V.tensor_scalar(cnt[:, 0, :], totals, -1.0, 0.0, ALU.add, ALU.max))
                link(V.tensor_copy(blocks_i[:, :], cnt[:, 0, :]))
                link(V.tensor_scalar(blocks_i[:, :], blocks_i[:, :], 5, None, ALU.arith_shift_right))
                link(V.tensor_copy(cnt[:, 1, :], blocks_i[:, :]))
                link(V.tensor_tensor_scan(cnt[:, 2, :], cnt[:, 1, :], C("zero"), 0.0, ALU.add, ALU.add))
                link(V.tensor_tensor(cnt[:, 3, :], cnt[:, 2, :], cnt[:, 1, :], ALU.subtract))
                link(V.tensor_scalar(cnt[:, 3, :], cnt[:, 3, :], float(CAP), float(NE * CAP - CAP), ALU.mult, ALU.add))
                link(V.tensor_tensor(cnt[:, 4, :], cnt[:, 3, :], C("slot0"), ALU.subtract))

                def b64(v):
                    return v.unsqueeze(1).to_broadcast((P, TT, NE))
                link(V.scalar_tensor_tensor(sv, bt, float(CAP), b64(cnt[:, 4, :]), ALU.is_ge, ALU.mult))
                V.tensor_tensor(pos0, bt, b64(C("slot0")), ALU.add).then_inc(*emptying("rank"))
                dve.wait_ge(*empty(JOB["rank"]))
                link(V.tensor_tensor(sv, sv, pos0, ALU.add))
                sel = rt[:, 0:512].rearrange("p (k c) -> p k c", k=2)
                link(V.tensor_tensor(sel, OH2.rearrange("p k t n -> p k (t n)"),
                                     sv.rearrange("p t n -> p (t n)").unsqueeze(1).to_broadcast((P, 2, TT * NE)), ALU.mult))
                sl = slf.rearrange("p k t -> p (k t)")
                link(V.reduce_sum(sl, rt[:, 0:512].rearrange("p (c n) -> p c n", n=NE), AX.X))
                link(V.tensor_tensor(oh[0], lane, slots_of(0), ALU.is_equal))
                link(V.tensor_tensor(oh_b, lane, slots_of(1), ALU.is_equal))
                V.tensor_tensor(oh[0], oh[0], oh_b, ALU.add).then_inc(main.oh[0], 1)
                link(V.tensor_copy(sloti[:, :, :].rearrange("p k t -> p (k t)"), sl))
                link(V.tensor_scalar(slf[:, :, :], slf[:, :, :], -float(P), None, ALU.add))
                upto_block = cnt[0:32, 3, :]
                link(V.tensor_scalar(upto_block, cnt[0:32, 2, :], C("row")[0:32], None, ALU.is_le))
                link(V.reduce_sum(block_col[:, 0:1], upto_block, AX.X))
                link(V.tensor_scalar(block_col[:, 0:1], block_col[:, 0:1], float(NE - 1), None, ALU.min))
                link(V.transpose(block_row[:, :], block_col[:, :]))
                link(V.tensor_copy(meta[:, 0:32], block_row[0:1, :]))
                link(V.tensor_scalar(cnt[0:1, 0, 0:SG], C("fours")[0:1], cnt[0:1, 2, NE - 1:NE], None, ALU.is_lt))
                link(V.reduce_sum(groups_f[:, :], cnt[0:1, 0, 0:SG], AX.X))
                V.tensor_copy(meta[:, 32:33], groups_f[:, :]).then_inc(*meta_ready.up())
                with dve.Fori(0, IT) as i:
                    for b in range(2):
                        group(main, b, i, i * 2 + b)
                n = spill_groups(dve)
                with dve.If(n > 0):
                    stored_all(dve)
                    dve.wait_ge(main.oh_step, EG * 3 + 3)
                    dve.wait_ge(main.oh[0], IT + 1)
                    V.sem_inc(spill.oh[0], 1)
                    with dve.Fori(0, n) as g:
                        group(spill, 0, g, g)
                with dve.Else():
                    pass
                for t in range(TT):
                    dve.wait_ge(y_scaled.sem, y_scaled.at(t + 1))
                    link(V.scalar_tensor_tensor(X[:, t, :], X[:, t, :], ALPHA, y_rows[t][0], ALU.mult, ALU.add))
                    link(V.scalar_tensor_tensor(X[:, t, :], y_rows[t][1], wts[:, 1, t:t + 1], X[:, t, :], ALU.mult, ALU.add))
                    statistics(t)
                    if t:
                        gain(t - 1, TT, 64).then_inc(*ln_scaled.up())
                link(gain(TT - 1, TT, 64))
                link(offset(TT - 1))
                end_layer(dve, l)

        @block.gpsimd
        def _(pool):
            nc.gpsimd.memset(R1[:, 3 * D:4 * D], 0.0).then_inc(small_set, 1)
            pool.wait_ge(small_set, 5)
            pool.wait_ge(*full(("a", 0)))
            for g in range(EG, G_ALL):
                pool.dma_start(y_dram[g * P:(g + 1) * P, :], R1[:, 3 * D:4 * D]).then_inc(y_zeroed, 16)

            with pool.Fori(0, L) as l:
                nc.gpsimd.memset(v1[:, :, :, DH:].rearrange("p t h o -> p (t h) o"), 1.0).then_inc(*v1_ones.up())
                for h in range(MH):
                    for s in range(TT):
                        pool.wait_ge(ptm_written.sem, ptm_written.at(h * TT + s + 1))
                        a = PTm[h % 2][:, pt_at[s]:pt_at[s] + P]
                        nc.gpsimd.affine_select(out=a, in_=a, compare_op=ALU.is_ge, fill=0.0, base=0, pattern=[[1, P]],
                                                channel_multiplier=-1).then_inc(*ptm_ready.up())
                pool.wait_ge(h_ready.sem, h_ready.at(MH))
                pool.wait_ge(*empty(JOB["kr"]))
                nc.gpsimd.tensor_copy(kT[NOPE:QK, :, :], krT[NOPE:QK, :].unsqueeze(1).to_broadcast((ROPE, H, S))).then_inc(*kr_copied.up())
                n = spill_groups(pool)
                stored_all(pool, n)
                for t in range(TT):
                    for k in range(2):
                        pool.indirect_dma_start(y_rows[t][k], None, y_dram, bass.IndirectOffsetOnAxis(ap=sloti[:, k, t:t + 1], axis=0)).then_inc(y_in[t], 16)
                for t in range(TT - 1):
                    pool.wait_ge(ln_scaled.sem, ln_scaled.at(t + 1))
                    last = nc.gpsimd.tensor_tensor(X[:, t, :], X[:, t, :], lnB, ALU.add)
                end_layer(pool, l)

        steps_counted = dstep.n, astep.n
        assert steps_counted == (DVE_STEPS, ACT_STEPS), steps_counted
        for e in "AD":
            assert emptied[e].n == n_of[e]
        assert bank_full.n == len(JOBS)


_INS = ["x", "positions", "w_in", "conv_w", "conv_b", "gate_b", "q_a_g", "kv_a_g", "w_qb", "w_kvb", "out_g", "w_out",
        "ln1_g", "ln1_b", "w_rg", "w_re", "w_gate", "w_up", "w_down", "ln2_g", "ln2_b"]


def kernel(**inputs):
    import numpy as _np
    import concourse.bacc as _bacc
    from concourse import mybir as _mybir
    from concourse.bass_utils import run_bass_kernel_spmd as _run

    nc = _bacc.Bacc("TRN2", target_bir_lowering=False, num_devices=1)
    arrays, args = {}, {}
    for name in _INS:
        a = _np.ascontiguousarray(inputs[name])
        arrays[f"in_{name}"] = a
        args[name] = nc.dram_tensor(f"in_{name}", a.shape, _mybir.dt.from_np(a.dtype), kind="ExternalInput").ap()
    arrays["in_constants"] = CONST
    const = nc.dram_tensor("in_constants", CONST.shape, _mybir.dt.float32, kind="ExternalInput").ap()
    out = nc.dram_tensor("out_0", (1, S, D), _mybir.dt.float32, kind="ExternalOutput").ap()
    hybrid_kernel(nc, args, const, out)
    r = _run(nc, [arrays], core_ids=[0])
    return r.results[0]["out_0"]
```

```python
import numpy as np
import concourse.bass as bass
from concourse import mybir
from contextlib import ExitStack

D, S, L = 1024, 512, 2
H, NOPE, ROPE, VD = 8, 64, 32, 64
QK = NOPE + ROPE
QR, KVR = 256, 128
MH, DH = 4, 128
DM = MH * DH
CW = 4
NG, EPG, NE, DE = 8, 8, 64, 256
P = 128
TT = S // P
KC = D // P
ALPHA = (2 * L) ** 0.25
LN_EPS, RMS_EPS = 1e-5, 1e-6
DIN = QR + KVR + ROPE + 4 * DM + 2 * MH
C_CQ, C_Q = 0, QR + KVR + ROPE
C_K, C_V, C_O = C_Q + DM, C_Q + 2 * DM, C_Q + 3 * DM
NA = C_Q
NC2 = (DM + 2 * MH) // 2
CAP = 32
GRP = P // CAP
EG = NE // GRP
SG = 8
SLOT_WORDS = 6144
BIG = 1e30

def constants():
    cols, at = [], {}

    def put(name, a):
        at[name] = (sum(c.shape[1] for c in cols), a.shape[1])
        cols.append(np.broadcast_to(a, (P, a.shape[1])).astype(np.float32))

    i = np.arange(P)
    put("ident", np.eye(P))
    put("upto", (i[:, None] <= i[None, :]) * 1.0)
    put("before", (i[:, None] < i[None, :]) * 1.0)
    put("ones", np.ones((1, P)))
    put("future", np.concatenate([np.zeros((P, S - P)), np.where(i[None, :] > i[:, None], -BIG, 0.0)], 1))
    put("lane", i[None, :] * 1.0)
    put("pick", (i[:, None] == np.arange(MH * P)[None, :] // P) * 1.0)
    put("down8", 8.0 - np.arange(8)[None, :])
    half = ROPE // 2
    put("freq", (np.float32(10000.0) ** (-np.arange(half, dtype=np.float32) / np.float32(half)))[None, :])
    put("slot0", CAP * np.arange(NE)[None, :] * 1.0)
    put("fours", 4 * np.arange(SG)[None, :] * 1.0)
    put("row", i[:, None] * 1.0)
    put("zero", np.zeros((1, NE)))
    return np.ascontiguousarray(np.concatenate(cols, 1)), at


CONST, CAT = constants()

DVE_STEPS, ACT_STEPS = 174, 53

def jobs():
    out = [(("xt", t, h), "AD"[h]) for t in range(TT) for h in range(2)] + [("vec", "D")]
    out += [(("a", t), "D") for t in range(TT)]
    out += [(("o", t, h), "A") for t in range(TT) for h in range(2)]
    out += [(("q", 0), "D"), ("cum", "D"), (("q", 1), "D"), ("at", "D")]
    out += [(("cq", 0), "A"), (("cq", 1), "A"), ("ckv", "A"), ("kr", "A")]
    out += [(("q", 2), "D"), ("acol", "D"), (("q", 3), "D")]
    out += [(("k", c), "D") for c in range(MH)] + [(("v", t), "A") for t in range(TT)]

    def g(h):
        return [(("abc", h), "A")] + [(("st", h, b), "D") for b in range(TT)]

    def n(h):
        return [(("num", h, b), "D") for b in range(2)]

    def m(h):
        return [(("mt", h), "A")]
    kn = [(("kn", h), "A") for h in range(H)]
    mv = [(("mv", t), "A") for t in range(TT)]

    def q(t):
        return [(("qa", t), "A"), (("qb", t), "A")]

    def qt(t):
        return [(("qt", t, 0), "D"), (("qt", t, 1), "D")]
    for part in (g(0), g(1), n(0), g(2), m(0), n(1), g(3), m(1), n(2), kn[:2], n(3), kn[2:], m(2), mv,
                 q(0), q(1), m(3), qt(0), q(2), qt(1), q(3), qt(2), qt(3)):
        out += part
    for u in range(TT * H + 6):
        if u < TT * H:
            out.append((("s", u), "A"))
        if 3 <= u < TT * H + 3:
            out.append((("pt", u - 3), "D"))
        if u >= 15 and (u - 15) % H == 0:
            out.append((("mx", (u - 15) // H), "A"))
    for t in range(TT):
        out += [(("out", t, h), "D") for h in range(2)]
        if t == 0:
            out += [(("mx", TT - 1), "A")]
        if t:
            out += [(("xt2", t - 1, h), "AD"[h]) for h in range(2)]
    out += [(("xt2", TT - 1, h), "AD"[h]) for h in range(2)]
    out += [("logit", "D"), ("rank", "D")]
    return out


JOBS = jobs()
JOB = {name: j for j, (name, _) in enumerate(JOBS)}
NB = 6


def banks():
    bank, prev, user, turn = {}, {}, {}, 0
    for name, _ in JOBS:
        if name[0] == "num":
            b = NB + name[2]
        elif name == "logit":
            b = NB
        else:
            b, turn = turn % NB, turn + 1
        bank[name], prev[name], user[b] = b, user.get(b), name
    return bank, prev


BANK, BEFORE = banks()


class Signal:

    def __init__(self, sem, per_layer):
        self.sem, self.per, self.n = sem, per_layer, 0

    def up(self):
        self.n += 1
        return self.sem, 1

    def at(self, k):
        assert 0 < k <= self.per, (k, self.per)
        return k


def hybrid_kernel(nc, A, const, out):
    f32, i32 = mybir.dt.float32, mybir.dt.int32
    ALU, ACT, AX = mybir.AluOpType, mybir.ActivationFunctionType, mybir.AxisListType

    ctx = ExitStack()
    with ctx:
        def sb(name, shape, dt=f32):
            return ctx.enter_context(nc.sbuf_tensor(name, shape, dt))

        ring = [sb(f"ring{i}", [P, SLOT_WORDS]) for i in range(4)]
        X = sb("X", [P, TT, D])
        XT = sb("XT", [P, KC, S])
        R1 = sb("R1", [P, 8 * S])
        R2 = sb("R2", [P, 4224])
        R4 = sb("R4", [P, 4224])
        R3 = sb("R3", [P, 8 * S])
        cqT = R3[:, 0:2 * S].rearrange("p (c t) -> p c t", c=2)
        ckvT = R3[:, 2 * S:3 * S]
        krT = R3[:, 3 * S:4 * S]
        qtok = [ring[2][:, 4096 + H * QK * i:4096 + H * QK * (i + 1)].rearrange("p (h d) -> p h d", h=H) for i in range(2)]
        K = sb("K", [P, CONST.shape[1]])
        vecs = R4[0:7, 3200:3200 + D]
        vecT = sb("vecT", [P, KC, 7])
        gate_b = sb("gate_b", [P, 2 * MH])
        wr = sb("wr", [P, KC, NG + NE])
        cos = sb("cos", [P, TT, ROPE // 2])
        sin = sb("sin", [P, TT, ROPE // 2])
        ang = R4[:, 0:192].rearrange("p (a n) -> p a n", a=3)
        turns = sb("turns", [P, TT * ROPE // 2], i32)
        pos_i = sb("pos_i", [P, TT], i32)
        pos_f = sb("pos_f", [P, TT])
        biases = sb("biases", [P, 4])

        def C(name, n=None):
            a, w = CAT[name]
            return K[:, a:a + (n or w)]

        ident = C("ident")
        qkT = R1[:, :].rearrange("p (c t) -> p c t", c=8)
        V1W = TT * MH * (DH + 1)
        v1 = R2[:, 0:V1W].rearrange("p (t h e) -> p t h e", t=TT, h=MH)
        osig = R2[:, V1W:V1W + TT * DM].rearrange("p (t n) -> p t n", t=TT)
        cqkv = R4[:, 0:TT * NA].rearrange("p (t n) -> p t n", t=TT)
        convt = [R4[:, TT * NA + S * i:TT * NA + S * (i + 1)] for i in range(3)]
        PTW = P * (4 + 3 + 2 + 1)
        pt_at = [0, 512, 896, 1152]
        PTm = [R4[:, PTW * i:PTW * (i + 1)] for i in range(2)]
        Wm = [R4[:, 2 * PTW + S * i:2 * PTW + S * (i + 1)] for i in range(2)]
        gates = sb("gates", [P, TT, 2 * MH])
        gt = sb("gt", [P, 3, TT, MH])
        logf = sb("logf", [P, TT, MH])
        Bc = sb("Bc", [P, TT, MH])
        ac = sb("ac", [P, TT, MH])
        em = sb("em", [P, TT, MH])
        Arow = R4[0:MH, 3584:3584 + S]
        hm = [R3[:, (4 + i) * S:(5 + i) * S].rearrange("p (t e) -> p t e", t=TT) for i in range(2)]
        hsq = R3[:, 6 * S:7 * S]
        arow = hsq[0:MH, :]
        den = sb("den", [P, 4, TT])
        ss = sb("ss", [P, 2, TT])
        qT = R1[:, :].rearrange("p (h t) -> p h t", h=H)
        kT7 = ring[1][:, 2560:6144].rearrange("p (h t) -> p h t", h=H - 1)
        kT = [kT7[:, h, :] for h in range(H - 1)] + [ring[2][:, 5632:6144]]
        mv = ring[3][:, 4096:6144].rearrange("p (t n) -> p t n", t=TT)
        Pm = [R4[:, 2048 + S * i:2048 + S * (i + 1)] for i in range(3)]
        PT = [R4[:, 3584:3584 + S], krT[:, :], ckvT[:, :]]
        smx = sb("smx", [P, TT * H])
        ssum = sb("ssum", [P, TT * H])
        mnorm = sb("mnorm", [P, 4, H])
        mix = [h[:, :, :].rearrange("p t e -> p (t e)") for h in hm]
        rtmp = R3[:, 7 * S:8 * S].rearrange("p (i n) -> p i n", i=4)
        lnG, lnB = R1[:, 0:D], R1[:, D:2 * D]
        oh, woh, woh_b = (R1[:, 2 * D + S * i:2 * D + S * (i + 1)].rearrange("p (t n) -> p t n", t=TT) for i in range(3))
        xgT, ysb, WT = R2[:, 0:D], R2[:, D:2 * D], R2[:, 2 * D:2 * D + S]
        acc = [XT[:, :, :].rearrange("p k t -> p (k t)")[:, D * t:D * (t + 1)] for t in range(TT)]
        ahead_gu = R3[:, :]
        ahead_down = [[R4[:, 3200:3712], R4[:, 3712:4224]], [R1[:, 3 * D + S:4 * D], R2[:, 2 * D + S:3 * D]]]
        stats = sb("stats", [P, 2, 6])
        mvar = [sb(f"mvar{t}", [P, 2]) for t in range(TT)]
        nmean = sb("nmean", [P, 2, TT])
        rstd = sb("rstd", [P, TT])
        at = [0]

        def r4(*shape):
            n = int(np.prod(shape))
            v = R4[:, at[0]:at[0] + n]
            at[0] += n
            return v if len(shape) == 1 else v.rearrange("p (a b) -> p a b", a=shape[0]) if len(shape) == 2 else \
                v.rearrange("p (a b c) -> p a b c", a=shape[0], b=shape[1])
        lg = r4(TT, NG + NE)
        r8 = r4(8, TT, 8)
        r1 = r4(16, TT)
        OH2 = r4(2, TT, NE)
        OHS = r4(TT, NE)
        pos0 = r4(TT, NE)
        cnt = r4(5, NE)
        sv = r4(TT, NE)
        slf = r4(2, TT)
        esb, hsb = ([r4(64) for _ in range(2)] for _ in range(2))
        hT = [r4(64) for _ in range(GRP)]
        rt = R2[:, 3 * D:4 * D]
        blocks_i = sb("blocks_i", [P, NE], i32)
        block_col = sb("block_col", [32, 32])
        block_row = sb("block_row", [32, 32])
        groups_f = sb("groups_f", [1, 1])
        meta = sb("meta", [1, 35], i32)
        wts = sb("wts", [P, 2, TT])

        PB = ctx.enter_context(nc.psum_tensor("PB", [P, 8, 512], f32))

        cleared = []

        def kept(name):
            return ctx.enter_context(nc.semaphore(name))

        def sem(name):
            cleared.append(kept(name))
            return cleared[-1]

        def sig(name, per):
            return Signal(sem(name), per)

        once = {n: kept(n) for n in (
            "consts_in", "x_in0", "x_in1", "x_in2", "x_in3", "pos_in", "rope_step", "rope_ready", "small_set", "vecs_in", "gate_b_in",
            "wr_in", "w_a", "w_qkvb", "w_v", "w_o", "out_stored", "arrived", "layer_open", "waited")}
        n_of = {e: sum(1 for _, x in JOBS if x == e) for e in "AD"}
        bank_full = sig("bank_full", len(JOBS))
        emptied = {"A": sig("emptied_by_act", n_of["A"]), "D": sig("emptied_by_dve", n_of["D"])}

        def bank(name):
            return PB[:, BANK[name], :]

        def full(name):
            return bank_full.sem, bank_full.at(JOB[name] + 1)

        def empty(j):
            e = JOBS[j][1]
            return emptied[e].sem, emptied[e].at(sum(1 for _, x in JOBS[:j + 1] if x == e))

        def emptying(name):
            e = JOBS[JOB[name]][1]
            mine = [n for n, x in JOBS if x == e]
            assert mine[emptied[e].n] == name, (name, mine[emptied[e].n])
            return emptied[e].up()

        consts_in, pos_in = once["consts_in"], once["pos_in"]
        x_in = [once[f"x_in{t}"] for t in range(TT)]
        rope_step, rope_ready = once["rope_step"], once["rope_ready"]
        small_set = once["small_set"]
        vecs_in, gate_b_in, wr_in, ln_in = once["vecs_in"], once["gate_b_in"], once["wr_in"], sem("ln_in")
        w_a, w_q, w_v, w_o = (once[f"w_{n}"] for n in ("a", "qkvb", "v", "o"))
        w_qm, w_k, w_out = (sem(f"w_{n}") for n in ("q", "k", "out"))
        dstep = sig("dve_step", DVE_STEPS)
        astep = sig("act_step", ACT_STEPS)
        cq_sq = sig("cq_squares", 1)
        cq_ready = sig("cq_ready", 2)
        gates_in = sig("gates_in", 1)
        gate_neg = sig("gate_neg", 1)
        gate_ln = sig("gate_ln", 1)
        logf_ready = sig("logf_ready", 1)
        ac_ready = sig("ac_ready", 1)
        arow_ready = sig("arow_ready", 1)
        m_ready = sig("m_ready", 1)
        em_ready = sig("em_ready", 1)
        conv_ready = sig("conv_ready", 8)
        silu_exp = sig("silu_exp", 8)
        qk_ready = sig("qk_ready", 8)
        v1_ones = sig("v1_ones", 1)
        w_ready = sig("w_ready", MH * TT)
        ptm_written = sig("ptm_written", MH * TT)
        ptm_ready = sig("ptm_ready", MH * TT)
        h_sq = sig("h_sumsq", MH)
        h_rs = sig("h_rstd", MH)
        h_ready = sig("h_ready", MH)
        kr_copied = sig("kr_copied", 2)
        q_turned = sig("q_turned", TT)
        mx_ready = sig("mx_ready", TT * H)
        p_ready = sig("p_ready", TT * H)
        o_full = sig("o_full", TT)
        o_read = sig("o_read", TT)
        o_sq = sig("o_sumsq", TT)
        o_rs = sig("o_rstd", TT)
        mix_ready = sig("mix_ready", TT)
        ln_var = sig("ln_var", 2 * TT)
        ln_rs = sig("ln_rstd", 2 * TT)
        ln_scaled = sig("ln_scaled", TT // 2)
        x_ready = sig("x_ready", TT)
        exp_in, exp_out = sig("exp_in", 2), sig("exp_out", 2)
        oh_ready = sig("oh_ready", 1)
        conv_first = sig("conv_first", 8)
        ln_norm = sig("ln_normalised", 2 * TT)
        meta_ready = sig("meta_ready", 1)
        acc_ready = sig("acc_ready", 1)
        out_stored, arrived, layer_open, waited = (once[n] for n in ("out_stored", "arrived", "layer_open", "waited"))

        ahead_in = sem("ahead_in")

        class Path:

            def __init__(self, name):
                self.w_in = [sem(f"{name}_w_in{q}") for q in range(GRP)]
                self.d_in = sem(f"{name}_d_in")
                self.oh = sem(f"{name}_oh")
                self.oh_step = sem(f"{name}_oh_step")
                self.xg_T = sem(f"{name}_xg_T")
                self.xgT_a, self.xgT_d = sem(f"{name}_xgT_a"), sem(f"{name}_xgT_d")
                self.wT_full, self.wT = sem(f"{name}_wT_full"), sem(f"{name}_wT")
                self.gu = [sem(f"{name}_gu{i}") for i in range(2)]
                self.ex = [sem(f"{name}_ex{i}") for i in range(2)]
                self.st = [sem(f"{name}_st{i}") for i in range(2)]
                self.hT = sem(f"{name}_hT")
                self.down_half, self.down = sem(f"{name}_down_half"), sem(f"{name}_down")
                self.y = [sem(f"{name}_y{i}") for i in range(2)]
                self.sum = [sem(f"{name}_sum{i}") for i in range(2)]
                self.added = [sem(f"{name}_added{i}") for i in range(2)]
                self.ahead = [(s, 1) for s in [self.down, self.xgT_a, self.xgT_d, self.wT_full] + self.st + self.y + self.added] \
                    + [(s, 2) for s in self.gu] + [(self.oh_step, 3)]

        main, spill = Path("main"), Path("spill")
        moe_step = {False: sem("moe_step"), True: sem("spill_step")}

        def turn_wait(eng, semaphore, value):
            eng.wait_ge(semaphore, value)
            eng.sem_inc(waited, 1)

        def experts_done(eng, spilled=None):
            for i in range(2):
                eng.wait_ge(main.added[i], EG * TT + 1)
                if spilled is not None:
                    turn_wait(eng, spill.added[i], spilled * TT + 1)

        def spill_groups(eng):
            eng.wait_ge(meta_ready.sem, meta_ready.at(1))
            return eng.value_load(meta[0:1, 32:33], min_val=0, max_val=SG)

        def end_layer(eng, l):
            eng.drain().then_inc(arrived, 1)
            turn_wait(eng, layer_open, l + 1)

        block = ctx.enter_context(nc.Block())

        @block.sync
        def _(sp):
            with nc.allow_non_contiguous_dma("512 positions"):
                sp.dma_start(pos_i[:, :], A["positions"][0].rearrange("(t p) -> p t", p=P)).then_inc(pos_in, 16)
            sp.dma_start(K[:, :], const).then_inc(consts_in, 16)
            for t in range(TT):
                sp.dma_start(X[:, t, :], A["x"][0, t * P:(t + 1) * P, :]).then_inc(x_in[t], 16)

            def gate_up(path, q, l, e):
                r = ring[q]
                sp.dma_start(r[:, 0:2048], A["w_gate"][l, e].rearrange("(p k) f -> p (k f)", k=KC)).then_inc(path.w_in[q], 16)
                sp.dma_start(r[:, 2048:4096], A["w_up"][l, e].rearrange("(p k) f -> p (k f)", k=KC)).then_inc(path.w_in[q], 16)

            def down_matrix(path, q, l, e):
                sp.dma_start(ring[q][:, 4096:6144].rearrange("p (c n) -> p c n", c=2),
                             A["w_down"][l, e].rearrange("(c p) n -> p c n", p=P)).then_inc(path.d_in, 16)

            def expert(path, q, l, e):
                gate_up(path, q, l, e)
                down_matrix(path, q, l, e)

            def cols(l, slot, a, b, s):
                w_in = A["w_in"][l].rearrange("(p k) n -> p k n", k=KC)
                sp.dma_start(ring[slot][:, 0:KC * (b - a)].rearrange("p (k n) -> p k n", k=KC), w_in[:, :, a:b]).then_inc(s, 16)

            def row(t, l):
                return t[l:l + 1] if isinstance(l, int) else t[bass.ds(l, 1)]

            def first_weights(l):
                sp.dma_start(vecs[0:4, :], A["conv_w"][l]).then_inc(vecs_in, 16)
                sp.dma_start(vecs[4:5, :], row(A["conv_b"], l)).then_inc(vecs_in, 16)
                sp.dma_start(vecs[5:6, :], row(A["out_g"], l)).then_inc(vecs_in, 16)
                sp.dma_start(vecs[6:7, 0:QR], row(A["q_a_g"], l)).then_inc(vecs_in, 16)
                sp.dma_start(vecs[6:7, QR:QR + KVR], row(A["kv_a_g"], l)).then_inc(vecs_in, 16)
                cols(l, 0, 0, NA, w_a)
                cols(l, 2, C_O, DIN, w_o)
                sp.dma_start(gate_b[:, :], row(A["gate_b"], l).to_broadcast((P, 2 * MH))).then_inc(gate_b_in, 16)
                cols(l, 3, C_V, C_O, w_v)
                sp.dma_start(ring[1][:, 0:1536].rearrange("p (c n) -> p c n", c=2),
                             A["w_qb"][l].rearrange("(c p) n -> p c n", p=P)).then_inc(w_q, 16)
                sp.dma_start(ring[1][:, 1536:2560], A["w_kvb"][l]).then_inc(w_q, 16)
                sp.dma_start(wr[:, :, 0:NG], A["w_rg"][l].rearrange("(p k) n -> p k n", k=KC)).then_inc(wr_in, 16)
                sp.dma_start(wr[:, :, NG:], A["w_re"][l].rearrange("(p k) n -> p k n", k=KC)).then_inc(wr_in, 16)

            def set_ahead():
                for path in (main, spill):
                    for s, n in path.ahead:
                        sp.sem_inc(s, n)

            first_weights(0)
            set_ahead()
            with sp.Fori(0, L) as l:
                sp.wait_ge(*full(("a", TT - 1)))
                cols(l, 0, C_Q, C_K, w_qm)
                sp.wait_ge(*full(("o", TT - 1, 1)))
                cols(l, 2, C_K, C_V, w_k)
                sp.wait_ge(*full(("v", TT - 1)))
                w_o3 = A["w_out"][l].rearrange("(k p) n -> p k n", p=P)
                sp.dma_start(ring[3][:, 0:4096].rearrange("p (k n) -> p k n", k=KC), w_o3[:, :, 0:512]).then_inc(w_out, 16)
                sp.wait_ge(*full(("k", MH - 1)))
                sp.dma_start(ring[2][:, 0:4096].rearrange("p (k n) -> p k n", k=KC), w_o3[:, :, 512:D]).then_inc(w_out, 16)
                expert(main, 0, l, 0)
                sp.wait_ge(*full(("s", TT * H - 1)))
                sp.dma_start(lnG, A["ln1_g"][bass.ds(l, 1)].to_broadcast((P, D))).then_inc(ln_in, 16)
                sp.dma_start(lnB, A["ln1_b"][bass.ds(l, 1)].to_broadcast((P, D))).then_inc(ln_in, 16)
                expert(main, 1, l, 1)
                sp.wait_ge(*full(("mx", TT - 1)))
                for i, name in enumerate(("w_gate", "w_up")):
                    sp.dma_start(ahead_gu[:, 2048 * i:2048 * (i + 1)], A[name][l, NE - 1].rearrange("(p k) f -> p (k f)", k=KC)).then_inc(ahead_in, 16)
                for c in range(2):
                    for half in range(2):
                        sp.dma_start(ahead_down[c][half], A["w_down"][l, NE - 1, c * P:(c + 1) * P, 512 * half:512 * (half + 1)]).then_inc(ahead_in, 16)
                sp.wait_ge(*full(("out", TT - 1, 1)))
                expert(main, 2, l, 2)
                expert(main, 3, l, 3)
                sp.wait_ge(x_ready.sem, x_ready.at(TT))
                sp.dma_start(lnG, A["ln2_g"][bass.ds(l, 1)].to_broadcast((P, D))).then_inc(ln_in, 16)
                sp.dma_start(lnB, A["ln2_b"][bass.ds(l, 1)].to_broadcast((P, D))).then_inc(ln_in, 16)
                def load_group(g, experts):
                    for q in range(experts):
                        turn_wait(sp, main.gu[q % 2], g * 2 + q // 2 + 1)
                        gate_up(main, q, l, g * GRP + q)
                    turn_wait(sp, main.down, g + 1)
                    for q in range(experts):
                        down_matrix(main, q, l, g * GRP + q)
                with sp.Fori(1, EG - 1) as g:
                    load_group(g, GRP)
                load_group(EG - 1, GRP - 1)
                n = spill_groups(sp)
                with sp.If(n > 0):
                    blocks = sp.value_load(meta[0:1, 33:34], min_val=1, max_val=SG * GRP)
                    for i in range(2):
                        sp.wait_ge(main.gu[i], EG * 2 + 2)
                    with sp.Fori(0, n) as g:
                        es = [sp.value_load(meta[0:1, bass.ds(g * GRP + q, 1)], min_val=0, max_val=NE - 1) for q in range(GRP)]
                        for q in range(GRP):
                            turn_wait(sp, spill.gu[q % 2], g * 2 + q // 2 + 1)
                            with sp.If(g * GRP + q < blocks):
                                gate_up(spill, q, l, es[q])
                            with sp.Else():
                                sp.sem_inc(spill.w_in[q], 32)
                        sp.wait_ge(main.down, EG + 1)
                        turn_wait(sp, spill.down, g + 1)
                        for q in range(GRP):
                            with sp.If(g * GRP + q < blocks):
                                down_matrix(spill, q, l, es[q])
                            with sp.Else():
                                sp.sem_inc(spill.d_in, 16)
                with sp.Else():
                    pass
                sp.wait_ge(main.down, EG + 1)
                turn_wait(sp, spill.down, n + 1)
                with sp.If(l < L - 1):
                    first_weights(L - 1)
                with sp.Else():
                    pass
                turn_wait(sp, arrived, 4 * l + 4)
                numbers = sorted(s.num for s in cleared)
                assert numbers == list(range(numbers[0], numbers[-1] + 1))
                sp.sem_clear(range(numbers[0], numbers[-1] + 1))
                set_ahead()
                sp.sem_inc(layer_open, 1)
            for t in range(TT):
                sp.dma_start(out[0, t * P:(t + 1) * P, :], X[:, t, :]).then_inc(out_stored, 16)
            sp.wait_ge(out_stored, 16 * TT)

        @block.tensor
        def _(pe):
            pe.wait_ge(consts_in, 16)

            def rows(path, m):
                turn_wait(pe, path.oh, m + 1)
                pe.wait_ge(path.xgT_a, m + 1)
                pe.wait_ge(path.xgT_d, m + 1)
                for k in range(KC):
                    for t in range(TT):
                        last = nc.tensor.matmul(PB[:, k // 4, (k % 4) * P:(k % 4 + 1) * P],
                                                X[:, t, :].rearrange("p (i k) -> p k i", k=KC)[:, k, :], oh[:, t, :],
                                                start=t == 0, stop=t == TT - 1)
                last.then_inc(path.xg_T, 1)

            def experts(path, m, more=False, last_group=False):
                pe.wait_ge(path.xgT_a, m + 2)
                pe.wait_ge(path.xgT_d, m + 2)
                for q in range(GRP):
                    outside = last_group and q == GRP - 1
                    if outside:
                        pe.wait_ge(ahead_in, 96)
                    else:
                        pe.wait_ge(path.w_in[q], m * 32 + 32)
                    pe.wait_ge(path.st[q % 2], m * 2 + q // 2 + 1)
                    w = (ahead_gu if outside else ring[q][:, 0:4096]).rearrange("p (g k c j f) -> p g k c j f", g=2, k=KC, c=2, j=4)
                    for k in range(KC):
                        for j in range(4):
                            last = nc.tensor.matmul(PB[32 * j:32 * j + 32, 2 + q % 2, 0:P], xgT[:, k * P + CAP * q:k * P + CAP * (q + 1)],
                                                    w[:, :, k, :, j, :], start=k == 0, stop=k == KC - 1,
                                                    tile_position=(0, 32 * j), skip_group_check=True)
                    last.then_inc(path.gu[q % 2], 1)
                    if q == 0:
                        pe.wait_ge(path.added[0], m * TT + 1)
                        for t in range(TT):
                            last = nc.tensor.transpose(PB[:, 6, t * P:(t + 1) * P], woh[:, t, :], ident)
                        last.then_inc(path.wT_full, 1)
                if more:
                    rows(path, m + 1)
                pe.wait_ge(path.d_in, m * 64 + (48 if last_group else 64))
                pe.wait_ge(path.hT, m * GRP + GRP)
                for half, signal in enumerate((path.down_half, path.down)):
                    pe.wait_ge(path.y[half], m + 1)
                    for c in range(2):
                        for q in range(GRP):
                            a = 4096 + c * D + half * 512
                            w = ahead_down[c][half] if last_group and q == GRP - 1 else ring[q][:, a:a + 512]
                            last = nc.tensor.matmul(PB[32 * q:32 * q + 32, 4 + half, :], hT[q][:, 32 * c:32 * c + 32], w,
                                                    start=c == 0, stop=c == 1, tile_position=(0, 32 * q), skip_group_check=True)
                    last.then_inc(signal, 1)
                pe.wait_ge(path.wT, m + 1)
                for t in range(TT):
                    for half in range(2):
                        if t == 0:
                            pe.wait_ge(path.y[half], m + 2)
                        pe.wait_ge(path.added[half], m * TT + t + 1)
                        nc.tensor.matmul(PB[:, 6 + half, :], WT[:, t * P:(t + 1) * P], ysb[:, 512 * half:512 * (half + 1)],
                                         start=True, stop=True).then_inc(path.sum[half], 1)

            with pe.Fori(0, L) as l:
                def room(name):
                    if BEFORE[name]:
                        pe.wait_ge(*empty(JOB[BEFORE[name]]))
                    return bank(name)

                def done(ins):
                    ins.then_inc(*bank_full.up())

                def transpose_x(kind, tiles):
                    for t in tiles:
                        if kind == "xt":
                            pe.wait_ge(x_in[t], 16)
                        for h in range(2):
                            b = room((kind, t, h))
                            xv = X[:, t, :].rearrange("p (i k) -> p k i", k=KC)
                            for k in range(4):
                                last = nc.tensor.transpose(b[:, k * P:(k + 1) * P], xv[:, 4 * h + k, :], ident)
                            done(last)
                transpose_x("xt", range(TT))
                turn_wait(pe, vecs_in, l * 80 + 80)
                b = room("vec")
                for k in range(KC):
                    r = 7 if k < 3 else 6
                    last = nc.tensor.transpose(b[:, 8 * k:8 * k + r], vecs[0:r, k * P:(k + 1) * P], K[0:r, 0:r])
                done(last)

                def xt_ready(kind, t):
                    pe.wait_ge(*empty(JOB[(kind, t, 0)]))
                    pe.wait_ge(*empty(JOB[(kind, t, 1)]))
                xt_ready("xt", TT - 1)

                def tokens(name, t, slot, width, a, n):
                    b = room(name)
                    w = ring[slot][:, 0:KC * width].rearrange("p (k n) -> p k n", k=KC)
                    for k in range(KC):
                        last = nc.tensor.matmul(b[:, 0:n], XT[:, k, t * P:(t + 1) * P], w[:, k, a:a + n],
                                                start=k == 0, stop=k == KC - 1)
                    done(last)
                turn_wait(pe, w_a, l * 16 + 16)
                for t in range(TT):
                    tokens(("a", t), t, 0, NA, 0, NA)
                turn_wait(pe, w_o, l * 16 + 16)
                for t in range(TT):
                    for h in range(2):
                        tokens(("o", t, h), t, 2, 2 * NC2, h * NC2, NC2)

                def channels(name, c, slot):
                    b = room(name)
                    w = ring[slot][:, 0:KC * DM].rearrange("p (k n) -> p k n", k=KC)
                    for k in range(KC):
                        last = nc.tensor.matmul(b, w[:, k, c * P:(c + 1) * P], XT[:, k, :], start=k == 0, stop=k == KC - 1)
                    done(last)
                pe.wait_ge(w_qm, 16)
                channels(("q", 0), 0, 0)
                b = room("cum")
                pe.wait_ge(logf_ready.sem, logf_ready.at(1))
                for t in range(TT):
                    for s in range(t + 1):
                        last = nc.tensor.matmul(b[:, MH * t:MH * (t + 1)], C("upto") if s == t else C("ones"), logf[:, s, :],
                                                start=s == 0, stop=s == t)
                done(last)
                channels(("q", 1), 1, 0)
                b = room("at")
                pe.wait_ge(ac_ready.sem, ac_ready.at(1))
                for t in range(TT):
                    last = nc.tensor.transpose(b[0:MH, t * P:(t + 1) * P], ac[:, t, :], ident)
                done(last)
                pe.wait_ge(cq_ready.sem, cq_ready.at(2))
                for name, a, n in ((("cq", 0), 0, P), (("cq", 1), P, P), ("ckv", QR, P), ("kr", QR + KVR, ROPE)):
                    b = room(name)
                    for t in range(TT):
                        last = nc.tensor.transpose(b[0:n, t * P:(t + 1) * P], cqkv[:, t, a:a + n], ident)
                    done(last)
                channels(("q", 2), 2, 0)
                b = room("acol")
                pe.wait_ge(arow_ready.sem, arow_ready.at(1))
                for t in range(TT):
                    last = nc.tensor.transpose(b[:, MH * t:MH * (t + 1)], Arow[:, t * P:(t + 1) * P], K[0:MH, 0:MH])
                done(last)
                channels(("q", 3), 3, 0)
                pe.wait_ge(w_k, 16)
                for c in range(MH):
                    channels(("k", c), c, 2)
                turn_wait(pe, w_v, l * 16 + 16)
                for t in range(TT):
                    tokens(("v", t), t, 3, DM, 0, DM)

                def scores(h):
                    b = room(("abc", h))
                    done(nc.tensor.matmul(b, C("pick")[0:MH, h * P:(h + 1) * P], Arow[:, :], start=True, stop=True))
                    pe.wait_ge(qk_ready.sem, qk_ready.at(MH + h + 1))
                    for s in range(TT):
                        b = room(("st", h, s))
                        done(nc.tensor.matmul(b[:, 0:S - s * P], qkT[:, MH + h, s * P:(s + 1) * P], qkT[:, h, s * P:S],
                                              start=True, stop=True))

                def numerators(h):
                    for half in range(2):
                        b = room(("num", h, half))
                        pe.wait_ge(ptm_ready.sem, ptm_ready.at(h * TT + 2 * half + 2))
                        for i in range(2):
                            t = 2 * half + i
                            for s in range(t + 1):
                                a = pt_at[s] + (t - s) * P
                                last = nc.tensor.matmul(b[:, i * (DH + 1):(i + 1) * (DH + 1)], PTm[h % 2][:, a:a + P], v1[:, s, h, :],
                                                        start=s == 0, stop=s == t)
                        done(last)

                def h_transposed(h):
                    b = room(("mt", h))
                    pe.wait_ge(h_ready.sem, h_ready.at(h + 1))
                    for t in range(TT):
                        last = nc.tensor.transpose(b[:, t * P:(t + 1) * P], hm[h % 2][:, t, :], ident)
                    done(last)
                scores(0)
                scores(1)
                pe.wait_ge(v1_ones.sem, v1_ones.at(1))
                pe.wait_ge(*empty(JOB[("v", TT - 1)]))
                numerators(0)
                scores(2)
                h_transposed(0)
                numerators(1)
                scores(3)
                h_transposed(1)
                numerators(2)

                turn_wait(pe, w_q, l * 32 + 32)
                wq = ring[1][:, 0:1536].rearrange("p (c n) -> p c n", c=2)
                wkv = ring[1][:, 1536:2560].rearrange("p (h n) -> p h n", h=H)

                def keys(heads):
                    for h in heads:
                        b = room(("kn", h))
                        done(nc.tensor.matmul(b[0:NOPE, :], wkv[:, h, 0:NOPE], ckvT[:, :], start=True, stop=True))
                keys(range(2))
                numerators(3)
                keys(range(2, H))
                h_transposed(2)
                for t in range(TT):
                    b = room(("mv", t))
                    done(nc.tensor.matmul(b, ckvT[:, t * P:(t + 1) * P], wkv[:, :, NOPE:], start=True, stop=True))

                def queries(t):
                    for n, name in enumerate(("qa", "qb")):
                        b = room((name, t))
                        for c in range(2):
                            last = nc.tensor.matmul(b[:, 0:384], cqT[:, c, t * P:(t + 1) * P], wq[:, c, 384 * n:384 * (n + 1)],
                                                    start=c == 0, stop=c == 1)
                        done(last)

                def queries_transposed(t):
                    pe.wait_ge(q_turned.sem, q_turned.at(t + 1))
                    for n in range(2):
                        b = room(("qt", t, n))
                        for i in range(4):
                            last = nc.tensor.transpose(b[0:QK, i * P:(i + 1) * P], qtok[t % 2][:, 4 * n + i, :], ident)
                        done(last)
                queries(0)
                queries(1)
                h_transposed(3)
                queries_transposed(0)
                queries(2)
                queries_transposed(1)
                queries(3)
                queries_transposed(2)
                queries_transposed(3)
                pe.wait_ge(*empty(JOB[("qt", TT - 1, 1)]))
                pe.wait_ge(*empty(JOB[("kn", H - 1)]))
                pe.wait_ge(*empty(JOB[("mv", TT - 1)]))
                pe.wait_ge(kr_copied.sem, kr_copied.at(2))

                def mix_transposed(t):
                    b = room(("mx", t))
                    pe.wait_ge(mix_ready.sem, mix_ready.at(t + 1))
                    for k in range(4):
                        last = nc.tensor.transpose(b[:, k * P:(k + 1) * P], mix[t % 2][:, k * P:(k + 1) * P], ident)
                    done(last)
                for u in range(TT * H + 6):
                    if u < TT * H:
                        t, h = divmod(u, H)
                        b = room(("s", u))
                        done(nc.tensor.matmul(b[:, 0:(t + 1) * P], qT[0:QK, h, t * P:(t + 1) * P], kT[h][0:QK, 0:(t + 1) * P],
                                              start=True, stop=True))
                    if 3 <= u < TT * H + 3:
                        t = (u - 3) // H
                        b = room(("pt", u - 3))
                        pe.wait_ge(p_ready.sem, p_ready.at(u - 2))
                        for s in range(t + 1):
                            last = nc.tensor.transpose(b[:, s * P:(s + 1) * P], Pm[u % 3][:, s * P:(s + 1) * P], ident)
                        done(last)
                    if 4 <= u < TT * H + 4:
                        t, h = divmod(u - 4, H)
                        if h == 0 and t >= 2:
                            pe.wait_ge(o_read.sem, o_read.at(t - 1))
                        pe.wait_ge(*empty(JOB[("pt", u - 4)]))
                        for s in range(t + 1):
                            last = nc.tensor.matmul(PB[:, 6 + t % 2, VD * h:VD * (h + 1)], PT[(u - 4) % 3][:, s * P:(s + 1) * P],
                                                    mv[:, s, VD * h:VD * (h + 1)], start=s == 0, stop=s == t)
                        if h == H - 1:
                            last.then_inc(*o_full.up())
                    if u >= 15 and (u - 15) % H == 0:
                        mix_transposed((u - 15) // H)

                pe.wait_ge(w_out, 32)
                pe.wait_ge(*empty(JOB[("mt", MH - 1)]))

                def out_projection(t):
                    pe.wait_ge(*empty(JOB[("mx", t)]))
                    for h in range(2):
                        b = room(("out", t, h))
                        w = ring[3 - h][:, 0:4096].rearrange("p (k n) -> p k n", k=KC)
                        for k in range(KC):
                            last = nc.tensor.matmul(b, XT[:, k, t * P:(t + 1) * P], w[:, k, :], start=k == 0, stop=k == KC - 1)
                        done(last)

                def router(t):
                    xt_ready("xt2", t)
                    for k in range(KC):
                        last = nc.tensor.matmul(bank("logit")[:, 72 * t:72 * (t + 1)], XT[:, k, t * P:(t + 1) * P], wr[:, k, :],
                                                start=k == 0, stop=k == KC - 1)
                    return last
                turn_wait(pe, wr_in, l * 32 + 32)
                for t in range(TT + 1):
                    if t < TT:
                        out_projection(t)
                    if t == 0:
                        mix_transposed(TT - 1)
                    if t >= 2:
                        router(t - 2)
                    if t:
                        pe.wait_ge(x_ready.sem, x_ready.at(t))
                        transpose_x("xt2", [t - 1])
                done(router(TT - 1))
                b = room("rank")
                pe.wait_ge(oh_ready.sem, oh_ready.at(1))

                def tiles_of(a, z):
                    return b[:, NE * a:NE * z].rearrange("p (t n) -> p t n", n=NE)
                nc.tensor.matmul(tiles_of(0, 1), C("before"), OHS[:, 0:1, :], start=True, stop=True, skip_group_check=True)
                for s in range(TT):
                    last = nc.tensor.matmul(tiles_of(s + 1, TT + 1), C("ones"), OHS[:, s, :].unsqueeze(1).to_broadcast((P, TT - s, NE)),
                                            start=s == 0, stop=s == TT - 1, skip_group_check=True)
                    if s == 0:
                        nc.tensor.matmul(tiles_of(1, TT), C("before"), OHS[:, 1:TT, :], start=False, stop=False, skip_group_check=True)
                done(last)
                rows(main, 0)
                with pe.Fori(0, EG - 1) as g:
                    experts(main, g, more=True)
                experts(main, EG - 1, last_group=True)
                n = spill_groups(pe)
                with pe.If(n > 0):
                    experts_done(pe)
                    rows(spill, 0)
                    first = pe.value_load(meta[0:1, 34:35], min_val=0, max_val=SG - 1)
                    with pe.If(first > 0):
                        with pe.Fori(0, first) as g:
                            experts(spill, g, more=True)
                    with pe.Else():
                        pass
                    experts(spill, first)
                with pe.Else():
                    pass
                end_layer(pe, l)

        @block.scalar
        def _(act):
            act.wait_ge(rope_ready, 1)
            nc.scalar.activation(sin[:, :, :].rearrange("p t f -> p (t f)"), ang[:, 0, :], ACT.Sin).then_inc(rope_ready, 1)
            nc.scalar.activation(cos[:, :, :].rearrange("p t f -> p (t f)"), ang[:, 1, :], ACT.Sin).then_inc(rope_ready, 1)
            act.wait_ge(small_set, 4)
            act.preload_act_table_set("natural_log_exp_and_others")

            def rows(path, m):
                act.wait_ge(path.xg_T, m + 1)
                nc.scalar.copy(xgT[:, 0:512], PB[:, 0, :]).then_inc(path.xgT_a, 1)

            def experts(path, m, more=False):
                for q in range(GRP):
                    act.wait_ge(path.gu[q % 2], m * 2 + q // 2 + 3)
                    act.wait_ge(path.st[q % 2], m * 2 + q // 2 + 1)
                    nc.scalar.activation(esb[q % 2][:, :], PB[:, 2 + q % 2, 0:64], ACT.Exp, scale=-1.0).then_inc(path.ex[q % 2], 1)
                    if q == 0:
                        act.wait_ge(path.wT_full, m + 2)
                        nc.scalar.copy(WT, PB[:, 6, :]).then_inc(path.wT, 1)
                if more:
                    rows(path, m + 1)
                act.wait_ge(path.down_half, m + 1)
                nc.scalar.copy(ysb[:, 0:512], PB[:, 4, :]).then_inc(path.y[0], 1)
                act.wait_ge(path.down, m + 2)
                nc.scalar.copy(ysb[:, 512:D], PB[:, 5, :]).then_inc(path.y[1], 1)

            with act.Fori(0, L) as l:
                def link(ins):
                    ins.then_inc(*astep.up())
                    act.wait_ge(astep.sem, astep.at(astep.n))

                def take(name):
                    act.wait_ge(*full(name))
                    return bank(name)

                def xt(kind, tiles):
                    for t in tiles:
                        b = take((kind, t, 0))
                        nc.scalar.copy(XT[:, 0:4, t * P:(t + 1) * P], b.rearrange("p (k i) -> p k i", k=4)).then_inc(*emptying((kind, t, 0)))
                xt("xt", range(TT))
                for t in range(TT):
                    for h in range(2):
                        b = take(("o", t, h))
                        n = NC2 if h == 0 else DM - NC2
                        e = nc.scalar.activation(osig[:, t, h * NC2:h * NC2 + n], b[:, 0:n], ACT.Exp, scale=-1.0)
                        if h:
                            e = nc.scalar.copy(gates[:, t, :], b[:, n:n + 2 * MH])
                        e.then_inc(*emptying(("o", t, h)))
                act.wait_ge(gate_neg.sem, gate_neg.at(1))
                link(nc.scalar.activation(gt[:, 1], gt[:, 0], ACT.Exp))
                nc.scalar.activation(gt[:, 2], gt[:, 1], ACT.Ln, bias=biases[:, 2:3]).then_inc(*gate_ln.up())
                act.wait_ge(*empty(JOB[("a", TT - 1)]))
                for t in range(TT):
                    link(nc.scalar.activation(hm[0][:, 0:2, :].rearrange("p t e -> p (t e)"), cqkv[:, t, 0:QR], ACT.Square, accum_out=ss[:, 0, t:t + 1]))
                    link(nc.scalar.activation(hm[0][:, 2, :], cqkv[:, t, QR:QR + KVR], ACT.Square, accum_out=ss[:, 1, t:t + 1]))
                link(nc.scalar.activation(ss[:, 0, :], ss[:, 0, :], ACT.Ln, bias=biases[:, 1:2], scale=1.0 / QR))
                link(nc.scalar.activation(ss[:, 1, :], ss[:, 1, :], ACT.Ln, bias=biases[:, 1:2], scale=1.0 / KVR))
                nc.scalar.activation(ss[:, :, :], ss[:, :, :], ACT.Exp, scale=-0.5).then_inc(*cq_sq.up())
                ov = osig[:, :, :]
                link(nc.scalar.activation(ov, ov, ACT.Ln, bias=biases[:, 2:3]))
                link(nc.scalar.activation(ov, ov, ACT.Exp, scale=-1.0))

                def conv_tap(c):
                    b = take(("q", c) if c < MH else ("k", c - MH))
                    if c >= 2:
                        act.wait_ge(qk_ready.sem, qk_ready.at(c - 1))
                    nc.scalar.activation(convt[c % 2], b, ACT.Identity, bias=vecT[:, c, 4:5], scale=vecT[:, c, 3:4]).then_inc(*conv_first.up())

                def silu_sigmoid(c):
                    act.wait_ge(conv_ready.sem, conv_ready.at(c + 1))
                    if c >= 1:
                        act.wait_ge(qk_ready.sem, qk_ready.at(c))
                    link(nc.scalar.activation(convt[2], convt[c % 2], ACT.Exp, scale=-1.0))
                    link(nc.scalar.activation(convt[2], convt[2], ACT.Ln, bias=biases[:, 2:3]))
                    nc.scalar.activation(convt[2], convt[2], ACT.Exp, scale=-1.0).then_inc(*silu_exp.up())
                conv_tap(0)
                conv_tap(1)
                silu_sigmoid(0)
                for c in range(2):
                    b = take(("cq", c))
                    nc.scalar.activation(cqT[:, c, :], b, ACT.Identity, scale=vecT[:, c, 6:7]).then_inc(*emptying(("cq", c)))
                b = take("ckv")
                nc.scalar.activation(ckvT[:, :], b, ACT.Identity, scale=vecT[:, 2, 6:7]).then_inc(*emptying("ckv"))
                b = take("kr")
                nc.scalar.copy(krT[NOPE:QK, :], b[0:ROPE, :]).then_inc(*emptying("kr"))
                for c in range(2, 8):
                    conv_tap(c)
                    silu_sigmoid(c - 1)
                    if c == 4:
                        act.wait_ge(m_ready.sem, m_ready.at(1))
                        nc.scalar.activation(em[:, :, :], gt[:, 0], ACT.Exp, scale=-1.0).then_inc(*em_ready.up())
                silu_sigmoid(7)
                for t in range(TT):
                    b = take(("v", t))
                    nc.scalar.copy(v1[:, t, :, 0:DH], b.rearrange("p (h e) -> p h e", h=MH)).then_inc(*emptying(("v", t)))

                def weights(h):
                    b = take(("abc", h))
                    for s in range(TT):
                        i = h * TT + s
                        if i >= 2:
                            act.wait_ge(ptm_written.sem, ptm_written.at(i - 1))
                        else:
                            act.wait_ge(qk_ready.sem, qk_ready.at(8))
                        w = nc.scalar.activation(Wm[i % 2][:, 0:S - s * P], b[:, s * P:S], ACT.Exp, bias=ac[:, s, h:h + 1], scale=-1.0)
                        if s == TT - 1:
                            w.then_inc(*emptying(("abc", h)))
                            act.wait_ge(*empty(JOB[("abc", h)]))
                            nc.scalar.sem_inc(w_ready.up()[0], 1)
                        else:
                            w.then_inc(*w_ready.up())

                def rsqrt(buf, n, eps, s_in, s_out, k):
                    act.wait_ge(s_in.sem, s_in.at(k))
                    link(nc.scalar.activation(buf, buf, ACT.Ln, bias=biases[:, eps:eps + 1], scale=1.0 / n))
                    nc.scalar.activation(buf, buf, ACT.Exp, scale=-0.5).then_inc(*s_out.up())

                def mix_m(h):
                    b = take(("mt", h))
                    nc.scalar.activation(XT[:, 4 + h, :], b, ACT.Identity, scale=vecT[:, 4 + h, 5:6]).then_inc(*emptying(("mt", h)))
                weights(0)
                weights(1)
                rsqrt(den[:, 3, :], DH, 1, h_sq, h_rs, 1)
                weights(2)
                mix_m(0)
                rsqrt(den[:, 3, :], DH, 1, h_sq, h_rs, 2)
                weights(3)
                mix_m(1)

                def keys(heads):
                    for h in heads:
                        b = take(("kn", h))
                        nc.scalar.copy(kT[h][0:NOPE, :], b[0:NOPE, :]).then_inc(*emptying(("kn", h)))
                keys(range(2))
                rsqrt(den[:, 3, :], DH, 1, h_sq, h_rs, 3)
                keys(range(2, H))
                rsqrt(den[:, 3, :], DH, 1, h_sq, h_rs, 4)
                mix_m(2)
                for t in range(TT):
                    b = take(("mv", t))
                    nc.scalar.copy(mv[:, t, :], b).then_inc(*emptying(("mv", t)))
                for t in range(TT):
                    if t == 2:
                        mix_m(3)
                    if t >= 2:
                        act.wait_ge(*full(("qt", t - 2, 1)))
                    for n, name in enumerate(("qa", "qb")):
                        b = take((name, t))
                        nc.scalar.copy(qtok[t % 2][:, 4 * n:4 * n + 4, :].rearrange("p h d -> p (h d)"), b[:, 0:384]).then_inc(*emptying((name, t)))

                def mix_a(t):
                    b = take(("mx", t))
                    for k in range(4):
                        e = nc.scalar.activation(XT[:, k, t * P:(t + 1) * P], b[:, k * P:(k + 1) * P], ACT.Identity, scale=vecT[:, k, 5:6])
                    e.then_inc(*emptying(("mx", t)))
                for u in range(TT * H):
                    t, h = divmod(u, H)
                    act.wait_ge(mx_ready.sem, mx_ready.at(u + 1))
                    if u >= 3:
                        act.wait_ge(*full(("pt", u - 3)))
                    n = (t + 1) * P
                    b = bank(("s", u))
                    e = nc.scalar.activation(Pm[u % 3][:, 0:n], b[:, 0:n], ACT.Exp, bias=smx[:, u:u + 1], scale=-1.0,
                                             accum_out=ssum[:, u:u + 1])
                    e.then_inc(*emptying(("s", u)))
                    act.wait_ge(*empty(JOB[("s", u)]))
                    nc.scalar.sem_inc(p_ready.up()[0], 1)
                    if h == 5 and t >= 1:
                        rsqrt(mnorm[:, 2 + (t - 1) % 2, :], VD, 1, o_sq, o_rs, t)
                    if u >= 15 and (u - 15) % H == 0:
                        mix_a((u - 15) // H)
                rsqrt(mnorm[:, 2 + (TT - 1) % 2, :], VD, 1, o_sq, o_rs, TT)
                mix_a(TT - 1)

                def normalise(t, k, x):
                    rsqrt(rstd[:, t:t + 1], 1, 0, ln_var, ln_rs, k + t + 1)
                    act.wait_ge(ln_rs.sem, ln_rs.at(k + t + 1))
                    link(nc.scalar.activation(nmean[:, 1, t:t + 1], rstd[:, t:t + 1], ACT.Identity, scale=nmean[:, 0, t:t + 1]))
                    nc.scalar.activation(X[:, t, :], x, ACT.Identity, bias=nmean[:, 1, t:t + 1], scale=rstd[:, t:t + 1]) \
                        .then_inc(*ln_norm.up())
                for t in range(TT):
                    if t:
                        xt("xt2", [t - 1])
                    normalise(t, 0, X[:, t, :])
                xt("xt2", [TT - 1])
                for k, (i, o) in enumerate(((r8[:, 1], r8[:, 2]), (r1[:, 6, :], r1[:, 7, :]))):
                    act.wait_ge(exp_in.sem, exp_in.at(k + 1))
                    nc.scalar.activation(o, i, ACT.Exp).then_inc(*exp_out.up())
                act.wait_ge(*full("logit"))
                for t in range(TT):
                    last = nc.scalar.activation(acc[t], X[:, t, :], ACT.Identity, scale=ALPHA)
                last.then_inc(*acc_ready.up())
                rows(main, 0)
                with act.Fori(0, EG - 1) as g:
                    experts(main, g, more=True)
                experts(main, EG - 1)
                n = spill_groups(act)
                with act.If(n > 0):
                    experts_done(act)
                    rows(spill, 0)
                    first = act.value_load(meta[0:1, 34:35], min_val=0, max_val=SG - 1)
                    with act.If(first > 0):
                        with act.Fori(0, first) as g:
                            experts(spill, g, more=True)
                    with act.Else():
                        pass
                    experts(spill, first)
                with act.Else():
                    pass
                for t in range(TT):
                    normalise(t, TT, acc[t])
                end_layer(act, l)

        @block.vector
        def _(dve):
            V = nc.vector
            V.memset(biases[:, 0:1], LN_EPS).then_inc(small_set, 1)
            V.memset(biases[:, 1:2], RMS_EPS).then_inc(small_set, 1)
            V.memset(biases[:, 2:3], 1.0).then_inc(small_set, 1)
            V.memset(block_col[:, :], 0.0).then_inc(small_set, 1)
            dve.wait_ge(consts_in, 16)
            dve.wait_ge(pos_in, 16)
            steps = [0]

            def rope(ins):
                steps[0] += 1
                ins.then_inc(rope_step, 1)
                dve.wait_ge(rope_step, steps[0])
            rope(V.tensor_copy(pos_f[:, :], pos_i[:, :]))
            HF = ROPE // 2
            for t in range(TT):
                rope(V.tensor_scalar(ang[:, 2, HF * t:HF * (t + 1)], C("freq"), pos_f[:, t:t + 1], None, ALU.mult))
            two_pi = 2 * np.pi
            c1 = float(np.float32(6.28125))
            c2 = float(np.float32(round((two_pi - c1) * 2 ** 19) / 2 ** 19))
            c3 = float(np.float32(two_pi - c1 - c2))
            for o, shift in ((0, 0.0), (1, 0.25)):
                a = ang[:, o, :]
                rope(V.tensor_scalar(a, ang[:, 2, :], 1.0 / two_pi, shift, ALU.mult, ALU.add))
                rope(V.tensor_copy(turns[:, :], a))
                rope(V.tensor_copy(pos_t := hsq[:, 0:TT * HF], turns[:, :]))
                rope(V.scalar_tensor_tensor(a, pos_t, -c1, ang[:, 2, :], ALU.mult, ALU.add))
                rope(V.scalar_tensor_tensor(a, pos_t, -c2, a, ALU.mult, ALU.add))
                rope(V.scalar_tensor_tensor(a, pos_t, -c3, a, ALU.mult, ALU.add))
                if o:
                    rope(V.tensor_scalar(a, a, float(np.pi / 2), None, ALU.add))
                over = hsq[:, 64:64 + TT * HF]
                for sign in (1.0, -1.0):
                    rope(V.tensor_scalar(over, a, sign, float(np.pi), ALU.mult, ALU.is_gt))
                    rope(V.scalar_tensor_tensor(a, over, -sign * two_pi, a, ALU.mult, ALU.add))
                last = V.tensor_scalar(a, a, float(np.float32(3.1415925)), -float(np.float32(3.1415925)), ALU.min, ALU.max)
                steps[0] += 1
                last.then_inc(rope_step, 1)
            dve.wait_ge(rope_step, steps[0])
            V.sem_inc(rope_ready, 1)
            dve.wait_ge(rope_ready, 3)
            dve.wait_ge(small_set, 4)

            def slots(path, m):
                dve.wait_ge(path.oh_step, m * 3 + 3)
                dve.wait_ge(path.wT_full, m + 1)
                for o, k in ((woh, 0), (woh_b, 1)):
                    for t in range(TT):
                        last = V.tensor_scalar(o[:, t, :], C("lane"), slf[:, k, t:t + 1], wts[:, k, t:t + 1], ALU.is_equal, ALU.mult)
                last.then_inc(path.oh_step, 1)
                dve.wait_ge(path.oh_step, m * 3 + 4)
                V.tensor_tensor(woh, woh, woh_b, ALU.add).then_inc(path.oh_step, 1)
                dve.wait_ge(path.oh_step, m * 3 + 5)
                V.tensor_scalar(oh, woh, 0.0, None, ALU.is_gt).then_inc(path.oh, 1)
                V.tensor_scalar(slf[:, :, :], slf[:, :, :], -float(P), None, ALU.add).then_inc(path.oh_step, 1)

            def rows(path, m):
                dve.wait_ge(path.xg_T, m + 1)
                V.tensor_copy(xgT[:, 512:D], PB[:, 1, :]).then_inc(path.xgT_d, 1)

            def experts(path, m, more=False):
                step = moe_step[path is spill]
                for q in range(GRP):
                    i, n = q % 2, m * 2 + q // 2
                    dve.wait_ge(path.ex[i], n + 1)
                    g2, u2 = PB[:, 2 + i, 0:64], PB[:, 2 + i, 64:P]
                    V.tensor_scalar(esb[i][:, :], esb[i][:, :], 1.0, None, ALU.add).then_inc(step, 1)
                    dve.wait_ge(step, m * 12 + q * 3 + 1)
                    V.reciprocal(esb[i][:, :], esb[i][:, :]).then_inc(step, 1)
                    dve.wait_ge(step, m * 12 + q * 3 + 2)
                    V.tensor_tensor(esb[i][:, :], g2, esb[i][:, :], ALU.mult).then_inc(step, 1)
                    dve.wait_ge(step, m * 12 + q * 3 + 3)
                    V.tensor_tensor(hsb[i][:, :], u2, esb[i][:, :], ALU.mult).then_inc(path.st[i], 1)
                    dve.wait_ge(path.st[i], n + 2)
                    dve.wait_ge(path.down, m + 1)
                    V.transpose(hT[q], hsb[i][:, :]).then_inc(path.hT, 1)
                    if q == 1 and more:
                        slots(path, m + 1)
                if more:
                    rows(path, m + 1)
                elif path is main:
                    dve.wait_ge(main.wT_full, EG + 1)
                    dve.wait_ge(main.oh_step, EG * 3 + 3)
                    slots(spill, 0)
                for t in range(TT):
                    for half in range(2):
                        dve.wait_ge(path.sum[half], m * TT + t + 1)
                        dve.wait_ge(path.added[half], m * TT + t + 1)
                        a = acc[t][:, 512 * half:512 * (half + 1)]
                        V.tensor_tensor(a, a, PB[:, 6 + half, :], ALU.add).then_inc(path.added[half], 1)

            with dve.Fori(0, L) as l:
                def link(ins):
                    ins.then_inc(*dstep.up())
                    dve.wait_ge(dstep.sem, dstep.at(dstep.n))

                def take(name):
                    dve.wait_ge(*full(name))
                    return bank(name)


                def xt(kind, tiles):
                    for t in tiles:
                        b = take((kind, t, 1))
                        V.tensor_copy(XT[:, 4:8, t * P:(t + 1) * P], b.rearrange("p (k i) -> p k i", k=4)).then_inc(*emptying((kind, t, 1)))
                xt("xt", range(TT))
                b = take("vec")
                bv = b[:, 0:8 * KC].rearrange("p (k r) -> p k r", k=KC)
                link(V.tensor_copy(vecT[:, :, 0:6], bv[:, :, 0:6]))
                V.tensor_copy(vecT[:, 0:3, 6:7], bv[:, 0:3, 6:7]).then_inc(*emptying("vec"))
                for t in range(TT):
                    b = take(("a", t))
                    V.tensor_copy(cqkv[:, t, :], b[:, 0:NA]).then_inc(*emptying(("a", t)))
                dve.wait_ge(*empty(JOB[("a", TT - 1)]))
                rt_ = [rtmp[:, i, 0:TT * HF].rearrange("p (t f) -> p t f", t=TT) for i in range(4)]
                k1, k2 = cqkv[:, :, QR + KVR:QR + KVR + HF], cqkv[:, :, QR + KVR + HF:NA]

                def turn(x1, x2, cs, sn, tmp, last_signal):
                    V.tensor_tensor(tmp[0], x1, cs, ALU.mult)
                    V.tensor_tensor(tmp[1], x2, sn, ALU.mult)
                    V.tensor_tensor(tmp[2], x2, cs, ALU.mult)
                    link(V.tensor_tensor(tmp[3], x1, sn, ALU.mult))
                    V.tensor_tensor(x1, tmp[0], tmp[1], ALU.subtract)
                    V.tensor_tensor(x2, tmp[2], tmp[3], ALU.add).then_inc(*last_signal.up())
                turn(k1, k2, cos[:, :, :], sin[:, :, :], rt_, cq_ready)
                dve.wait_ge(*empty(JOB[("o", TT - 1, 1)]))
                turn_wait(dve, gate_b_in, l * 16 + 16)
                link(V.tensor_tensor(gates[:, :, :], gates[:, :, :], gate_b[:, :].unsqueeze(1).to_broadcast((P, TT, 2 * MH)), ALU.add))
                gi, gf = gates[:, :, 0:MH], gates[:, :, MH:]
                link(V.tensor_scalar(gt[:, 1], gf, -1.0, None, ALU.mult))
                V.tensor_tensor(gt[:, 0], gt[:, 1], gf, ALU.min).then_inc(*gate_neg.up())
                dve.wait_ge(gate_ln.sem, gate_ln.at(1))
                V.scalar_tensor_tensor(logf[:, :, :], gf, 0.0, gt[:, 2], ALU.min, ALU.subtract).then_inc(*logf_ready.up())
                dve.wait_ge(cq_sq.sem, cq_sq.at(1))
                for t in range(TT):
                    V.tensor_scalar(cqkv[:, t, 0:QR], cqkv[:, t, 0:QR], ss[:, 0, t:t + 1], None, ALU.mult)
                    last = V.tensor_scalar(cqkv[:, t, QR:QR + KVR], cqkv[:, t, QR:QR + KVR], ss[:, 1, t:t + 1], None, ALU.mult)
                last.then_inc(*cq_ready.up())
                def cumulated():
                    b = take("cum")
                    link(V.tensor_copy(Bc[:, :, :], b[:, 0:TT * MH].rearrange("p (t h) -> p t h", t=TT)))
                    V.tensor_tensor(ac[:, :, :], gi, Bc[:, :, :], ALU.subtract).then_inc(*emptying("cum"))
                    dve.wait_ge(*empty(JOB["cum"]))
                    V.sem_inc(ac_ready.up()[0], 1)

                def conv(c):
                    name = ("q", c) if c < MH else ("k", c - MH)
                    b = take(name)
                    y = convt[c % 2]
                    dve.wait_ge(conv_first.sem, conv_first.at(c + 1))
                    for j in range(1, CW):
                        last = V.scalar_tensor_tensor(y[:, j:S], b[:, 0:S - j], vecT[:, c, 3 - j:4 - j], y[:, j:S], ALU.mult, ALU.add)
                        if j < CW - 1:
                            link(last)
                    last.then_inc(*emptying(name))
                    dve.wait_ge(*empty(JOB[name]))
                    V.sem_inc(conv_ready.up()[0], 1)

                def silu(c):
                    dve.wait_ge(silu_exp.sem, silu_exp.at(c + 1))
                    V.tensor_tensor(qkT[:, c, :], convt[c % 2], convt[2], ALU.mult).then_inc(*qk_ready.up())
                conv(0)
                cumulated()
                conv(1)
                b = take("at")
                link(V.tensor_copy(arow[:, :], b[0:MH, :]))
                V.tensor_tensor_scan(Arow[:, :], arow[:, :], arow[:, :], 0.0, ALU.max, ALU.max).then_inc(*emptying("at"))
                dve.wait_ge(*empty(JOB["at"]))
                V.sem_inc(arow_ready.up()[0], 1)
                silu(0)
                conv(2)
                silu(1)
                b = take("acol")
                V.tensor_tensor(gt[:, 0], b[:, 0:TT * MH].rearrange("p (t h) -> p t h", t=TT), Bc[:, :, :], ALU.add).then_inc(*emptying("acol"))
                dve.wait_ge(*empty(JOB["acol"]))
                V.sem_inc(m_ready.up()[0], 1)
                for c in range(3, 8):
                    conv(c)
                    silu(c - 1)
                silu(7)

                def weigh(h):
                    for s in range(TT):
                        b = take(("st", h, s))
                        dve.wait_ge(w_ready.sem, w_ready.at(h * TT + s + 1))
                        if h >= 2 and s == 0:
                            dve.wait_ge(*full(("num", h - 2, 1)))
                        n = S - s * P
                        V.scalar_tensor_tensor(PTm[h % 2][:, pt_at[s]:pt_at[s] + n], b[:, 0:n], DH ** -0.5, Wm[(h * TT + s) % 2][:, 0:n],
                                               ALU.mult, ALU.mult).then_inc(*emptying(("st", h, s)))
                        dve.wait_ge(*empty(JOB[("st", h, s)]))
                        V.sem_inc(ptm_written.up()[0], 1)

                def normalise(h):
                    d, o = den, hm[h % 2]
                    for i in range(2):
                        b = take(("num", h, i))
                        bv = b[:, 0:2 * (DH + 1)].rearrange("p (t e) -> p t e", t=2)
                        dv = d[:, 0, 2 * i:2 * i + 2].unsqueeze(2)
                        link(V.tensor_copy(dv, bv[:, :, DH:]))
                        link(V.tensor_scalar(d[:, 1, 2 * i:2 * i + 2], d[:, 0, 2 * i:2 * i + 2], -1.0, None, ALU.mult))
                        link(V.tensor_tensor(d[:, 0, 2 * i:2 * i + 2], d[:, 0, 2 * i:2 * i + 2], d[:, 1, 2 * i:2 * i + 2], ALU.max))
                        if i == 0 and h == 0:
                            dve.wait_ge(em_ready.sem, em_ready.at(1))
                        link(V.tensor_tensor(d[:, 0, 2 * i:2 * i + 2], d[:, 0, 2 * i:2 * i + 2], em[:, 2 * i:2 * i + 2, h], ALU.max))
                        link(V.reciprocal(d[:, 1, 2 * i:2 * i + 2], d[:, 0, 2 * i:2 * i + 2]))
                        if i == 0 and h >= 2:
                            dve.wait_ge(*full(("mt", h - 2)))
                        V.tensor_tensor(o[:, 2 * i:2 * i + 2, :], bv[:, :, 0:DH], d[:, 1, 2 * i:2 * i + 2].unsqueeze(2).to_broadcast((P, 2, DH)),
                                        ALU.mult).then_inc(*emptying(("num", h, i)))
                    dve.wait_ge(*empty(JOB[("num", h, 1)]))
                    hs = hsq[:, :].rearrange("p (t e) -> p t e", t=TT)
                    link(V.tensor_tensor(hs, o[:, :, :], o[:, :, :], ALU.mult))
                    V.reduce_sum(d[:, 3, :], hs, AX.X).then_inc(*h_sq.up())
                    dve.wait_ge(h_rs.sem, h_rs.at(h + 1))
                    link(V.tensor_tensor(o[:, :, :], o[:, :, :], d[:, 3, :].unsqueeze(2).to_broadcast((P, TT, DH)), ALU.mult))
                    V.tensor_tensor(o[:, :, :], o[:, :, :], osig[:, :, h * DH:(h + 1) * DH], ALU.mult).then_inc(*h_ready.up())
                weigh(0)
                weigh(1)
                normalise(0)
                weigh(2)
                normalise(1)
                weigh(3)
                normalise(2)
                normalise(3)
                cs8 = [cos[:, t, :].unsqueeze(1).to_broadcast((P, H, HF)) for t in range(TT)]
                sn8 = [sin[:, t, :].unsqueeze(1).to_broadcast((P, H, HF)) for t in range(TT)]
                rt8 = [rtmp[:, i, :].rearrange("p (h f) -> p h f", h=H) for i in range(4)]

                def turn_q(t):
                    dve.wait_ge(*empty(JOB[("qb", t)]))
                    if t:
                        dve.wait_ge(q_turned.sem, q_turned.at(t))
                    turn(qtok[t % 2][:, :, NOPE:NOPE + HF], qtok[t % 2][:, :, NOPE + HF:], cs8[t], sn8[t], rt8, q_turned)

                def put_q(t):
                    for n in range(2):
                        b = take(("qt", t, n))
                        V.tensor_copy(qT[0:QK, 4 * n:4 * n + 4, t * P:(t + 1) * P], b[0:QK, :].rearrange("p (h i) -> p h i", h=4)).then_inc(*emptying(("qt", t, n)))
                turn_q(0)
                turn_q(1)
                put_q(0)
                turn_q(2)
                put_q(1)
                turn_q(3)
                put_q(2)
                put_q(3)

                def softmax_max(u):
                    n = (u // H + 1) * P
                    b = take(("s", u))
                    V.tensor_tensor_reduce(out=b[:, 0:n], in0=b[:, 0:n], in1=C("future")[:, S - n:], scale=-QK ** -0.5, scalar=3e38,
                                           op0=ALU.add, op1=ALU.min, accum_out=smx[:, u:u + 1]).then_inc(*mx_ready.up())

                def put_pt(u):
                    b = take(("pt", u))
                    n = (u // H + 1) * P
                    V.tensor_copy(PT[u % 3][:, 0:n], b[:, 0:n]).then_inc(*emptying(("pt", u)))

                def head_norm(t, part):
                    o = mix[t % 2]
                    o3 = o[:, :].rearrange("p (h e) -> p h e", h=H)
                    r = mnorm[:, 0, :]
                    q = mnorm[:, 2 + t % 2, :]
                    if part == 0:
                        dve.wait_ge(o_full.sem, o_full.at(t + 1))
                        if t >= 2:
                            dve.wait_ge(*full(("mx", t - 2)))
                        link(V.reciprocal(r, ssum[:, t * H:(t + 1) * H]))
                        link(V.tensor_tensor(o3, PB[:, 6 + t % 2, :].rearrange("p (h e) -> p h e", h=H), r.unsqueeze(2).to_broadcast((P, H, VD)), ALU.mult))
                        V.sem_inc(o_read.up()[0], 1)
                        link(V.tensor_tensor(hsq[:, :], o[:, :], o[:, :], ALU.mult))
                        V.reduce_sum(q, hsq[:, :].rearrange("p (h e) -> p h e", h=H), AX.X).then_inc(*o_sq.up())
                    else:
                        dve.wait_ge(o_rs.sem, o_rs.at(t + 1))
                        V.tensor_tensor(o3, o3, q.unsqueeze(2).to_broadcast((P, H, VD)), ALU.mult).then_inc(*mix_ready.up())
                for u in range(TT * H + 6):
                    if u < TT * H:
                        softmax_max(u)
                    if 3 <= u < TT * H + 3:
                        put_pt(u - 3)
                    if u >= 12 and (u - 12) % H < 2:
                        head_norm((u - 12) // H, (u - 12) % H)

                def statistics(t, x):
                    link(V.bn_stats(stats[:, 0, :], x[:, 0:512]))
                    link(V.bn_stats(stats[:, 1, :], x[:, 512:D]))
                    link(V.bn_aggr(mvar[t][:, :], stats[:, :, :].rearrange("p a s -> p (a s)")))
                    link(V.tensor_scalar(nmean[:, 0, t:t + 1], mvar[t][:, 0:1], -1.0, None, ALU.mult))
                    V.tensor_copy(rstd[:, t:t + 1], mvar[t][:, 1:2]).then_inc(*ln_var.up())

                def gain(t, k, gain_waits):
                    dve.wait_ge(ln_norm.sem, ln_norm.at(k + t + 1))
                    dve.wait_ge(ln_in, gain_waits)
                    return V.tensor_tensor(X[:, t, :], X[:, t, :], lnG, ALU.mult)

                def offset(t):
                    return V.tensor_tensor(X[:, t, :], X[:, t, :], lnB, ALU.add)
                for t in range(TT):
                    for h in range(2):
                        b = take(("out", t, h))
                        V.scalar_tensor_tensor(X[:, t, 512 * h:512 * (h + 1)], X[:, t, 512 * h:512 * (h + 1)], ALPHA, b, ALU.mult, ALU.add) \
                            .then_inc(*emptying(("out", t, h)))
                    dve.wait_ge(*empty(JOB[("out", t, 1)]))
                    statistics(t, X[:, t, :])
                    if t:
                        xt("xt2", [t - 1])
                    link(gain(t, 0, 32))
                    offset(t).then_inc(*x_ready.up())
                xt("xt2", [TT - 1])

                b = take("logit")
                V.tensor_copy(lg[:, :, :], b[:, 0:TT * 72].rearrange("p (t n) -> p t n", t=TT)).then_inc(*emptying("logit"))
                dve.wait_ge(*empty(JOB["logit"]))
                d8 = C("down8").unsqueeze(1).to_broadcast((P, TT, 8))

                def b8(v):
                    return v.unsqueeze(2).to_broadcast((P, TT, 8))

                def first_max(scores, mx, shifted, tmp, best, onehot):
                    link(V.reduce_max(mx, scores, AX.X))
                    link(V.tensor_tensor(shifted, scores, b8(mx), ALU.subtract))
                    link(V.scalar_tensor_tensor(tmp, shifted, 0.0, d8, ALU.is_ge, ALU.mult))
                    link(V.reduce_max(best, tmp, AX.X))
                    link(V.tensor_tensor(onehot, d8, b8(best), ALU.is_equal))
                first_max(lg[:, :, 0:8], r1[:, 0], r8[:, 1], r8[:, 3], r1[:, 1], r8[:, 0])
                V.sem_inc(exp_in.up()[0], 1)
                dve.wait_ge(exp_out.sem, exp_out.at(1))
                link(V.reduce_sum(r1[:, 2], r8[:, 2], AX.X))
                link(V.reciprocal(r1[:, 3], r1[:, 2]))
                goh = r8[:, 0]
                prod = rt[:, 0:256].rearrange("p (t g e) -> p t g e", t=TT, g=8)
                link(V.tensor_tensor(prod, lg[:, :, 8:].rearrange("p t (g e) -> p t g e", g=8), goh.unsqueeze(3).to_broadcast((P, TT, 8, 8)), ALU.mult))
                link(V.reduce_sum(r8[:, 4], prod.rearrange("p t g e -> p t e g"), AX.X))
                first_max(r8[:, 4], r1[:, 4], r8[:, 5], r8[:, 3], r1[:, 1], r8[:, 6])
                link(V.scalar_tensor_tensor(r8[:, 5], r8[:, 6], -BIG, r8[:, 5], ALU.mult, ALU.add))
                first_max(r8[:, 5], r1[:, 6], r8[:, 4], r8[:, 3], r1[:, 1], r8[:, 7])
                V.sem_inc(exp_in.up()[0], 1)
                dve.wait_ge(exp_out.sem, exp_out.at(2))
                link(V.tensor_scalar(r1[:, 8], r1[:, 7], 1.0, None, ALU.add))
                link(V.reciprocal(r1[:, 9], r1[:, 8]))
                link(V.tensor_tensor(wts[:, 0], r1[:, 9], r1[:, 3], ALU.mult))
                link(V.tensor_tensor(wts[:, 1], wts[:, 0], r1[:, 7], ALU.mult))
                for k in range(2):
                    link(V.tensor_tensor(OH2[:, k].rearrange("p t (g e) -> p t g e", g=8), goh.unsqueeze(3).to_broadcast((P, TT, 8, 8)),
                                         r8[:, 6 + k].unsqueeze(2).to_broadcast((P, TT, 8, 8)), ALU.mult))
                V.tensor_tensor(OHS[:, :, :], OH2[:, 0], OH2[:, 1], ALU.add).then_inc(*oh_ready.up())
                b = take("rank")
                bt, totals = b[:, 0:TT * NE].rearrange("p (t n) -> p t n", t=TT), b[:, TT * NE:(TT + 1) * NE]
                link(V.tensor_scalar(cnt[:, 0, :], totals, -1.0, 0.0, ALU.add, ALU.max))
                link(V.tensor_copy(blocks_i[:, :], cnt[:, 0, :]))
                link(V.tensor_scalar(blocks_i[:, :], blocks_i[:, :], 5, None, ALU.arith_shift_right))
                link(V.tensor_copy(cnt[:, 1, :], blocks_i[:, :]))
                link(V.tensor_tensor_scan(cnt[:, 2, :], cnt[:, 1, :], C("zero"), 0.0, ALU.add, ALU.add))
                link(V.tensor_tensor(cnt[:, 3, :], cnt[:, 2, :], cnt[:, 1, :], ALU.subtract))
                link(V.tensor_scalar(cnt[:, 3, :], cnt[:, 3, :], float(CAP), float(NE * CAP - CAP), ALU.mult, ALU.add))
                link(V.tensor_tensor(cnt[:, 4, :], cnt[:, 3, :], C("slot0"), ALU.subtract))

                def b64(v):
                    return v.unsqueeze(1).to_broadcast((P, TT, NE))
                link(V.scalar_tensor_tensor(sv, bt, float(CAP), b64(cnt[:, 4, :]), ALU.is_ge, ALU.mult))
                V.tensor_tensor(pos0, bt, b64(C("slot0")), ALU.add).then_inc(*emptying("rank"))
                dve.wait_ge(*empty(JOB["rank"]))
                link(V.tensor_tensor(sv, sv, pos0, ALU.add))
                sel = rt[:, 0:512].rearrange("p (k c) -> p k c", k=2)
                link(V.tensor_tensor(sel, OH2.rearrange("p k t n -> p k (t n)"),
                                     sv.rearrange("p t n -> p (t n)").unsqueeze(1).to_broadcast((P, 2, TT * NE)), ALU.mult))
                sl = slf.rearrange("p k t -> p (k t)")
                link(V.reduce_sum(sl, rt[:, 0:512].rearrange("p (c n) -> p c n", n=NE), AX.X))
                slots(main, 0)
                upto_block = cnt[0:32, 3, :]
                link(V.tensor_scalar(upto_block, cnt[0:32, 2, :], C("row")[0:32], None, ALU.is_le))
                link(V.reduce_sum(block_col[:, 0:1], upto_block, AX.X))
                link(V.tensor_scalar(block_col[:, 0:1], block_col[:, 0:1], float(NE - 1), None, ALU.min))
                link(V.transpose(block_row[:, :], block_col[:, :]))
                link(V.tensor_copy(meta[:, 0:32], block_row[0:1, :]))
                link(V.tensor_copy(meta[:, 33:34], cnt[0:1, 2, NE - 1:NE]))
                link(V.tensor_scalar(cnt[0:1, 0, 0:SG], C("fours")[0:1], cnt[0:1, 2, NE - 1:NE], None, ALU.is_lt))
                link(V.reduce_sum(groups_f[:, :], cnt[0:1, 0, 0:SG], AX.X))
                link(V.tensor_copy(meta[:, 32:33], groups_f[:, :]))
                link(V.tensor_scalar(groups_f[:, :], groups_f[:, :], -1.0, 0.0, ALU.add, ALU.max))
                V.tensor_copy(meta[:, 34:35], groups_f[:, :]).then_inc(*meta_ready.up())
                dve.wait_ge(acc_ready.sem, acc_ready.at(1))
                rows(main, 0)
                with dve.Fori(0, EG - 1) as g:
                    experts(main, g, more=True)
                experts(main, EG - 1)
                n = spill_groups(dve)
                with dve.If(n > 0):
                    experts_done(dve)
                    rows(spill, 0)
                    first = dve.value_load(meta[0:1, 34:35], min_val=0, max_val=SG - 1)
                    with dve.If(first > 0):
                        with dve.Fori(0, first) as g:
                            experts(spill, g, more=True)
                    with dve.Else():
                        pass
                    experts(spill, first)
                with dve.Else():
                    pass
                experts_done(dve, n)
                for t in range(TT):
                    statistics(t, acc[t])
                for t in range(TT // 2, TT):
                    link(gain(t, TT, 64))
                    link(offset(t))
                end_layer(dve, l)

        @block.gpsimd
        def _(pool):
            with pool.Fori(0, L) as l:
                nc.gpsimd.memset(v1[:, :, :, DH:].rearrange("p t h o -> p (t h) o"), 1.0).then_inc(*v1_ones.up())
                pool.wait_ge(*empty(JOB["kr"]))
                pool.wait_ge(v1_ones.sem, v1_ones.at(1))
                nc.gpsimd.tensor_copy(kT7[NOPE:QK, :, :], krT[NOPE:QK, :].unsqueeze(1).to_broadcast((ROPE, H - 1, S))).then_inc(*kr_copied.up())
                pool.wait_ge(kr_copied.sem, kr_copied.at(1))
                nc.gpsimd.tensor_copy(kT[H - 1][NOPE:QK, :], krT[NOPE:QK, :]).then_inc(*kr_copied.up())
                pool.wait_ge(kr_copied.sem, kr_copied.at(2))
                for h in range(MH):
                    for s in range(TT):
                        pool.wait_ge(ptm_written.sem, ptm_written.at(h * TT + s + 1))
                        a = PTm[h % 2][:, pt_at[s]:pt_at[s] + P]
                        nc.gpsimd.affine_select(out=a, in_=a, compare_op=ALU.is_ge, fill=0.0, base=0, pattern=[[1, P]],
                                                channel_multiplier=-1).then_inc(*ptm_ready.up())
                pool.wait_ge(ln_in, 64)
                for t in range(TT // 2):
                    pool.wait_ge(ln_norm.sem, ln_norm.at(TT + t + 1))
                    nc.gpsimd.tensor_tensor(X[:, t, :], X[:, t, :], lnG, ALU.mult).then_inc(*ln_scaled.up())
                    pool.wait_ge(ln_scaled.sem, ln_scaled.at(t + 1))
                    nc.gpsimd.tensor_tensor(X[:, t, :], X[:, t, :], lnB, ALU.add)
                end_layer(pool, l)

        steps_counted = dstep.n, astep.n
        assert steps_counted == (DVE_STEPS, ACT_STEPS), steps_counted
        for e in "AD":
            assert emptied[e].n == n_of[e]
        assert bank_full.n == len(JOBS)


_INS = ["x", "positions", "w_in", "conv_w", "conv_b", "gate_b", "q_a_g", "kv_a_g", "w_qb", "w_kvb", "out_g", "w_out",
        "ln1_g", "ln1_b", "w_rg", "w_re", "w_gate", "w_up", "w_down", "ln2_g", "ln2_b"]


def kernel(**inputs):
    import numpy as _np
    import concourse.bacc as _bacc
    from concourse import mybir as _mybir
    from concourse.bass_utils import run_bass_kernel_spmd as _run

    nc = _bacc.Bacc("TRN2", target_bir_lowering=False, num_devices=1)
    arrays, args = {}, {}
    for name in _INS:
        a = _np.ascontiguousarray(inputs[name])
        arrays[f"in_{name}"] = a
        args[name] = nc.dram_tensor(f"in_{name}", a.shape, _mybir.dt.from_np(a.dtype), kind="ExternalInput").ap()
    arrays["in_constants"] = CONST
    const = nc.dram_tensor("in_constants", CONST.shape, _mybir.dt.float32, kind="ExternalInput").ap()
    out = nc.dram_tensor("out_0", (1, S, D), _mybir.dt.float32, kind="ExternalOutput").ap()
    hybrid_kernel(nc, args, const, out)
    r = _run(nc, [arrays], core_ids=[0])
    return r.results[0]["out_0"]
```
